# Optimizing a Trainium2 kernel written in Bass

```python
import jax, jax.numpy as jnp
from jax import lax
import numpy as np

D_MODEL = 1024
BATCH = 1
SEQ = 512
DEPTH = 2

N_MIXERS = 2
EPS = 1e-6

SSM_EXPAND = 2
SSM_D_INNER = SSM_EXPAND * D_MODEL
SSM_HEAD_DIM = 64
SSM_HEADS = SSM_D_INNER // SSM_HEAD_DIM
SSM_GROUPS = 8
SSM_HEADS_PER_GROUP = SSM_HEADS // SSM_GROUPS
SSM_STATE = 128
SSM_CONV = 4
SSM_CHUNK = 128
SSM_BC_DIM = SSM_GROUPS * SSM_STATE
SSM_CONV_DIM = SSM_D_INNER + 2 * SSM_BC_DIM
SSM_IN_DIM = SSM_D_INNER + SSM_CONV_DIM + SSM_HEADS

ATT_HEAD_DIM = 64
ATT_Q_HEADS = D_MODEL // ATT_HEAD_DIM
ATT_KV_HEADS = 4
ATT_GQA = ATT_Q_HEADS // ATT_KV_HEADS
ATT_WIDTH = ATT_Q_HEADS * ATT_HEAD_DIM
ATT_KV_WIDTH = ATT_KV_HEADS * ATT_HEAD_DIM
ATT_IN_DIM = 2 * ATT_WIDTH + 2 * ATT_KV_WIDTH
WINDOW = 128
ATT_BLOCK = 128
ROPE_THETA = 500000.0
ROPE_DIM = ATT_HEAD_DIM // 4

N_SSM_LAYERS = (DEPTH + 1) // 2
N_ATT_LAYERS = DEPTH // 2


def rmsnorm(x, w):
    xf = x.astype(jnp.float32)
    y = xf * lax.rsqrt(jnp.mean(xf * xf, axis=-1, keepdims=True) + EPS)
    return (y * w.astype(jnp.float32)).astype(x.dtype)

def causal_depthwise_conv(u, w, b):
    c = u.shape[-1]
    out = lax.conv_general_dilated(
        u, w[:, None, :].astype(u.dtype), window_strides=(1,),
        padding=((SSM_CONV - 1, 0),), dimension_numbers=('NWC', 'WIO', 'NWC'),
        feature_group_count=c)
    return out + b.astype(u.dtype)

def ssd_chunked(xs, dt, A, Bm, Cm):
    b, L = xs.shape[:2]
    c, l = L // SSM_CHUNK, SSM_CHUNK
    G, R, P, N = SSM_GROUPS, SSM_HEADS_PER_GROUP, SSM_HEAD_DIM, SSM_STATE
    x = (xs * dt[..., None]).reshape(b, c, l, G, R, P)
    a = jnp.moveaxis((dt * A).reshape(b, c, l, G, R), 2, -1)
    a_cs = jnp.cumsum(a, axis=-1)
    Bc = Bm.reshape(b, c, l, G, N)
    Cc = Cm.reshape(b, c, l, G, N)
    causal = jnp.tril(jnp.ones((l, l), dtype=bool))
    seg = a_cs[..., :, None] - a_cs[..., None, :]
    decay = jnp.exp(jnp.where(causal, seg, -jnp.inf))
    cb = jnp.einsum('bclgn,bcsgn->bcgls', Cc, Bc)
    y_diag = jnp.einsum('bcgrls,bcsgrp->bclgrp', cb[:, :, :, None] * decay, x)
    decay_to_end = jnp.exp(a_cs[..., -1:] - a_cs)
    states = jnp.einsum('bclgn,bcgrl,bclgrp->bcgrpn', Bc, decay_to_end, x)
    chunk_decay = jnp.exp(a_cs[..., -1])

    def step(h, inp):
        s, d = inp
        return h * d[..., None, None] + s, h

    h0 = jnp.zeros_like(states[:, 0])
    _, h_in = lax.scan(step, h0, (jnp.moveaxis(states, 1, 0), jnp.moveaxis(chunk_decay, 1, 0)))
    h_in = jnp.moveaxis(h_in, 0, 1)
    y_off = jnp.einsum('bclgn,bcgrpn,bcgrl->bclgrp', Cc, h_in, jnp.exp(a_cs))
    return (y_diag + y_off).reshape(b, L, SSM_HEADS, P)

def mamba2_mixer(h, w_in, conv_w, conv_b, dt_bias, a_log, d_skip, gate_norm, w_out):
    b, L, _ = h.shape
    f32 = jnp.float32
    z, xbc, dt = jnp.split(h @ w_in, [SSM_D_INNER, SSM_D_INNER + SSM_CONV_DIM], axis=-1)
    xbc = jax.nn.silu(causal_depthwise_conv(xbc, conv_w, conv_b))
    xs, Bm, Cm = jnp.split(xbc, [SSM_D_INNER, SSM_D_INNER + SSM_BC_DIM], axis=-1)
    xs = xs.reshape(b, L, SSM_HEADS, SSM_HEAD_DIM).astype(f32)
    Bm = Bm.reshape(b, L, SSM_GROUPS, SSM_STATE).astype(f32)
    Cm = Cm.reshape(b, L, SSM_GROUPS, SSM_STATE).astype(f32)
    dt = jax.nn.softplus(dt.astype(f32) + dt_bias.astype(f32))
    A = -jnp.exp(a_log.astype(f32))
    y = ssd_chunked(xs, dt, A, Bm, Cm) + d_skip.astype(f32)[:, None] * xs
    y = y.reshape(b, L, SSM_D_INNER) * jax.nn.silu(z.astype(f32))
    y = rmsnorm(y, gate_norm)
    return y.astype(h.dtype) @ w_out

def rope_tables(positions):
    inv = ROPE_THETA ** (-jnp.arange(0, ROPE_DIM, 2, dtype=jnp.float32) / ROPE_DIM)
    ang = positions.astype(jnp.float32)[..., None] * inv
    return jnp.cos(ang)[:, :, None, :], jnp.sin(ang)[:, :, None, :]

def apply_partial_rope(t, cos, sin):
    half = ROPE_DIM // 2
    t1, t2, rest = t[..., :half], t[..., half:ROPE_DIM], t[..., ROPE_DIM:]
    return jnp.concatenate([t1 * cos - t2 * sin, t2 * cos + t1 * sin, rest], axis=-1)

def swa_sink_mixer(h, cos, sin, w_in, sinks, w_out):
    b, L, _ = h.shape
    f32 = jnp.float32
    Hk, D, BLK = ATT_KV_HEADS, ATT_HEAD_DIM, ATT_BLOCK
    q, k, v, gate = jnp.split(
        h @ w_in, [ATT_WIDTH, ATT_WIDTH + ATT_KV_WIDTH, ATT_WIDTH + 2 * ATT_KV_WIDTH], axis=-1)
    q = apply_partial_rope(q.reshape(b, L, ATT_Q_HEADS, D).astype(f32), cos, sin)
    k = apply_partial_rope(k.reshape(b, L, Hk, D).astype(f32), cos, sin)
    v = v.reshape(b, L, Hk, D).astype(f32)
    nb = L // BLK
    qb = q.reshape(b, nb, BLK, Hk, ATT_GQA, D)

    def band(t):
        tp = jnp.pad(t, ((0, 0), (BLK, 0), (0, 0), (0, 0))).reshape(b, nb + 1, BLK, Hk, D)
        return jnp.concatenate([tp[:, :-1], tp[:, 1:]], axis=2)

    kb, vb = band(k), band(v)
    s = jnp.einsum('bnikgd,bnjkd->bnkgij', qb, kb) * (D ** -0.5)
    qi = jnp.arange(BLK)[:, None]
    kj = jnp.arange(2 * BLK)[None, :]
    dist = qi + BLK - kj
    blk = jnp.arange(nb)[:, None, None]
    valid = (dist >= 0) & (dist < WINDOW) & ((blk - 1) * BLK + kj >= 0)
    s = jnp.where(valid[None, :, None, None], s, -jnp.inf)
    sink = sinks.astype(f32).reshape(Hk, ATT_GQA)[None, None, :, :, None, None]
    m = jnp.maximum(jnp.max(s, axis=-1, keepdims=True), sink)
    p = jnp.exp(s - m)
    denom = jnp.sum(p, axis=-1, keepdims=True) + jnp.exp(sink - m)
    o = jnp.einsum('bnkgij,bnjkd->bnikgd', p / denom, vb)
    o = o.reshape(b, L, ATT_WIDTH) * jax.nn.silu(gate.astype(f32))
    return o.astype(h.dtype) @ w_out

def first_inputs(seed: int = 0) -> dict:
    key = jax.random.key(seed)
    ks = jax.random.split(key, 16)
    f32 = jnp.float32
    nS, nA = N_SSM_LAYERS, N_ATT_LAYERS
    x = jax.random.normal(ks[0], (BATCH, SEQ, D_MODEL), f32)
    positions = jnp.broadcast_to(jnp.arange(SEQ, dtype=jnp.int32), (BATCH, SEQ))
    pre_norm = 1.0 + 0.1 * jax.random.normal(ks[1], (DEPTH, D_MODEL), f32)
    post_norm = 1.0 + 0.1 * jax.random.normal(ks[2], (DEPTH, D_MODEL), f32)
    ssm_w_in = jax.random.normal(ks[3], (nS, D_MODEL, SSM_IN_DIM), f32) * D_MODEL ** -0.5
    ssm_conv_w = jax.random.normal(ks[4], (nS, SSM_CONV, SSM_CONV_DIM), f32) * SSM_CONV ** -0.5
    ssm_conv_b = 0.02 * jax.random.normal(ks[5], (nS, SSM_CONV_DIM), f32)
    dt0 = jnp.exp(jax.random.uniform(ks[6], (nS, SSM_HEADS), f32)
                  * (np.log(0.1) - np.log(0.001)) + np.log(0.001)).astype(f32)
    ssm_dt_bias = dt0 + jnp.log(-jnp.expm1(-dt0))
    ssm_a_log = jnp.log(jax.random.uniform(ks[7], (nS, SSM_HEADS), f32, 1.0, 16.0))
    ssm_d = 1.0 + 0.1 * jax.random.normal(ks[8], (nS, SSM_HEADS), f32)
    ssm_gate_norm = 1.0 + 0.1 * jax.random.normal(ks[9], (nS, SSM_D_INNER), f32)
    ssm_w_out = jax.random.normal(ks[10], (nS, SSM_D_INNER, D_MODEL), f32) * SSM_D_INNER ** -0.5
    att_w_in = jax.random.normal(ks[11], (nA, D_MODEL, ATT_IN_DIM), f32) * D_MODEL ** -0.5
    att_sinks = 0.5 * jax.random.normal(ks[12], (nA, ATT_Q_HEADS), f32)
    att_w_out = jax.random.normal(ks[13], (nA, ATT_WIDTH, D_MODEL), f32) * ATT_WIDTH ** -0.5
    return {"x": x, "positions": positions, "pre_norm": pre_norm, "post_norm": post_norm,
            "ssm_w_in": ssm_w_in, "ssm_conv_w": ssm_conv_w, "ssm_conv_b": ssm_conv_b,
            "ssm_dt_bias": ssm_dt_bias, "ssm_a_log": ssm_a_log, "ssm_d": ssm_d,
            "ssm_gate_norm": ssm_gate_norm, "ssm_w_out": ssm_w_out,
            "att_w_in": att_w_in, "att_sinks": att_sinks, "att_w_out": att_w_out}

def first_block(x, positions, pre_norm, post_norm, ssm_w_in, ssm_conv_w, ssm_conv_b,
              ssm_dt_bias, ssm_a_log, ssm_d, ssm_gate_norm, ssm_w_out,
              att_w_in, att_sinks, att_w_out):
    cos, sin = rope_tables(positions)
    for i in range(DEPTH):
        h = rmsnorm(x, pre_norm[i])
        j = i // N_MIXERS
        if i % N_MIXERS == 0:
            y = mamba2_mixer(h, ssm_w_in[j], ssm_conv_w[j], ssm_conv_b[j], ssm_dt_bias[j],
                             ssm_a_log[j], ssm_d[j], ssm_gate_norm[j], ssm_w_out[j])
        else:
            y = swa_sink_mixer(h, cos, sin, att_w_in[j], att_sinks[j], att_w_out[j])
        x = x + rmsnorm(y, post_norm[i])
    return x


CHUNK = 64
D_CONV = D_MODEL // 2
N_CONV_GROUPS = 4
CONV_WIDTH = 31
D_POOL = D_MODEL // 2
POOL_WINDOWS = (2, 4, 8, 16)
N_POOL_GROUPS = len(POOL_WINDOWS)
POOL_GROUP = D_POOL // N_POOL_GROUPS
HG_HEADS = 8
HG_DK = D_MODEL // HG_HEADS
HG_DV = HG_DK
D_HG = HG_HEADS * HG_DK
D_FF = -(-8 * D_MODEL // (3 * 256)) * 256
N_EVEN = (DEPTH + 1) // 2
N_ODD = DEPTH // 2


def rmsnorm_2(x, g):
    xf = x.astype(jnp.float32)
    y = xf * lax.rsqrt(jnp.mean(xf * xf, axis=-1, keepdims=True) + EPS)
    return (y * g.astype(jnp.float32)).astype(x.dtype)

def layernorm(x, g, b):
    xf = x.astype(jnp.float32)
    mu = jnp.mean(xf, axis=-1, keepdims=True)
    var = jnp.mean(jnp.square(xf - mu), axis=-1, keepdims=True)
    y = (xf - mu) * lax.rsqrt(var + EPS)
    return (y * g.astype(jnp.float32) + b.astype(jnp.float32)).astype(x.dtype)

def swiglu_ffn(h, w1, w3, w2):
    return (jax.nn.silu(h @ w1) * (h @ w3)) @ w2

def conv_pool_mixer(h, w_in, dw_w, dw_b, ln_g, ln_b, pool_w, pool_scale, w_out):
    B, T, _ = h.shape
    z = h @ w_in
    a_val = z[..., :D_CONV]
    a_gate = z[..., D_CONV:2 * D_CONV]
    u = z[..., 2 * D_CONV:]

    a = a_val * jax.nn.sigmoid(a_gate)
    a = lax.conv_general_dilated(
        a, dw_w[:, None, :].astype(a.dtype), window_strides=(1,),
        padding=[(CONV_WIDTH - 1, 0)],
        dimension_numbers=('NWC', 'WIO', 'NWC'),
        feature_group_count=D_CONV) + dw_b
    a = jax.nn.silu(layernorm(a, ln_g, ln_b))

    ug = u.reshape(B, T, N_POOL_GROUPS, POOL_GROUP)
    cs = jnp.cumsum(ug.astype(jnp.float32), axis=1)
    cs = jnp.pad(cs, ((0, 0), (1, 0), (0, 0), (0, 0)))
    t = jnp.arange(T)
    means = []
    for g, w in enumerate(POOL_WINDOWS):
        lo = jnp.maximum(t + 1 - w, 0)
        s = cs[:, 1:, g] - cs[:, lo, g]
        cnt = jnp.minimum(t + 1, w).astype(jnp.float32)[:, None]
        means.append(s / cnt)
    pooled = jnp.stack(means, axis=2)
    d = (pooled - ug.astype(jnp.float32)).astype(u.dtype)
    p = jnp.einsum('btgc,gcd->btgd', d, pool_w).reshape(B, T, D_POOL) * pool_scale

    return jnp.concatenate([a, p], axis=-1) @ w_out

def hgrn2_mixer(h, w_in, lb, gn_g, w_out):
    B, T, _ = h.shape
    NC = T // CHUNK
    z = h @ w_in
    q, f_raw, i, g = jnp.split(z, 4, axis=-1)
    f = lb + (1.0 - lb) * jax.nn.sigmoid(f_raw.astype(jnp.float32))
    log_f = jnp.log(f)
    k = 1.0 - f

    def to_chunks(a, dh):
        a = a.astype(jnp.float32).reshape(B, NC, CHUNK, HG_HEADS, dh)
        return a.transpose(1, 0, 3, 2, 4)

    qc = to_chunks(q, HG_DK)
    kc = to_chunks(k, HG_DK)
    vc = to_chunks(i, HG_DV)
    bc = jnp.cumsum(to_chunks(log_f, HG_DK), axis=3)
    tril = jnp.tril(jnp.ones((CHUNK, CHUNK), dtype=bool))

    def step(S, inp):
        qt, kt, vt, bt = inp
        diff = bt[:, :, :, None, :] - bt[:, :, None, :, :]
        decay = jnp.exp(jnp.where(tril[:, :, None], diff, -jnp.inf))
        scores = jnp.einsum('bhtk,bhsk,bhtsk->bhts', qt, kt, decay)
        o = (jnp.einsum('bhts,bhsv->bhtv', scores, vt)
             + jnp.einsum('bhtk,bhkv->bhtv', qt * jnp.exp(bt), S))
        b_last = bt[:, :, -1:, :]
        S = (jnp.exp(b_last[:, :, 0, :])[..., None] * S
             + jnp.einsum('bhsk,bhsv->bhkv', kt * jnp.exp(b_last - bt), vt))
        return S, o

    S0 = jnp.zeros((B, HG_HEADS, HG_DK, HG_DV), jnp.float32)
    _, o = lax.scan(step, S0, (qc, kc, vc, bc))
    o = o.transpose(1, 0, 3, 2, 4).reshape(B, T, HG_HEADS, HG_DV)
    o = o * lax.rsqrt(jnp.mean(o * o, axis=-1, keepdims=True) + EPS)
    o = o * gn_g.astype(jnp.float32).reshape(HG_HEADS, HG_DV)
    o = o.reshape(B, T, D_HG).astype(h.dtype) * jax.nn.silu(g)
    return o @ w_out

def second_inputs(seed: int = 0) -> dict:
    key = jax.random.key(seed)
    ks = jax.random.split(key, 20)
    nrm = lambda k, shape, s: jax.random.normal(k, shape, jnp.float32) * s
    gain = lambda k, shape: 1.0 + 0.05 * jax.random.normal(k, shape, jnp.float32)
    d_in0 = 2 * D_CONV + D_POOL
    return {
        "x": jax.random.normal(ks[0], (BATCH, SEQ, D_MODEL), jnp.float32),
        "norm_mix_g": gain(ks[1], (DEPTH, D_MODEL)),
        "norm_ffn_g": gain(ks[2], (DEPTH, D_MODEL)),
        "final_g": gain(ks[3], (D_MODEL,)),
        "cp_w_in": nrm(ks[4], (N_EVEN, D_MODEL, d_in0), D_MODEL ** -0.5),
        "cp_dw_w": nrm(ks[5], (N_EVEN, CONV_WIDTH, D_CONV), CONV_WIDTH ** -0.5),
        "cp_dw_b": nrm(ks[6], (N_EVEN, D_CONV), 0.01),
        "cp_ln_g": gain(ks[7], (N_EVEN, D_CONV)),
        "cp_ln_b": nrm(ks[8], (N_EVEN, D_CONV), 0.01),
        "cp_pool_w": nrm(ks[9], (N_EVEN, N_POOL_GROUPS, POOL_GROUP, POOL_GROUP), POOL_GROUP ** -0.5),
        "cp_pool_scale": gain(ks[10], (N_EVEN, D_POOL)),
        "cp_w_out": nrm(ks[11], (N_EVEN, D_CONV + D_POOL, D_MODEL), (D_CONV + D_POOL) ** -0.5),
        "hg_w_in": nrm(ks[12], (N_ODD, D_MODEL, 4 * D_HG), D_MODEL ** -0.5),
        "hg_lb_logits": nrm(ks[13], (DEPTH, D_HG), 0.1),
        "hg_gn_g": gain(ks[14], (N_ODD, D_HG)),
        "hg_w_out": nrm(ks[15], (N_ODD, D_HG, D_MODEL), D_HG ** -0.5),
        "ffn_w1": nrm(ks[16], (DEPTH, D_MODEL, D_FF), D_MODEL ** -0.5),
        "ffn_w3": nrm(ks[17], (DEPTH, D_MODEL, D_FF), D_MODEL ** -0.5),
        "ffn_w2": nrm(ks[18], (DEPTH, D_FF, D_MODEL), D_FF ** -0.5),
    }

def second_block(x, norm_mix_g, norm_ffn_g, final_g, cp_w_in, cp_dw_w, cp_dw_b,
              cp_ln_g, cp_ln_b, cp_pool_w, cp_pool_scale, cp_w_out, hg_w_in,
              hg_lb_logits, hg_gn_g, hg_w_out, ffn_w1, ffn_w3, ffn_w2):
    p = jax.nn.softmax(hg_lb_logits.astype(jnp.float32), axis=0)
    lower_bounds = jnp.cumsum(p, axis=0) - p[0:1]
    h = x
    for layer in range(DEPTH):
        hn = rmsnorm_2(h, norm_mix_g[layer])
        j = layer // 2
        if layer % 2 == 0:
            mix = conv_pool_mixer(hn, cp_w_in[j], cp_dw_w[j], cp_dw_b[j], cp_ln_g[j],
                                  cp_ln_b[j], cp_pool_w[j], cp_pool_scale[j], cp_w_out[j])
        else:
            mix = hgrn2_mixer(hn, hg_w_in[j], lower_bounds[layer], hg_gn_g[j], hg_w_out[j])
        h = h + mix
        h = h + swiglu_ffn(rmsnorm_2(h, norm_ffn_g[layer]), ffn_w1[layer], ffn_w3[layer], ffn_w2[layer])
    return rmsnorm_2(h, final_g)


def setup_inputs(seed=0):
    out = dict(first_inputs(seed))
    for name, value in second_inputs(seed + 1).items():
        if name != "x":
            out[name + "_2"] = value
    return out


def reference(
    x, positions, pre_norm, post_norm, ssm_w_in, ssm_conv_w, ssm_conv_b, ssm_dt_bias, ssm_a_log,
    ssm_d, ssm_gate_norm, ssm_w_out, att_w_in, att_sinks, att_w_out, norm_mix_g_2, norm_ffn_g_2,
    final_g_2, cp_w_in_2, cp_dw_w_2, cp_dw_b_2, cp_ln_g_2, cp_ln_b_2, cp_pool_w_2,
    cp_pool_scale_2, cp_w_out_2, hg_w_in_2, hg_lb_logits_2, hg_gn_g_2, hg_w_out_2, ffn_w1_2,
    ffn_w3_2, ffn_w2_2,
):
    x = first_block(
        x, positions, pre_norm, post_norm, ssm_w_in, ssm_conv_w, ssm_conv_b, ssm_dt_bias,
        ssm_a_log, ssm_d, ssm_gate_norm, ssm_w_out, att_w_in, att_sinks, att_w_out,
    )
    return second_block(
        x, norm_mix_g_2, norm_ffn_g_2, final_g_2, cp_w_in_2, cp_dw_w_2, cp_dw_b_2, cp_ln_g_2,
        cp_ln_b_2, cp_pool_w_2, cp_pool_scale_2, cp_w_out_2, hg_w_in_2, hg_lb_logits_2,
        hg_gn_g_2, hg_w_out_2, ffn_w1_2, ffn_w3_2, ffn_w2_2,
    )


_drawn_inputs = setup_inputs


def setup_inputs(seed=0):
    import zlib

    import numpy as np

    out = dict(_drawn_inputs(seed))
    spreads = {}
    factors = {'att_sinks': 6.453,
     'cp_dw_b_2': 8.0,
     'cp_ln_g_2': 3.464,
     'cp_ln_b_2': 8.0,
     'cp_pool_scale_2': 2.769,
     'hg_gn_g_2': 3.843}
    for name, (base, spread) in spreads.items():
        noise = np.random.default_rng([zlib.crc32(name.encode()), seed]).standard_normal(out[name].shape)
        drawn = base * np.exp(spread * noise) if base else spread * noise
        out[name] = __import__('jax').numpy.asarray(drawn.astype(out[name].dtype))
    for name, factor in factors.items():
        out[name] = (out[name] * factor).astype(out[name].dtype)
    return out
```

```python
from contextlib import ExitStack

import concourse.bass as bass
import numpy as np
from concourse import mybir

ALU = mybir.AluOpType
ACT = mybir.ActivationFunctionType
AX = mybir.AxisListType
F32 = mybir.dt.float32
F32R = mybir.dt.float32r
I32 = mybir.dt.int32
U32 = mybir.dt.uint32

P = 128
L = 512
D = 1024
KT = D // P
NCH = L // P
EPS = 1e-6
PHASES = 6

SI = 2048
SH = 32
SG = 8
HPG = SH // SG
HD = 64
SB0, SC0, SDT0 = 2 * SI, 2 * SI + 1024, 2 * SI + 2048
TAPS = 4
KVH = 4
CW = 31
POOLW = (2, 4, 8, 16)
HH = 8
LEVELS = (64, 32, 16, 8, 4, 2, 1)
DFF = 2816
FT = DFF // P
UC = 256
NEG = -1.0e30
MAGIC = 1.5 * 2.0 ** 23
N_PAR = 19
DT_V = 3

C_ID, C_CAUSAL, C_BAND, C_ROT, C_RESET, C_RC, C_INV = 0, 128, 256, 512, 640, 1152, 1216
C_N = 1217
P_CONVW, P_DW = 0, 128
P_PRE, P_POST, P_CONVB, P_GATE, P_MIX, P_FFN, P_FINAL, P_GN = 256, 272, 288, 320, 336, 352, 368, 376
P_DWB, P_LNG, P_LNB, P_PSC, P_LB, P_SKIP = 384, 388, 392, 396, 400, 416


def shape_constants():
    i = np.arange(P)
    c = np.zeros((P, C_N), np.float32)
    c[:, C_ID:C_ID + P] = np.eye(P)
    c[:, C_CAUSAL:C_CAUSAL + P] = i[:, None] <= i[None, :]
    c[:, C_BAND:C_BAND + P] = np.where(i[None, :] > i[:, None], 0.0, NEG)
    c[:, C_BAND + P:C_BAND + 2 * P] = np.where(i[None, :] <= i[:, None], 0.0, NEG)
    for base in (0, 64):
        for d in range(8):
            c[base + d + 8, C_ROT + base + d] = -1.0
            c[base + d, C_ROT + base + d + 8] = 1.0
    c[:, C_RESET:C_RESET + L] = np.arange(L)[None, :] % P != 0
    for g, w in enumerate(POOLW):
        c[:, C_RC + 16 * g:C_RC + 16 * g + 16] = 1.0 / np.minimum(np.arange(16) + 1, w)
    inv = np.float32(500000.0) ** (-np.arange(0, 16, 2, dtype=np.float32) / np.float32(16))
    c[:, C_INV] = [inv[d % 64 % 8] if d % 64 < 16 else 0.0 for d in i]
    m = np.zeros((P, (len(LEVELS) + 1) * P), np.float32)
    for n, w in enumerate(LEVELS):
        s, t = i[:, None], i[None, :]
        m[:, n * P:(n + 1) * P] = (s // (2 * w) == t // (2 * w)) & (s % (2 * w) < w) & (t % (2 * w) >= w)
    m[:, len(LEVELS) * P:] = np.eye(P)
    return c, m


def conv_tile(g, j):
    return (2 * g, 2 * g + 1, 16 + g, 24 + g)[j]


PI_BELOW = 3.1415925


def two_pi_parts():
    left, out = 2 * np.pi, []
    for n in (5, 13, 21):
        out.append(float(np.floor(left * 2.0 ** n) / 2.0 ** n))
        left -= out[-1]
    return out + [float(np.float32(left))]


class Unit:

    def __init__(self, w, pieces, k0, kt, tiles, first, last):
        self.w, self.pieces, self.k0, self.kt = w, pieces, k0, kt
        self.tiles, self.first, self.last = tiles, first, last
        self.cols = max(c + n for c, _, n in pieces)


def plan(w):
    units, phases = [], {}
    state = {"tile": 0}

    def add(name, weight, columns, kts):
        u0, t0 = len(units), state["tile"]
        k0 = 0
        n = sum(x[2] for x in columns) // P
        tiles = list(range(t0, t0 + n))
        for j, kt in enumerate(kts):
            units.append(Unit(weight, columns, k0, kt, tiles, j == 0, j == len(kts) - 1))
            k0 += kt
        state["tile"] += n
        lo, hi, a, b = phases.get(name, (u0, None, t0, None))
        phases[name] = (lo, len(units), a, state["tile"])

    whole = [KT]

    def out_proj(name, weight, kts):
        for n in range(D // UC):
            add(name, weight, [(0, n * UC, UC)], kts)

    def ffn(i):
        for n in range(DFF // UC):
            add(f"up{i}", w["w1"][i], [(0, n * UC, UC)], whole)
            add(f"up{i}", w["w3"][i], [(0, n * UC, UC)], whole)
        out_proj(f"down{i}", w["w2"][i], [8, 8, 6])

    add("dt", w["ssm_in"], [(0, SDT0, 32), (32, SDT0 - 96, 96)], whole)
    for g in range(SG):
        add("ssm", w["ssm_in"], [(0, SI + g * UC, UC)], whole)
        add("ssm", w["ssm_in"], [(0, SB0 + g * P, P), (P, SC0 + g * P, P)], whole)
        add("ssm", w["ssm_in"], [(0, g * UC, UC)], whole)
    out_proj("ssm_out", w["ssm_out"], [8, 8])
    for h in range(KVH):
        add("att", w["att_in"], [(0, h * UC, UC)], whole)
        add("att", w["att_in"], [(0, D + h * HD, HD), (HD, D + 256 + h * HD, HD)], whole)
        add("att", w["att_in"], [(0, D + 512 + h * UC, UC)], whole)
    out_proj("att_out", w["att_out"], whole)
    for n in range(2):
        add("cp", w["cp_in"], [(0, 512 + n * UC, UC)], whole)
        add("cp", w["cp_in"], [(0, n * UC, UC)], whole)
    for n in range(2):
        add("cp", w["cp_in"], [(0, 1024 + n * UC, UC)], whole)
    out_proj("cp_out", w["cp_out"], whole)
    ffn(0)
    for p in range(HH // 2):
        for j in range(4):
            add("hg", w["hg_in"], [(0, j * D + p * UC, UC)], whole)
    out_proj("hg_out", w["hg_out"], whole)
    ffn(1)
    return units, phases


def build(nc, x, positions, pre_norm, post_norm, ssm_w_in, ssm_conv_w, ssm_conv_b, ssm_dt_bias,
          ssm_a_log, ssm_d, ssm_gate_norm, ssm_w_out, att_w_in, att_sinks, att_w_out, norm_mix,
          norm_ffn, final_g, cp_w_in, cp_dw_w, cp_dw_b, cp_ln_g, cp_ln_b, cp_pool_w, cp_pool_scale,
          cp_w_out, hg_w_in, hg_lb_logits, hg_gn_g, hg_w_out, ffn_w1, ffn_w3, ffn_w2,
          shape_const, level_mask, out):
    units, phases = plan({
        "ssm_in": ssm_w_in[0], "ssm_out": ssm_w_out[0], "att_in": att_w_in[0], "att_out": att_w_out[0],
        "cp_in": cp_w_in[0], "cp_out": cp_w_out[0], "hg_in": hg_w_in[0], "hg_out": hg_w_out[0],
        "w1": [ffn_w1[0], ffn_w1[1]], "w3": [ffn_w3[0], ffn_w3[1]], "w2": [ffn_w2[0], ffn_w2[1]]})
    order = [["dt", "ssm", "ssm_out"], ["att", "att_out"], ["cp", "cp_out"], ["up0", "down0"],
             ["hg", "hg_out"], ["up1", "down1"]]
    n_units = phases[order[PHASES - 1][-1]][1]
    part_end, unit_end, parts = {}, [], 0
    for u in units:
        for t in u.tiles:
            parts += 1
            part_end[t] = parts
        unit_end.append(parts)

    def tiles_of(name):
        return range(phases[name][2], phases[name][3])

    def end_of(name):
        return unit_end[phases[name][1] - 1]

    split0, n = {}, 0
    for name, count in (("pre0", KT), ("y", 16), ("pre1", KT), ("att", KT), ("pre2", KT), ("cp", KT),
                        ("pre3", KT), ("up0", FT), ("pre4", KT), ("hg", KT), ("pre5", KT), ("up1", FT)):
        split0[name] = n
        n += count

    pre_round, post_round = [0, 2, 4, 5, 6, 7, 8], [1, 3]
    deferred = [v for v in (1, 2, 3, 5) if v < PHASES]

    with ExitStack() as ctx:
        def sb(name, shape, dt=F32):
            return ctx.enter_context(nc.sbuf_tensor(name, shape, dt))

        def sem(name):
            return ctx.enter_context(nc.semaphore(name))

        cst = sb("cst", [P, C_N])
        ones = sb("ones", [P, P])
        prm = sb("prm", [P, 4 * P])
        eps_col = sb("eps_col", [P, 1])
        xT = sb("xT", [P, KT, L])
        hh = sb("hh", [P, KT, L], F32R)
        hl = sb("hl", [P, KT, L], F32R)
        stage = sb("stage", [P, 2, KT * UC])
        wh = sb("wh", [P, 2, KT * UC], F32R)
        wl = sb("wl", [P, 2, KT * UC], F32R)
        sq = sb("sq", [P, 2, L])
        val = sb("val", [P, 2, L])
        root = sb("root", [P, L])
        rstd = sb("rstd", [P, L])
        sqsum = sb("sqsum", [P, L])
        arena_bytes = 92704
        arena = sb("arena", [P, arena_bytes // 4])
        a0 = nc.sbuf_base - arena_bytes if not callable(nc.sbuf_base) else nc.sbuf_base() - arena_bytes

        class Region:

            def __init__(self, at=0):
                self.at = at

            def take(self, name, shape, dt=F32):
                size = 4
                for d in shape[1:]:
                    size *= d
                t = nc.alloc_sbuf_tensor_at(name, shape, dt, offset=a0 + self.at)
                self.at += -(-size // 32) * 32
                assert self.at <= arena_bytes, (name, self.at)
                return t

        ident = cst[:, C_ID:C_ID + P]

        R = Region()
        xin = R.take("xin", [P, NCH, D])
        prow = R.take("prow", [P, 4, P])
        skip_raw = R.take("skip_raw", [16, 2])
        R = Region()
        y = R.take("m_y", [P, 16, L])
        after_y = R.at
        raw = R.take("m_raw", [P, 2, TAPS - 1 + L])
        xs = R.take("m_xs", [P, 2, 4, L])
        sz = R.take("m_sz", [P, 2, L])
        xdt = R.take("m_xdt", [P, NCH, HPG * HD])
        xde = R.take("m_xde", [P, NCH - 1, HPG * HD])
        Bt = R.take("m_Bt", [P, NCH - 1, P])
        cbm = R.take("m_cbm", [P, NCH, P])
        G = R.take("m_G", [P, HPG, L])
        EC = R.take("m_EC", [P, HPG, L])
        Hs = R.take("m_Hs", [P, NCH - 1, HPG * HD])
        cd = R.take("m_cd", [P, HPG, NCH])
        tokT = R.take("m_tokT", [P, 3, NCH, SH])
        acs = R.take("m_acs", [SH, L])
        R = Region(after_y - 12 * 2048)
        dtmp = [R.take(f"m_dt{i}", [SH, L]) for i in range(10)]
        hcol = R.take("m_hcol", [SH, 4])
        R = Region(after_y)
        yl = R.take("m_yl", [P, 16, L], F32R)
        yo_m = R.take("m_yo", [P, KT, L])
        rg = R.take("m_rg", [P, L])

        R = Region()
        oh = R.take("a_oh", [P, KT, L], F32R)
        ol = R.take("a_ol", [P, KT, L], F32R)
        yo_a = nc.alloc_sbuf_tensor_at("a_yo", [P, KT, L], F32, offset=a0 + R.at)
        cosT = R.take("a_cos", [P, L])
        sinT = R.take("a_sin", [P, L])
        qraw = R.take("a_qraw", [P, 2, L])
        kvraw = R.take("a_kvraw", [P, L])
        qr = R.take("a_qr", [P, 2, 2, L])
        kd = R.take("a_kd", [P, 2, 2, L])
        vt = R.take("a_vt", [P, 2, NCH, HD])
        rtmp = R.take("a_rtmp", [P, 2, L])
        pp = R.take("a_pp", [P, 2, 2, UC])
        pT = R.take("a_pT", [P, 2, 2, 2, P])
        sgate = R.take("a_sgate", [P, 2, 2, L])
        srow = R.take("a_srow", [P, 2, 12])
        sinks = R.take("a_sinks", [P, 16])
        posi = nc.alloc_sbuf_tensor_at("a_posi", [P, L], I32, offset=a0)
        R = Region(2048)
        trig = [R.take(f"a_trig{i}", [P, L]) for i in range(4)]
        R = Region()
        ch = R.take("c_h", [P, KT, L], F32R)
        cl = R.take("c_l", [P, KT, L], F32R)
        apad = R.take("c_a", [P, 4, CW - 1 + L])
        acc = R.take("c_acc", [P, 4, L])
        sig = R.take("c_sig", [P, 2, L])
        ub = R.take("c_u", [P, 4, 16 + L])
        ws = R.take("c_ws", [P, 2, 16 + L])
        dp = R.take("c_dp", [P, 2, L])
        poolw = R.take("c_pw", [P, 4, P])
        lrstd = R.take("c_lrstd", [P, L])
        R = Region()
        gh = R.take("f_h", [P, FT, L], F32R)
        gl = R.take("f_l", [P, FT, L], F32R)
        R = Region()
        hoh = R.take("h_oh", [P, KT, L], F32R)
        hol = R.take("h_ol", [P, KT, L], F32R)
        hq = R.take("h_q", [P, 2, 2, L])
        hk = R.take("h_k", [P, 2, 2, L])
        hb = R.take("h_b", [P, 2, 2, L])
        hvt = R.take("h_vt", [P, 2, 2, L])
        hg = R.take("h_g", [P, 3, L])
        XL = R.take("h_x", [P, 3, L])
        SM = R.take("h_sm", [P, 2, L])
        Ke = R.take("h_ke", [P, NCH - 1, P])
        Kt = R.take("h_kt", [P, NCH - 1, P])
        Qe = R.take("h_qe", [P, NCH - 1, P])
        St = R.take("h_st", [P, NCH - 1, P])
        lmask = R.take("h_mask", [P, len(LEVELS) + 1, P])
        lbc = R.take("h_lb", [P, 3, 8])
        ebl = R.take("h_ebl", [P, 2, NCH])

        gp = [ctx.enter_context(nc.psum_tensor(f"gp{i}", [P, L], F32)) for i in range(4)]
        mp = [ctx.enter_context(nc.psum_tensor(f"mp{i}", [P, L], F32)) for i in range(4)]

        landed = [sem(f"weights_landed{i}") for i in range(2)]
        hi_done = sem("weights_hi_done")
        weights_split = sem("weights_split")
        gemm_part = sem("gemm_part")
        bank_read = [sem(f"bank_read{i}") for i in range(4)]
        value_ready, hi_ready, split_done = sem("value_ready"), sem("hi_ready"), sem("split_done")
        sq_ready, sq_added, sum_ready, rstd_ready = (sem(s) for s in ("sq_ready", "sq_added", "sum_ready", "rstd_ready"))
        silu_ready = sem("silu_ready")
        x_tile = sem("x_tile")
        dve_step, act_step, pe_step = sem("dve_step"), sem("act_step"), sem("pe_step")
        in_landed, par_landed, prm_turned, prm_ready, x_turned, x_taken = (sem(s) for s in (
            "in_landed", "par_landed", "prm_turned", "prm_ready", "x_turned", "x_taken"))
        skip_ready = sem("skip_ready")
        const_set = sem("const_set")
        dt_a, dt_v, dt_turned, tok_ready = (sem(s) for s in ("dt_act", "dt_vec", "dt_turned", "tok_ready"))
        conv_done, silu_done = sem("conv_done"), sem("silu_done")
        xt_ready, xt_read, bt_ready, bt_read, cb_ready, cb_read = (sem(s) for s in (
            "xt_ready", "xt_read", "bt_ready", "bt_read", "cb_ready", "cb_read"))
        bc_ready, e_ready, seg_ready, dec_ready, gc_ready = (sem(s) for s in (
            "bc_ready", "e_ready", "seg_ready", "dec_ready", "gc_ready"))
        st_ready, h_ready, y_ready, y_read, yg_ready, gsq_ready = (sem(s) for s in (
            "st_ready", "h_ready", "y_ready", "y_read", "yg_ready", "gsq_ready"))
        gate_sq, gate_sum, gate_rstd = (sem(s) for s in ("gate_sq", "gate_sum", "gate_rstd"))
        posi_landed, trig_ready, sin_done = sem("posi_landed"), sem("trig_ready"), sem("sin_done")
        rot_ready, v_turned, qk_ready = sem("rot_ready"), sem("v_turned"), sem("qk_ready")
        s_ready, s_read, m_ready, p_ready, pn_ready, pt_turned, pt_copied, pv_done = (sem(s) for s in (
            "s_ready", "s_read", "m_ready", "p_ready", "pn_ready", "pt_turned", "pt_copied", "pv_done"))
        poolw_landed, conv_ready, mean_ready, centred, lsq_ready, var_ready = (sem(s) for s in (
            "poolw_landed", "conv_ready", "mean_ready", "centred", "lsq_ready", "var_ready"))
        lrstd_ready, ln_ready, window_ready, pool_ready = (sem(s) for s in (
            "lrstd_ready", "ln_ready", "window_ready", "pool_ready"))
        mask_landed, lb_diff, lb_exp, f_lin, f_ready, ln_f, hb_ready = (sem(s) for s in (
            "mask_landed", "lb_diff", "lb_exp", "f_lin", "f_ready", "ln_f", "hb_ready"))
        vt_turned, vt_ready, diff_ready, dexp_ready, x_ready, lv_ready, lv_read = (sem(s) for s in (
            "vt_turned", "vt_ready", "diff_ready", "dexp_ready", "x_ready", "lv_ready", "lv_read"))
        ke_diff, ke_exp, ke_ready, kt_turned, kt_ready, hst_ready, hs_ready = (sem(s) for s in (
            "ke_diff", "ke_exp", "ke_ready", "kt_turned", "kt_ready", "hst_ready", "hs_ready"))
        qe_exp, qe_ready = sem("qe_exp"), sem("qe_ready")
        ho_ready, hsq_ready, hsum_ready, hrstd_ready, hscaled = (sem(s) for s in (
            "ho_ready", "hsq_ready", "hsum_ready", "hrstd_ready", "hscaled"))
        out_turned, out_ready, out_landed = sem("out_turned"), sem("out_ready"), sem("out_landed")
        final_ready, sig_ready = sem("final_ready"), sem("sig_ready")

        def tile_whole(eng, t):
            eng.wait_ge(gemm_part, part_end[t])

        def tile_taken(eng, t):
            eng.wait_ge(bank_read[t % 4], t // 4 + 1)

        def out_tile(name, k):
            return phases[name][2] + k

        out_names = ["ssm_out", "att_out", "cp_out", "down0", "hg_out", "down1"]

        def x_wait(eng, v, k):
            if v <= 2:
                eng.wait_ge(x_tile, KT * v + k + 1)
            else:
                tile_taken(eng, out_tile(out_names[v - 1], k))

        block = ctx.enter_context(nc.Block())

        @block.sync
        def _(sp):
            for c in range(NCH):
                sp.dma_start(xin[:, c, :], x[0, c * P:(c + 1) * P, :]).then_inc(in_landed, 16)
            count = [0, 0]
            for u in range(n_units):
                un = units[u]
                if u >= 2:
                    sp.wait_ge(weights_split, u - 1)
                dst = stage[:, u % 2, 0:un.kt * un.cols].rearrange("p (k n) -> p k n", k=un.kt)
                for c, n0, w in un.pieces:
                    src = un.w[un.k0 * P:(un.k0 + un.kt) * P, n0:n0 + w].rearrange("(k p) n -> p k n", p=P)
                    sp.dma_start(dst[:, :, c:c + w], src).then_inc(landed[u % 2], 16)
            for c in range(NCH):
                sp.wait_ge(out_ready, 2 * c + 2)
                sp.dma_start(out[0, c * P:(c + 1) * P, :], xin[:, c, :]).then_inc(out_landed, 16)
            sp.wait_ge(out_landed, 16 * NCH)

        @block.gpsimd
        def _(pool):
            count = [0, 0]
            for u in range(n_units):
                un, s = units[u], u % 2
                n = un.kt * un.cols
                count[s] += 16 * len(un.pieces)
                pool.wait_ge(landed[s], count[s])
                if u >= 2:
                    pool.wait_ge(gemm_part, unit_end[u - 2])
                pool.tensor_scalar(wh[:, s, 0:n], stage[:, s, 0:n], 1.0, 1.0, ALU.mult, ALU.mult).then_inc(hi_done, 1)
                pool.wait_ge(hi_done, u + 1)
                pool.tensor_tensor(wl[:, s, 0:n], stage[:, s, 0:n], wh[:, s, 0:n].bitcast(F32),
                                   ALU.subtract).then_inc(weights_split, 1)

        @block.tensor
        def _(pe):
            def granules(name, hi, lo, split, lead=0, after_first=None):
                u0, u1, t0, _ = phases[name]
                for k in range(KT if lead else 0):
                    pe.wait_ge(split_done, split(k) + 1)
                    for u in range(u0, u0 + lead):
                        s = u % 2
                        wvh = wh[:, s, 0:KT * units[u].cols].rearrange("p (k n) -> p k n", k=KT)
                        wvl = wl[:, s, 0:KT * units[u].cols].rearrange("p (k n) -> p k n", k=KT)
                        if k == 0:
                            pe.wait_ge(weights_split, u + 1)
                        for m, t in enumerate(units[u].tiles):
                            if k == 0 and t >= 4:
                                pe.wait_ge(bank_read[t % 4], t // 4)
                            cols = slice(m * P, (m + 1) * P)
                            bank = gp[t % 4]
                            pe.matmul(bank[:, :], wvh[:, k, cols], hi(k), start=(k == 0), stop=False)
                            pe.matmul(bank[:, :], wvl[:, k, cols], hi(k), start=False, stop=False)
                            mm = pe.matmul(bank[:, :], wvh[:, k, cols], lo(k), start=False, stop=(k == KT - 1))
                            if k == KT - 1:
                                mm.then_inc(gemm_part, 1)
                                if t == t0 and after_first:
                                    after_first()
                            if k >= KT - 2:
                                yield
                for u in range(u0 + lead, u1):
                    un, s = units[u], u % 2
                    wvh = wh[:, s, 0:un.kt * un.cols].rearrange("p (k n) -> p k n", k=un.kt)
                    wvl = wl[:, s, 0:un.kt * un.cols].rearrange("p (k n) -> p k n", k=un.kt)
                    for m, t in enumerate(un.tiles):
                        bank = gp[t % 4]
                        if m == 0:
                            pe.wait_ge(weights_split, u + 1)
                        if un.first and t >= 4:
                            pe.wait_ge(bank_read[t % 4], t // 4)
                        for k in range(un.kt):
                            if k == un.kt // 2:
                                yield
                            kk = un.k0 + k
                            if t == t0:
                                pe.wait_ge(split_done, split(kk) + 1)
                            cols = slice(m * P, (m + 1) * P)
                            start = un.first and k == 0
                            stop = un.last and k == un.kt - 1
                            pe.matmul(bank[:, :], wvh[:, k, cols], hi(kk), start=start, stop=False)
                            pe.matmul(bank[:, :], wvl[:, k, cols], hi(kk), start=False, stop=False)
                            mm = pe.matmul(bank[:, :], wvh[:, k, cols], lo(kk), start=False, stop=stop)
                        mm.then_inc(gemm_part, 1)
                        yield

            def h_granules(name, norm, lead=0, after_first=None):
                return granules(name, lambda k: hh[:, k, :], lambda k: hl[:, k, :], lambda k: split0[norm] + k,
                                lead, after_first)

            def run(gran, n=None):
                if n is None:
                    for _ in gran:
                        pass
                else:
                    for _ in range(n):
                        next(gran, None)

            def sum_squares(r):
                pe.wait_ge(sq_added, (KT - 1) * (r + 1))
                pe.matmul(mp[3][:, :], ones[:, :], sqsum[:, :], start=True, stop=True).then_inc(sum_ready, 1)

            pe.wait_ge(par_landed, 16 * N_PAR)
            pe.wait_ge(skip_ready, 1)
            for s, rows in enumerate((P, CW * 4, P, 48)):
                mm = pe.transpose(mp[0][:, s * P:s * P + rows], prow[0:rows, s, :], ident[0:rows, 0:rows])
            mm.then_inc(prm_turned, 1)
            for k in range(KT):
                pe.wait_ge(in_landed, 16 * NCH)
                if k >= 2:
                    pe.wait_ge(x_tile, k - 1)
                for c in range(NCH):
                    mm = pe.transpose(mp[1 + k % 2][:, c * P:(c + 1) * P], xin[:, c, k * P:(k + 1) * P], ident)
                mm.then_inc(x_turned, 1)
            sum_squares(0)

            def mamba():
                run(h_granules("dt", "pre0"))
                gran = h_granules("ssm", "pre0")

                def turn_dt():
                    pe.wait_ge(dt_v, DT_V)
                    for i, src in enumerate((acs, dtmp[6], dtmp[8])):
                        for c in range(NCH):
                            mm = pe.transpose(mp[2][:, (i * NCH + c) * SH:(i * NCH + c + 1) * SH],
                                              src[:, c * P:(c + 1) * P], ident[0:SH, 0:SH])
                    mm.then_inc(dt_turned, 1)

                def turn_and_cb(g):
                    xg = xs[:, g % 2]
                    for t in range(2):
                        pe.wait_ge(silu_done, 4 * g + t + 1)
                        pe.wait_ge(y_read, 2 * g)
                        for c in range(NCH):
                            mm = pe.transpose(mp[t][:, c * P:(c + 1) * P], xg[:, t, c * P:(c + 1) * P], ident)
                        mm.then_inc(xt_ready, 1)
                    pe.wait_ge(silu_done, 4 * g + 4)
                    pe.wait_ge(h_ready, g)
                    pe.wait_ge(tok_ready, 1)
                    for c in range(NCH - 1):
                        mm = pe.transpose(mp[2][:, c * P:(c + 1) * P], xg[:, 2, c * P:(c + 1) * P], ident)
                    mm.then_inc(bt_ready, 1)
                    for c in range(NCH):
                        s = slice(c * P, (c + 1) * P)
                        mm = pe.matmul(mp[3][:, s], xg[:, 2, s], xg[:, 3, s], start=True, stop=True)
                    mm.then_inc(cb_ready, 1)

                def spread(g, h):
                    if h < 2:
                        pe.wait_ge(xt_read, 2 * g + h + 1)
                    else:
                        pe.wait_ge(e_ready, 4 * g + h - 1)
                        pe.wait_ge(seg_ready, 4 * g + h - 1)
                    hd = HPG * g + h
                    pe.matmul(mp[h % 2][:, :], ident[0:SH, hd:hd + 1].to_broadcast([SH, P]), acs[:, :],
                              start=True, stop=True).then_inc(bc_ready, 1)

                def states(g):
                    pe.wait_ge(bt_read, g + 1)
                    pe.wait_ge(cb_read, g + 1)
                    pe.wait_ge(xt_read, 2 * g + 2)
                    for c in range(NCH - 1):
                        dst = mp[2][:, c * 256:(c + 1) * 256] if c < 2 else mp[3][:, 0:256]
                        mm = pe.matmul(dst, Bt[:, c, :], xde[:, c, :], start=True, stop=True)
                    mm.then_inc(st_ready, 1)

                def y_tile(g, t):
                    pe.wait_ge(e_ready, 4 * g + 3 + t)
                    pe.wait_ge(seg_ready, 4 * g + 3 + t)
                    pe.wait_ge(gc_ready, 4 * g + 2 * t + 2)
                    pe.wait_ge(h_ready, g + 1)
                    for j in range(2):
                        h = 2 * t + j
                        hs = slice(h * HD, (h + 1) * HD)
                        for c in range(NCH):
                            s = slice(c * P, (c + 1) * P)
                            dst = mp[t][j * HD:(j + 1) * HD, s]
                            mm = pe.matmul(dst, xdt[:, c, hs], G[:, h, s], start=True, stop=(c == 0))
                            if c:
                                mm = pe.matmul(dst, Hs[:, c - 1, hs], EC[:, h, s], start=False, stop=True)
                    mm.then_inc(y_ready, 1)

                for g in range(SG + 1):
                    def mix(slot):
                        if g == 0:
                            if slot == 2:
                                turn_dt()
                            return
                        p = g - 1
                        if slot == 0:
                            turn_and_cb(p)
                        elif slot == 1:
                            spread(p, 0)
                            spread(p, 1)
                        elif slot == 2:
                            spread(p, 2)
                            spread(p, 3)
                            states(p)
                        elif slot == 3:
                            y_tile(p, 0)
                        elif slot == 4:
                            y_tile(p, 1)

                    for slot in range(6):
                        run(gran, 2 if g < SG else 0)
                        mix(slot)
                pe.wait_ge(gate_sq, 1)
                pe.matmul(mp[3][:, :], ones[:, :], sqsum[:, :], start=True, stop=True).then_inc(gate_sum, 1)
                run(granules("ssm_out", lambda k: (hh if k < KT else hl)[:, k % KT, :],
                             lambda k: yl[:, k, :], lambda k: split0["y"] + k))
                pe.wait_ge(gate_rstd, 1)
                sum_squares(post_round[0])

            def attention():
                gran = h_granules("att", "pre1", 2, lambda: sum_squares(pre_round[1]))

                def rotate(h):
                    for j in range(3):
                        tile_taken(pe, tiles_of("att")[0] + 5 * h + j)
                        if j < 2:
                            pe.wait_ge(s_read, 8 * h)
                        else:
                            pe.wait_ge(pt_copied, 8 * h)
                        src = qraw[:, j, :] if j < 2 else kvraw[:, :]
                        pe.matmul(mp[j][:, :], cst[:, C_ROT:C_ROT + P], src, start=True,
                                  stop=True).then_inc(rot_ready, 1)
                    if h:
                        pe.wait_ge(value_ready, split0["att"] + 2 * h - 1 + 1)
                    for c in range(NCH):
                        mm = pe.transpose(mp[3][:, c * P:(c + 1) * P], kvraw[:, c * P:(c + 1) * P], ident)
                    mm.then_inc(v_turned, 1)

                def scores(h, i):
                    t, n = i // 4, i % 4
                    pe.wait_ge(qk_ready, h + 1)
                    if i >= 2:
                        pe.wait_ge(s_read, 8 * h + i - 1)
                    for j in range(2):
                        k0 = max(n - 1, 0) * P
                        w = (n + 1) * P - k0
                        mm = pe.matmul(mp[i % 2][:, (j + 1) * UC - w:(j + 1) * UC],
                                       qr[:, h % 2, t, n * P:(n + 1) * P], kd[:, h % 2, j, k0:k0 + w],
                                       start=True, stop=True)
                    mm.then_inc(s_ready, 1)

                def turn_p(h, i):
                    pe.wait_ge(pn_ready, 8 * h + i + 1)
                    pe.wait_ge(pt_copied, 8 * h + i)
                    for j in range(2):
                        for half in range(2):
                            if i % 4 or half:
                                mm = pe.transpose(mp[2][:, (2 * j + half) * P:(2 * j + half + 1) * P],
                                                  pp[:, i % 2, j, half * P:(half + 1) * P], ident)
                    mm.then_inc(pt_turned, 1)

                def pv(h, i):
                    t, n = i // 4, i % 4
                    pe.wait_ge(pt_copied, 8 * h + i + 1)
                    if i == 4:
                        pe.wait_ge(value_ready, split0["att"] + 2 * h + 1)
                    for j in range(2):
                        for half in range(0 if n else 1, 2):
                            mm = pe.matmul(mp[3][j * HD:(j + 1) * HD, n * P:(n + 1) * P],
                                           vt[:, h % 2, n - 1 + half, :], pT[:, i % 2, j, half, :],
                                           start=(half == 0 or n == 0), stop=(half == 1))
                    mm.then_inc(pv_done, 1)

                for h in range(KVH + 1):
                    for k in range(11):
                        run(gran, 1 if h < KVH and k < 10 else 0)
                        if h:
                            if 0 <= k - 2 < 8:
                                turn_p(h - 1, k - 2)
                            if 0 <= k - 3 < 8:
                                pv(h - 1, k - 3)
                            if k < 8:
                                scores(h - 1, k)
                    if h < KVH:
                        rotate(h)
                run(granules("att_out", lambda k: oh[:, k, :], lambda k: ol[:, k, :], lambda k: split0["att"] + k))
                sum_squares(post_round[1])

            def conv_pool():
                run(h_granules("cp", "pre2", 2, lambda: sum_squares(pre_round[2])))
                for g in range(4):
                    pe.wait_ge(window_ready, g + 1)
                    pe.wait_ge(poolw_landed, 16)
                    if g >= 1:
                        pe.wait_ge(value_ready, split0["cp"] + g - 1 + 1)
                    pe.matmul(mp[2][:, :], poolw[:, g, :], dp[:, g % 2, :], start=True,
                              stop=True).then_inc(pool_ready, 1)
                for t in range(4):
                    pe.wait_ge(conv_ready, t + 1)
                    mm = pe.matmul(mp[0][:, :], ones[:, :], acc[:, t, :], start=(t == 0), stop=(t == 3))
                mm.then_inc(mean_ready, 1)
                for t in range(4):
                    pe.wait_ge(lsq_ready, t + 1)
                    pe.matmul(mp[1][:, :], ones[:, :], sq[:, t % 2, :], start=(t == 0),
                              stop=(t == 3)).then_inc(var_ready, 1)
                run(granules("cp_out", lambda k: ch[:, k, :], lambda k: cl[:, k, :],
                             lambda k: split0["cp"] + (k + 4) % KT))

            def ffn(i, v):
                run(h_granules(f"up{i}", f"pre{v}", 1, lambda: sum_squares(pre_round[v])))
                run(granules(f"down{i}", lambda k: gh[:, k, :], lambda k: gl[:, k, :],
                             lambda k: split0[f"up{i}"] + k))
                sum_squares(pre_round[v + 1])

            def hgrn():
                gran = h_granules("hg", "pre4", 2)

                def level(n, s):
                    m = 8 * n + s
                    b, j = n // 2 % 2, n % 2
                    if m >= 2:
                        pe.wait_ge(lv_read, m - 1)
                    if s:
                        pe.wait_ge(x_ready, 7 * n + s)
                    else:
                        pe.wait_ge(hb_ready, n + 1)
                        tile_taken(pe, tiles_of("hg")[0] + 8 * (n // 2) + j)
                    x = XL[:, (7 * n + s - 1) % 3, :]
                    for c in range(NCH):
                        cs = slice(c * P, (c + 1) * P)
                        mm = pe.matmul(mp[m % 2][:, cs], x[:, cs] if s else hk[:, b, j, cs],
                                       x[:, cs] if s else hq[:, b, j, cs], start=True, stop=True)
                    mm.then_inc(lv_ready, 1)

                def turn_k(n):
                    pe.wait_ge(ke_ready, n + 1)
                    pe.wait_ge(vt_ready, 2 * (n // 2 + 1))
                    pe.wait_ge(hs_ready, n)
                    for c in range(NCH - 1):
                        mm = pe.transpose(mp[2][:, c * P:(c + 1) * P], Ke[:, c, :], ident)
                    mm.then_inc(kt_turned, 1)

                def states(n):
                    b, j = n // 2 % 2, n % 2
                    pe.wait_ge(kt_ready, n + 1)
                    if n:
                        pe.wait_ge(hrstd_ready, n)
                    for c in range(NCH - 1):
                        cs = slice(c * P, (c + 1) * P)
                        mm = pe.matmul(mp[2][:, cs], Kt[:, c, :], hvt[:, b, j, cs], start=True, stop=True)
                    mm.then_inc(hst_ready, 1)

                def turn_v(p, j):
                    tile_taken(pe, tiles_of("hg")[0] + 8 * p + 4 + j)
                    if j == 0:
                        pe.wait_ge(hs_ready, 2 * p)
                    else:
                        pe.wait_ge(vt_ready, 2 * p + 1)
                    for c in range(NCH):
                        mm = pe.transpose(mp[2][:, c * P:(c + 1) * P], hvt[:, p % 2, j, c * P:(c + 1) * P], ident)
                    mm.then_inc(vt_turned, 1)

                def output(n):
                    b, j = n // 2 % 2, n % 2
                    pe.wait_ge(lv_read, 8 * n + 8)
                    pe.wait_ge(hs_ready, n + 1)
                    pe.wait_ge(qe_ready, n + 1)
                    if n:
                        pe.wait_ge(hscaled, n)
                    for c in range(NCH):
                        cs = slice(c * P, (c + 1) * P)
                        mm = pe.matmul(mp[3][:, cs], hvt[:, b, j, cs], SM[:, n % 2, cs], start=True, stop=(c == 0))
                        if c:
                            mm = pe.matmul(mp[3][:, cs], St[:, c - 1, :], Qe[:, c - 1, :], start=False, stop=True)
                    mm.then_inc(ho_ready, 1)

                def head_sum(n):
                    pe.wait_ge(hsq_ready, n + 1)
                    if n + 1 < HH:
                        pe.wait_ge(kt_ready, n + 2)
                    pe.matmul(mp[2][:, :], ones[:, :], sq[:, n % 2, :], start=True, stop=True).then_inc(hsum_ready, 1)

                for p in range(HH // 2 + 1):
                    for k in range(16):
                        n, s = 2 * (p - 1) + k // 8, k % 8
                        run(gran, 1 if p < HH // 2 else 0)
                        if p:
                            level(n, s)
                            if s == 1 and n:
                                output(n - 1)
                            elif s == 2:
                                turn_k(n)
                            elif s == 3 and n:
                                head_sum(n - 1)
                            elif s == 5:
                                states(n)
                        if p < HH // 2 and k >= 14:
                            turn_v(p, k - 14)
                output(HH - 1)
                head_sum(HH - 1)
                run(granules("hg_out", lambda k: hoh[:, k, :], lambda k: hol[:, k, :], lambda k: split0["hg"] + k))

            for part in (mamba, attention, conv_pool, lambda: ffn(0, 3), hgrn, lambda: ffn(1, 5))[:PHASES]:
                part()
            if PHASES < 3:
                sum_squares(pre_round[PHASES])
            for c in range(NCH):
                for half in range(2):
                    n = 2 * c + half
                    if c == 0:
                        pe.wait_ge(final_ready, 4 * half + 4)
                    if n >= 2:
                        pe.wait_ge(out_ready, n - 1)
                    for j in range(4):
                        mm = pe.transpose(mp[half][:, j * P:(j + 1) * P],
                                          xT[:, 4 * half + j, c * P:(c + 1) * P], ident)
                    mm.then_inc(out_turned, 1)

        @block.scalar
        def _(act):
            steps = [0]

            def step(ins):
                ins.then_inc(act_step, 1)
                steps[0] += 1
                return steps[0]

            def after(n=None):
                act.wait_ge(act_step, steps[0] if n is None else n)

            def high(n, dst):
                act.wait_ge(value_ready, n + 1)
                act.activation(dst, val[:, n % 2, :], ACT.Copy).then_inc(hi_ready, 1)

            def square(r, k, src):
                if k:
                    n = (KT - 1) * r + k - 2
                    if n > 0:
                        act.wait_ge(sq_added, n)
                    dst = sq[:, k % 2, :]
                else:
                    if r:
                        act.wait_ge(sum_ready, r)
                    dst = sqsum[:, :]
                act.activation(dst, src[:, k, :], ACT.Square).then_inc(sq_ready, 1)

            def inverse_root(bank, n, dst):
                step(act.activation(root[:, :], bank[:, :], ACT.Ln, bias=eps_col[:, 0:1], scale=1.0 / n))
                after()
                return act.activation(dst, root[:, :], ACT.Exp, scale=-0.5)

            def take_rstd(r):
                act.wait_ge(sum_ready, r + 1)
                inverse_root(mp[3], D, rstd[:, :]).then_inc(rstd_ready, 1)

            def post_norm_of(i, yo):
                for k in range(KT):
                    tile_taken(act, out_tile(out_names[i], k))
                    square(post_round[i], k, yo)
                take_rstd(post_round[i])

            def pre_norm_of(v):
                r = pre_round[v]
                for k in range(KT):
                    if v in deferred:
                        if k == 0:
                            act.wait_ge(gemm_part, end_of(out_names[v - 1]) if v == 1 else end_of(order[v - 1][0]))
                        high(split0[f"pre{v}"] + k, hh[:, k, :])
                    x_wait(act, v, k)
                    square(r, k, xT)
                take_rstd(r)
                if v < PHASES and v not in deferred:
                    if v > 0:
                        act.wait_ge(gemm_part, end_of(order[v - 1][0]))
                    for k in range(KT):
                        high(split0[f"pre{v}"] + k, hh[:, k, :])

            def load(dst, src):
                act.dma_start(dst, src).then_inc(par_landed, 16)

            def rows(s, r0, n, src):
                load(prow[r0:r0 + n, s, :], src)

            load(cst[:, :], shape_const)
            rows(0, 0, P, ssm_conv_w.rearrange("o k (t p) -> (o k t) p", p=P))
            rows(1, 0, CW * 4, cp_dw_w.rearrange("o k (t p) -> (o k t) p", p=P))
            rows(2, 0, 16, pre_norm.rearrange("l (t p) -> (l t) p", p=P))
            rows(2, 16, 16, post_norm.rearrange("l (t p) -> (l t) p", p=P))
            rows(2, 32, 32, ssm_conv_b.rearrange("l (t p) -> (l t) p", p=P))
            rows(2, 64, 16, ssm_gate_norm.rearrange("l (t p) -> (l t) p", p=P))
            rows(2, 80, 16, norm_mix.rearrange("l (t p) -> (l t) p", p=P))
            rows(2, 96, 16, norm_ffn.rearrange("l (t p) -> (l t) p", p=P))
            rows(2, 112, 8, final_g.rearrange("(t p) -> t p", p=P))
            rows(2, 120, 8, hg_gn_g.rearrange("l (t p) -> (l t) p", p=P))
            rows(3, 0, 4, cp_dw_b.rearrange("l (t p) -> (l t) p", p=P))
            rows(3, 4, 4, cp_ln_g.rearrange("l (t p) -> (l t) p", p=P))
            rows(3, 8, 4, cp_ln_b.rearrange("l (t p) -> (l t) p", p=P))
            rows(3, 12, 4, cp_pool_scale.rearrange("l (t p) -> (l t) p", p=P))
            rows(3, 16, 16, hg_lb_logits.rearrange("l (t p) -> (l t) p", p=P))
            load(skip_raw[:, :], ssm_d.rearrange("o (t j) -> (o t) j", j=2))
            load(hcol[:, 0:1], ssm_dt_bias.rearrange("o h -> h o"))
            load(hcol[:, 1:2], ssm_a_log.rearrange("o h -> h o"))

            act.wait_ge(const_set, 1)
            pre_norm_of(0)

            def mamba():
                u, ab, e, w, lw = dtmp[0:5]
                act.activation(hcol[:, 2:3], hcol[:, 1:2], ACT.Exp).then_inc(dt_a, 1)
                tile_whole(act, 0)
                act.activation(u[:, :], gp[0][0:SH, :], ACT.Identity, bias=hcol[:, 0:1]).then_inc(bank_read[0], 1)
                tile_taken(act, 0)
                step(act.activation(ab[:, :], u[:, :], ACT.Abs))
                after()
                act.activation(e[:, :], ab[:, :], ACT.Exp, scale=-1.0).then_inc(dt_a, 1)
                act.wait_ge(dt_v, 1)
                act.activation(lw[:, :], w[:, :], ACT.Ln).then_inc(dt_a, 1)
                act.wait_ge(dt_v, DT_V - 1)
                act.activation(dtmp[7][:, :], dtmp[7][:, :], ACT.Exp).then_inc(dt_a, 1)

                def take_conv(g, j):
                    t = tiles_of("ssm")[0] + 6 * g + j
                    n = 4 * g + j
                    col = P_CONVW + 3 * 32 + conv_tile(g, j)
                    tile_whole(act, t)
                    if n >= 2:
                        act.wait_ge(conv_done, n - 1)
                    if g >= 2:
                        act.wait_ge(y_read, 2 * (g - 1))
                    step(act.activation(raw[:, n % 2, TAPS - 1:], gp[t % 4][:, :], ACT.Copy))
                    act.activation(xs[:, g % 2, j, :], gp[t % 4][:, :], ACT.Copy,
                                   scale=prm[:, col:col + 1]).then_inc(bank_read[t % 4], 1)

                def silu(g, j):
                    col = P_CONVB + conv_tile(g, j)
                    act.wait_ge(conv_done, 4 * g + j + 1)
                    v = xs[:, g % 2, j, :]
                    act.activation(v, v, ACT.Silu, bias=prm[:, col:col + 1]).then_inc(silu_done, 1)

                def take_z(g, j):
                    t = tiles_of("ssm")[0] + 6 * g + 4 + j
                    tile_whole(act, t)
                    if g:
                        act.wait_ge(yg_ready, 2 * g)
                    act.activation(sz[:, j, :], gp[t % 4][:, :], ACT.Silu).then_inc(bank_read[t % 4], 1)

                def copy_B(g):
                    act.wait_ge(bt_ready, g + 1)
                    act.activation(Bt[:, :, :].rearrange("p c n -> p (c n)"), mp[2][:, 0:3 * P],
                                   ACT.Copy).then_inc(bt_read, 1)

                def decay(g, h):
                    act.wait_ge(bc_ready, 4 * g + h + 1)
                    if h == 0:
                        act.wait_ge(y_ready, 2 * g)
                    act.activation(EC[:, h, :], mp[h % 2][:, :], ACT.Exp).then_inc(e_ready, 1)
                    act.wait_ge(seg_ready, 4 * g + h + 1)
                    act.activation(G[:, h, :], G[:, h, :], ACT.Exp).then_inc(dec_ready, 1)

                def gate_square(g, t):
                    n = 2 * g + t
                    act.wait_ge(yg_ready, n + 1)
                    act.activation(sq[:, t, :], val[:, t, :], ACT.Square).then_inc(gsq_ready, 1)

                for g in range(SG + 1):
                    p = g - 1
                    for slot in range(6):
                        if g < SG:
                            if slot < 4:
                                take_conv(g, slot)
                        if g > 0:
                            if slot == 0:
                                copy_B(p)
                            elif slot == 1:
                                decay(p, 0)
                                decay(p, 1)
                            elif slot == 2:
                                decay(p, 2)
                                decay(p, 3)
                            elif slot == 3:
                                gate_square(p, 0)
                            elif slot == 4:
                                gate_square(p, 1)
                        if g < SG:
                            if slot >= 4:
                                take_z(g, slot - 4)
                            if 2 <= slot < 4:
                                silu(g, slot - 2)
                            if slot == 5:
                                silu(g, 2)
                                silu(g, 3)
                act.wait_ge(gate_sum, 1)
                inverse_root(mp[3], SI, rg[:, :]).then_inc(gate_rstd, 1)
                act.wait_ge(gemm_part, end_of("ssm"))
                for k in range(16):
                    act.wait_ge(value_ready, split0["y"] + k + 1)
                    act.activation((hh if k < KT else hl)[:, k % KT, :], y[:, k, :], ACT.Copy).then_inc(hi_ready, 1)
                post_norm_of(0, yo_m)

            def attention():
                act.dma_start(posi[:, :], positions[0:1, :].to_broadcast([P, L])).then_inc(posi_landed, 16)
                act.dma_start(sinks[:, :], att_sinks[0:1, :].to_broadcast([P, 16])).then_inc(posi_landed, 16)

                def gate(h, j):
                    tile_taken(act, tiles_of("att")[0] + 5 * h + 3 + j)
                    v = sgate[:, h % 2, j, :]
                    act.activation(v, v, ACT.Silu).then_inc(silu_ready, 1)

                def exps(h, i):
                    act.wait_ge(m_ready, 8 * h + i + 1)
                    b = i % 2
                    k0 = 0 if i % 4 else P
                    for j in range(2):
                        v = pp[:, b, j, k0:]
                        act.activation(v, v, ACT.Exp, bias=srow[:, b, 2 + j:3 + j], scale=0.125,
                                       accum_out=srow[:, b, 6 + j:7 + j])
                    act.activation(srow[:, b, 8:10], srow[:, b, 4:6], ACT.Exp).then_inc(p_ready, 1)

                def copy_p(h, i):
                    act.wait_ge(pt_turned, 8 * h + i + 1)
                    if i >= 2 or h:
                        act.wait_ge(pv_done, 8 * h + i - 1)
                    k0 = 0 if i % 4 else 1
                    act.activation(pT[:, i % 2, :, k0:, :],
                                   mp[2][:, :].rearrange("p (j k i) -> p j k i", j=2, k=2)[:, :, k0:, :],
                                   ACT.Copy).then_inc(pt_copied, 1)

                act.wait_ge(trig_ready, 1)
                act.activation(sinT[:, :], sinT[:, :], ACT.Sin)
                act.activation(cosT[:, :], cosT[:, :], ACT.Sin).then_inc(sin_done, 1)
                for h in range(KVH + 1):
                    for k in range(12):
                        if h:
                            if 0 <= k - 2 < 8:
                                copy_p(h - 1, k - 2)
                            if k in (7, 11):
                                n = 2 * (h - 1) + (k == 11)
                                high(split0["att"] + n, oh[:, n, :])
                            if k < 8:
                                exps(h - 1, k)
                        if h < KVH and k in (7, 9):
                            gate(h, (k - 7) // 2)
                post_norm_of(1, yo_a)

            def conv_pool():
                act.dma_start(poolw[:, :, :], cp_pool_w[0].rearrange("g c d -> c g d")).then_inc(poolw_landed, 16)
                t0 = tiles_of("cp")[0]
                for half in range(2):
                    for j in range(2):
                        t = t0 + 4 * half + j
                        tile_taken(act, t)
                        act.activation(sig[:, j, :], sig[:, j, :], ACT.Sigmoid).then_inc(sig_ready, 1)
                n0 = split0["cp"]
                for g in range(4):
                    high(n0 + g, ch[:, 4 + g, :])
                for t in range(4):
                    act.wait_ge(centred, t + 1)
                    if t >= 2:
                        act.wait_ge(var_ready, t - 1)
                    act.activation(sq[:, t % 2, :], acc[:, t, :], ACT.Square).then_inc(lsq_ready, 1)
                act.wait_ge(var_ready, 4)
                inverse_root(mp[1], 4 * P, lrstd[:, :]).then_inc(lrstd_ready, 1)
                for t in range(4):
                    act.wait_ge(ln_ready, t + 1)
                    act.activation(acc[:, t, :], acc[:, t, :], ACT.Silu,
                                   bias=prm[:, P_LNB + t:P_LNB + t + 1]).then_inc(value_ready, 1)
                    act.wait_ge(value_ready, n0 + 4 + t + 1)
                    act.activation(ch[:, t, :], acc[:, t, :], ACT.Copy).then_inc(hi_ready, 1)

            def ffn(i, v):
                t0, n0 = tiles_of(f"up{i}")[0], split0[f"up{i}"]
                for n in range(FT // 2):
                    for j in range(2):
                        tile_taken(act, t0 + 4 * n + j)
                        act.activation(sq[:, j, :], sq[:, j, :], ACT.Silu).then_inc(silu_ready, 1)
                    for j in range(2):
                        high(n0 + 2 * n + j, gh[:, 2 * n + j, :])

            def hgrn():
                act.dma_start(lmask[:, :, :].rearrange("p l t -> p (l t)"), level_mask).then_inc(mask_landed, 16)
                act.wait_ge(lb_diff, 1)
                act.activation(lbc[:, 0:2, :], lbc[:, 0:2, :], ACT.Exp).then_inc(lb_exp, 1)
                t0 = tiles_of("hg")[0]

                def take(p, j):
                    t = t0 + 8 * p + j
                    b = p % 2
                    tile_whole(act, t)
                    if j < 2:
                        dst, f = hq[:, b, j, :], ACT.Copy
                    elif j < 4:
                        dst, f = hb[:, b, j - 2, :], ACT.Sigmoid
                    elif j < 6:
                        dst, f = hvt[:, b, j - 4, :], ACT.Copy
                    else:
                        q = 2 * p + j - 6
                        if q >= 3:
                            act.wait_ge(value_ready, split0["hg"] + q - 3 + 1)
                        dst, f = hg[:, q % 3, :], ACT.Silu
                    if j < 6 and p >= 2:
                        act.wait_ge(ho_ready, 2 * (p - 1))
                    act.activation(dst, gp[t % 4][:, :], f).then_inc(bank_read[t % 4], 1)

                def log_f(p, j):
                    act.wait_ge(f_ready, 2 * p + j + 1)
                    v = hb[:, p % 2, j, :]
                    act.activation(v, v, ACT.Ln).then_inc(ln_f, 1)

                def level_exp(m):
                    n, s = m // 8, m % 8
                    if s and n < HH:
                        x = XL[:, (7 * n + s - 1) % 3, :]
                        act.wait_ge(diff_ready, 7 * n + s)
                        act.activation(x, x, ACT.Exp, scale=-1.0).then_inc(dexp_ready, 1)

                def key_exp(n):
                    act.wait_ge(ke_diff, n + 1)
                    ke = Ke[:, :, :].rearrange("p c t -> p (c t)")
                    act.activation(ke, ke, ACT.Exp).then_inc(ke_exp, 1)

                def query_exp(n):
                    b, j = n // 2 % 2, n % 2
                    act.wait_ge(ho_ready, n) if n else None
                    act.activation(ebl[:, n % 2, :], hb[:, b, j, P - 1::P], ACT.Exp)
                    act.activation(Qe[:, :, :].rearrange("p c t -> p (c t)"), hb[:, b, j, P:],
                                   ACT.Exp).then_inc(qe_exp, 1)

                def copy_kt(n):
                    act.wait_ge(kt_turned, n + 1)
                    act.activation(Kt[:, :, :].rearrange("p c t -> p (c t)"), mp[2][:, 0:3 * P],
                                   ACT.Copy).then_inc(kt_ready, 1)

                def copy_vt(p, j):
                    act.wait_ge(vt_turned, 2 * p + j + 1)
                    if p >= 2:
                        act.wait_ge(ho_ready, 2 * (p - 1))
                    act.activation(hvt[:, p % 2, j, :], mp[2][:, :], ACT.Copy).then_inc(vt_ready, 1)

                def head_square(n):
                    act.wait_ge(ho_ready, n + 1)
                    if n >= 2:
                        act.wait_ge(hsum_ready, n - 1)
                    act.activation(sq[:, n % 2, :], mp[3][:, :], ACT.Square).then_inc(hsq_ready, 1)

                def head_root(n):
                    act.wait_ge(hsum_ready, n + 1)
                    if n:
                        act.wait_ge(hscaled, n)
                    inverse_root(mp[2], P, rstd[:, :]).then_inc(hrstd_ready, 1)

                def head_high(n):
                    high(split0["hg"] + n, hoh[:, n, :])

                for p in range(HH // 2 + 1):
                    for k in range(16):
                        n, s = 2 * (p - 1) + k // 8, k % 8
                        if p:
                            level_exp(8 * n + s + 2)
                            if s == 0:
                                key_exp(n)
                            elif s == 1 and n:
                                head_square(n - 1)
                            elif s == 2:
                                copy_kt(n)
                                query_exp(n)
                            elif s == 3 and n:
                                head_root(n - 1)
                            elif s == 5 and n:
                                head_high(n - 1)
                        if p < HH // 2:
                            if k % 2:
                                take(p, k // 2)
                            if k in (7, 9):
                                log_f(p, (k - 7) // 2)
                            if k >= 14:
                                copy_vt(p, k - 14)
                    if p == 0:
                        level_exp(1)
                head_square(HH - 1)
                head_root(HH - 1)
                head_high(HH - 1)

            mixers = (mamba, attention, conv_pool, lambda: ffn(0, 3), hgrn, lambda: ffn(1, 5))
            for v in range(PHASES):
                mixers[v]()
                pre_norm_of(v + 1)
            for c in range(NCH):
                n = 2 * c + 1
                act.wait_ge(out_turned, n)
                act.activation(xin[:, c, 0:512], mp[0][:, :], ACT.Copy).then_inc(out_ready, 1)
                act.wait_ge(out_turned, n + 1)
                act.activation(xin[:, c, 512:1024], mp[1][:, :], ACT.Copy).then_inc(out_ready, 1)

        @block.vector
        def _(dve):
            steps = [0]

            def step(ins):
                ins.then_inc(dve_step, 1)
                steps[0] += 1
                return steps[0]

            def after(n=None):
                dve.wait_ge(dve_step, steps[0] if n is None else n)

            norm_cols = (P_PRE, P_PRE + KT, P_MIX, P_FFN, P_MIX + KT, P_FFN + KT, P_FINAL)

            def value_slot(n):
                if n >= 2:
                    dve.wait_ge(split_done, n - 1)
                return val[:, n % 2, :]

            def low(n, hi, lo):
                dve.wait_ge(hi_ready, n + 1)
                dve.tensor_tensor(lo, val[:, n % 2, :], hi.bitcast(F32), ALU.subtract).then_inc(split_done, 1)

            def add_square(r, k):
                if k:
                    dve.wait_ge(sq_ready, KT * r + k + 1)
                    n = (KT - 1) * r + k - 1
                    if k > 1:
                        dve.wait_ge(sq_added, n)
                    dve.tensor_tensor(sqsum[:, :], sqsum[:, :], sq[:, k % 2, :], ALU.add).then_inc(sq_added, 1)

            def value_of_x(v, k):
                x_wait(dve, v, k)
                col = norm_cols[v] + k
                dve.tensor_scalar(value_slot(split0[f"pre{v}"] + k), xT[:, k, :], prm[:, col:col + 1], None,
                                  ALU.mult).then_inc(value_ready, 1)

            def low_of_x(v, k):
                if k == 0:
                    dve.wait_ge(gemm_part, end_of(out_names[v - 1]) if v == 1 else end_of(order[v - 1][0]))
                low(split0[f"pre{v}"] + k, hh[:, k, :], hl[:, k, :])
                add_square(pre_round[v], k)

            def pre_norm_of(v):
                if v in deferred:
                    dve.wait_ge(rstd_ready, pre_round[v] + 1)
                    return
                col = norm_cols[v]
                dve.wait_ge(rstd_ready, pre_round[v] + 1)
                if v < PHASES:
                    if v > 0:
                        dve.wait_ge(gemm_part, end_of(order[v - 1][0]))
                    n0 = split0[f"pre{v}"]
                    for k in range(KT + 1):
                        if k < KT:
                            dve.scalar_tensor_tensor(value_slot(n0 + k), xT[:, k, :], prm[:, col + k:col + k + 1],
                                                     rstd[:, :], ALU.mult, ALU.mult).then_inc(value_ready, 1)
                        if k > 0:
                            low(n0 + k - 1, hh[:, k - 1, :], hl[:, k - 1, :])
                else:
                    for k in range(KT):
                        dve.scalar_tensor_tensor(xT[:, k, :], xT[:, k, :], prm[:, P_FINAL + k:P_FINAL + k + 1],
                                                 rstd[:, :], ALU.mult, ALU.mult).then_inc(final_ready, 1)

            def post_norm_of(i, yo):
                v = i + 1
                dve.wait_ge(rstd_ready, post_round[i] + 1)
                n = [0] * KT
                for k in range(KT + 2):
                    if k < KT:
                        col = P_POST + KT * i + k
                        n[k] = step(dve.scalar_tensor_tensor(yo[:, k, :], yo[:, k, :], prm[:, col:col + 1],
                                                             rstd[:, :], ALU.mult, ALU.mult))
                    if 0 < k <= KT:
                        after(n[k - 1])
                        dve.tensor_tensor(xT[:, k - 1, :], xT[:, k - 1, :], yo[:, k - 1, :],
                                          ALU.add).then_inc(x_tile, 1)
                        if v in deferred:
                            value_of_x(v, k - 1)
                    if k > 1:
                        if v in deferred:
                            low_of_x(v, k - 2)
                        else:
                            add_square(pre_round[v], k - 2)

            dve.memset(ones[:, :], 1.0)
            dve.memset(eps_col[:, :], EPS).then_inc(const_set, 1)
            dve.wait_ge(par_landed, 16 * N_PAR)
            dve.tensor_copy(prow[32:48, 3, :].rearrange("t (j d) -> t j d", j=2),
                            skip_raw[:, :].unsqueeze(2).to_broadcast([16, 2, HD])).then_inc(skip_ready, 1)
            dve.wait_ge(prm_turned, 1)
            step(dve.tensor_copy(prm[:, 0:252], mp[0][:, 0:252]))
            step(dve.tensor_copy(prm[:, 256:432], mp[0][:, 256:432]))
            after()
            for k in range(KT):
                dve.wait_ge(x_turned, k + 1)
                dve.tensor_copy(xT[:, k, :], mp[1 + k % 2][:, :]).then_inc(x_tile, 1)
                if k:
                    add_square(pre_round[0], k - 1)
            add_square(pre_round[0], KT - 1)
            pre_norm_of(0)

            def mamba():
                u, e, w, lw, a, dt, dx, co = (dtmp[0], dtmp[2], dtmp[3], dtmp[4], dtmp[5], dtmp[6],
                                              dtmp[8], dtmp[9])
                df = dtmp[7]
                step(dve.memset(raw[:, :, 0:TAPS - 1], 0.0))
                step(dve.memset(sqsum[:, :], 0.0))
                dve.wait_ge(dt_a, 2)
                step(dve.tensor_scalar(hcol[:, 3:4], hcol[:, 2:3], -1.0, None, ALU.mult))
                dve.tensor_scalar(w[:, :], e[:, :], 1.0, None, ALU.add).then_inc(dt_v, 1)
                dve.wait_ge(dt_v, 1)
                step(dve.tensor_scalar(co[:, :], w[:, :], -1.0, None, ALU.add))
                step(dve.reciprocal(dx[:, :], w[:, :]))
                after()
                step(dve.tensor_tensor(co[:, :], e[:, :], co[:, :], ALU.subtract))
                after()
                step(dve.tensor_tensor(co[:, :], co[:, :], dx[:, :], ALU.mult))
                dve.wait_ge(dt_a, 3)
                after()
                step(dve.tensor_tensor(co[:, :], co[:, :], lw[:, :], ALU.add))
                after()
                step(dve.scalar_tensor_tensor(dt[:, :], u[:, :], 0.0, co[:, :], ALU.max, ALU.add))
                after()
                step(dve.tensor_scalar(a[:, :], dt[:, :], hcol[:, 3:4], None, ALU.mult))
                after()
                step(dve.tensor_tensor_scan(acs[:, :], cst[0:SH, C_RESET:C_RESET + L], a[:, :], 0.0,
                                            ALU.mult, ALU.add))
                after()
                acs3 = acs[:, :].rearrange("h (c l) -> h c l", c=NCH)
                dve.tensor_tensor(df[:, :].rearrange("h (c l) -> h c l", c=NCH),
                                  acs3[:, :, P - 1:P].to_broadcast([SH, NCH, P]), acs3,
                                  ALU.subtract).then_inc(dt_v, 1)
                dve.wait_ge(dt_a, 4)
                dve.tensor_tensor(dx[:, :], df[:, :], dt[:, :], ALU.mult).then_inc(dt_v, 1)
                dve.wait_ge(dt_turned, 1)
                dve.tensor_copy(tokT[:, :, :, :].rearrange("p i c h -> p (i c h)"),
                                mp[2][:, 0:3 * NCH * SH]).then_inc(tok_ready, 1)
                dve.wait_ge(tok_ready, 1)

                def conv(g, j):
                    t = tiles_of("ssm")[0] + 6 * g + j
                    n = 4 * g + j
                    tile_taken(dve, t)
                    v = xs[:, g % 2, j, :]
                    for i in range(TAPS - 2, -1, -1):
                        col = P_CONVW + i * 32 + conv_tile(g, j)
                        ins = dve.scalar_tensor_tensor(v, raw[:, n % 2, i:i + L], prm[:, col:col + 1], v,
                                                       ALU.mult, ALU.add)
                        if i:
                            step(ins)
                            after()
                        else:
                            ins.then_inc(conv_done, 1)

                def scale_x(g, t):
                    dve.wait_ge(xt_ready, 2 * g + t + 1)
                    if t == 0:
                        dve.wait_ge(y_ready, 2 * g)
                    src = mp[t][:, :].rearrange("p (c h d) -> p c h d", c=NCH, h=2)
                    for dst, i, n in ((xdt, 1, NCH), (xde, 2, NCH - 1)):
                        o = dst[:, :, t * P:(t + 1) * P].rearrange("p c (h d) -> p c h d", h=2)
                        f = tokT[:, i, 0:n, HPG * g + 2 * t:HPG * g + 2 * t + 2].unsqueeze(3).to_broadcast([P, n, 2, HD])
                        ins = dve.tensor_tensor(o, src[:, 0:n], f, ALU.mult)
                        if i == 1:
                            step(ins)
                    ins.then_inc(xt_read, 1)

                def mask_cb(g):
                    dve.wait_ge(cb_ready, g + 1)
                    m = cst[:, C_CAUSAL:C_CAUSAL + P].unsqueeze(1).to_broadcast([P, NCH, P])
                    dve.tensor_tensor(cbm[:, :, :], mp[3][:, :].rearrange("p (c l) -> p c l", c=NCH), m,
                                      ALU.mult).then_inc(cb_read, 1)

                def segment(g, h):
                    dve.wait_ge(e_ready, 4 * g + h + 1)
                    for c in range(NCH):
                        s = slice(c * P, (c + 1) * P)
                        f = tokT[:, 0, c, HPG * g + h:HPG * g + h + 1]
                        ins = dve.tensor_scalar(G[:, h, s], mp[h % 2][:, s], f, f, ALU.min, ALU.subtract)
                        if c < NCH - 1:
                            step(ins)
                    ins.then_inc(seg_ready, 1)

                def products(g, h):
                    dve.wait_ge(dec_ready, 4 * g + h + 1)
                    dve.wait_ge(cb_read, g + 1)
                    step(dve.tensor_copy(cd[:, h, :], EC[:, h, P - 1::P]))
                    step(dve.tensor_tensor(G[:, h, :], G[:, h, :], cbm[:, :, :].rearrange("p c l -> p (c l)"), ALU.mult))
                    after()
                    dve.tensor_tensor(EC[:, h, :], EC[:, h, :], xs[:, g % 2, 3, :], ALU.mult).then_inc(gc_ready, 1)

                def recur(g):
                    dve.wait_ge(st_ready, g + 1)
                    step(dve.tensor_copy(Hs[:, 0, :], mp[2][:, 0:256]))
                    for c in (1, 2):
                        after()
                        f = cd[:, :, c].unsqueeze(2).to_broadcast([P, HPG, HD])
                        step(dve.tensor_tensor(Hs[:, c, :].rearrange("p (h d) -> p h d", h=HPG),
                                               Hs[:, c - 1, :].rearrange("p (h d) -> p h d", h=HPG), f, ALU.mult))
                        after()
                        ins = dve.tensor_tensor(Hs[:, c, :], Hs[:, c, :],
                                                mp[2][:, 256:512] if c == 1 else mp[3][:, 0:256], ALU.add)
                        if c == 1:
                            step(ins)
                    ins.then_inc(h_ready, 1)

                def gate_y(g, t):
                    n = 2 * g + t
                    col = P_SKIP + n
                    dve.wait_ge(y_ready, n + 1)
                    tile_taken(dve, tiles_of("ssm")[0] + 6 * g + 4 + t)
                    if n >= 2:
                        dve.wait_ge(gsq_ready, n - 1)
                    v = val[:, t, :]
                    dve.scalar_tensor_tensor(v, xs[:, g % 2, t, :], prm[:, col:col + 1], mp[t][:, :],
                                             ALU.mult, ALU.add).then_inc(y_read, 1)
                    dve.wait_ge(y_read, n + 1)
                    dve.tensor_tensor(v, v, sz[:, t, :], ALU.mult).then_inc(yg_ready, 1)
                    dve.wait_ge(yg_ready, n + 1)
                    dve.tensor_scalar(y[:, n, :], v, prm[:, P_GATE + n:P_GATE + n + 1], None,
                                      ALU.mult).then_inc(value_ready, 1)
                    dve.wait_ge(gsq_ready, n + 1)
                    ins = dve.tensor_tensor(sqsum[:, :], sqsum[:, :], sq[:, t, :], ALU.add)
                    if n < 15:
                        step(ins)
                        after()
                    else:
                        ins.then_inc(gate_sq, 1)

                for g in range(SG + 1):
                    p = g - 1
                    for slot in range(6):
                        if g > 0:
                            if slot == 0:
                                scale_x(p, 0)
                                scale_x(p, 1)
                                mask_cb(p)
                            elif slot == 1:
                                segment(p, 0)
                                segment(p, 1)
                                products(p, 0)
                                products(p, 1)
                            elif slot == 2:
                                segment(p, 2)
                                segment(p, 3)
                                products(p, 2)
                                products(p, 3)
                                recur(p)
                            elif slot == 3:
                                gate_y(p, 0)
                            elif slot == 4:
                                gate_y(p, 1)
                        if g < SG and 1 <= slot <= 4:
                            conv(g, slot - 1)
                dve.wait_ge(gemm_part, end_of("ssm"))
                n0 = split0["y"]
                for k in range(16):
                    dve.wait_ge(hi_ready, n0 + k + 1)
                    dve.tensor_tensor(yl[:, k, :], y[:, k, :], (hh if k < KT else hl)[:, k % KT, :].bitcast(F32),
                                      ALU.subtract).then_inc(split_done, 1)
                dve.wait_ge(gate_rstd, 1)
                for k in range(KT):
                    t = out_tile("ssm_out", k)
                    tile_whole(dve, t)
                    dve.tensor_tensor(yo_m[:, k, :], gp[t % 4][:, :], rg[:, :], ALU.mult).then_inc(bank_read[t % 4], 1)
                    if k:
                        add_square(post_round[0], k - 1)
                add_square(post_round[0], KT - 1)
                post_norm_of(0, yo_m)

            def attention():
                parts = two_pi_parts()
                posf, t0, t1 = trig[0], trig[1], trig[2]
                for b in range(2):
                    step(dve.memset(kd[HD:, b, 0, :], 0.0))
                    step(dve.memset(kd[0:HD, b, 1, :], 0.0))
                dve.wait_ge(posi_landed, 32)
                step(dve.tensor_copy(posf[:, :], posi[:, :]))
                after()
                step(dve.tensor_scalar(posf[:, :], posf[:, :], cst[:, C_INV:C_INV + 1], None, ALU.mult))
                after()
                for dst, shift in ((sinT, 0.0), (cosT, 0.25)):
                    step(dve.tensor_scalar(t0[:, :], posf[:, :], 0.15915494309189535, shift, ALU.mult, ALU.add))
                    after()
                    step(dve.tensor_scalar(t0[:, :], t0[:, :], MAGIC, None, ALU.add))
                    after()
                    step(dve.tensor_scalar(t0[:, :], t0[:, :], -MAGIC, None, ALU.add))
                    after()
                    src = posf
                    for c in parts:
                        step(dve.scalar_tensor_tensor(t1[:, :], t0[:, :], -c, src[:, :], ALU.mult, ALU.add))
                        after()
                        src = t1
                    if shift:
                        step(dve.tensor_scalar(t1[:, :], t1[:, :], float(np.pi / 2), None, ALU.add))
                        after()
                    ins = dve.tensor_scalar(dst[:, :], t1[:, :], PI_BELOW, -PI_BELOW, ALU.min, ALU.max)
                    if shift:
                        ins.then_inc(trig_ready, 1)
                    else:
                        step(ins)
                dve.wait_ge(sin_done, 1)

                def mask_scores(h, i):
                    dve.wait_ge(s_ready, 8 * h + i + 1)
                    if i >= 2 or h:
                        dve.wait_ge(pt_turned, 8 * h + i - 1)
                    b, k0 = i % 2, (0 if i % 4 else P)
                    v = pp[:, b, :, k0:]
                    src = mp[i % 2][:, :].rearrange("p (j k) -> p j k", j=2)[:, :, k0:]
                    band = cst[:, C_BAND + k0:C_BAND + UC].unsqueeze(1).to_broadcast([P, 2, UC - k0])
                    dve.tensor_tensor(v, src, band, ALU.add).then_inc(s_read, 1)
                    dve.wait_ge(s_read, 8 * h + i + 1)
                    step(dve.tensor_reduce(srow[:, b, 0:2], v, AX.X, ALU.max))
                    after()
                    sk = sinks[:, HPG * h + 2 * (i // 4):HPG * h + 2 * (i // 4) + 2]
                    step(dve.scalar_tensor_tensor(srow[:, b, 0:2], srow[:, b, 0:2], 0.125, sk, ALU.mult, ALU.max))
                    after()
                    step(dve.tensor_scalar(srow[:, b, 2:4], srow[:, b, 0:2], -1.0, None, ALU.mult))
                    dve.tensor_tensor(srow[:, b, 4:6], sk, srow[:, b, 0:2], ALU.subtract).then_inc(m_ready, 1)

                def normalise(h, i):
                    dve.wait_ge(p_ready, 8 * h + i + 1)
                    b, k0 = i % 2, (0 if i % 4 else P)
                    step(dve.tensor_tensor(srow[:, b, 6:8], srow[:, b, 6:8], srow[:, b, 8:10], ALU.add))
                    after()
                    step(dve.reciprocal(srow[:, b, 10:12], srow[:, b, 6:8]))
                    after()
                    step(dve.tensor_scalar(pp[:, b, 0, k0:], pp[:, b, 0, k0:], srow[:, b, 10:11], None, ALU.mult))
                    dve.tensor_scalar(pp[:, b, 1, k0:], pp[:, b, 1, k0:], srow[:, b, 11:12], None,
                                      ALU.mult).then_inc(pn_ready, 1)

                def gate_o(h, t):
                    n = split0["att"] + 2 * h + t
                    dve.wait_ge(pv_done, 8 * h + 4 * t + 4)
                    dve.wait_ge(silu_ready, 2 * h + t + 1)
                    dve.tensor_tensor(value_slot(n), mp[3][:, :], sgate[:, h % 2, t, :],
                                      ALU.mult).then_inc(value_ready, 1)

                def take(h, j):
                    t = tiles_of("att")[0] + 5 * h + j
                    tile_whole(dve, t)
                    if h:
                        dve.wait_ge(qk_ready, h)
                    dst = qraw[:, j, :] if j < 2 else kvraw[:, :] if j == 2 else sgate[:, h % 2, j - 3, :]
                    dve.tensor_tensor(dst, gp[t % 4][:, :], rstd[:, :], ALU.mult).then_inc(bank_read[t % 4], 1)

                def rope(h):
                    t0 = tiles_of("att")[0] + 5 * h
                    for j in range(3):
                        dve.wait_ge(rot_ready, 3 * h + j + 1)
                        tile_taken(dve, t0 + j)
                        rows = slice(0, P if j < 2 else HD)
                        src = qraw[rows, j, :] if j < 2 else kvraw[rows, :]
                        dst = qr[rows, h % 2, j, :] if j < 2 else kd[rows, h % 2, 0, :]
                        if j:
                            after()
                        step(dve.tensor_tensor(rtmp[rows, 0, :], mp[j][rows, :], sinT[rows, :], ALU.mult))
                        step(dve.tensor_tensor(rtmp[rows, 1, :], src, cosT[rows, :], ALU.mult))
                        after()
                        step(dve.tensor_tensor(dst, rtmp[rows, 0, :], rtmp[rows, 1, :], ALU.add))
                    after()
                    step(dve.tensor_copy(kd[HD:, h % 2, 1, :], kd[0:HD, h % 2, 0, :]))
                    dve.wait_ge(v_turned, h + 1)
                    dve.tensor_copy(vt[:, h % 2, :, :], mp[3][:, :].rearrange("p (c d) -> p c d", c=NCH)[:, :, HD:]
                                    ).then_inc(qk_ready, 1)

                for h in range(KVH + 1):
                    for k in range(12):
                        if h:
                            if k in (7, 11):
                                gate_o(h - 1, int(k == 11))
                            if k < 8:
                                mask_scores(h - 1, k)
                            if 1 <= k <= 8:
                                normalise(h - 1, k - 1)
                            if k in (7, 11):
                                n = 2 * (h - 1) + (k == 11)
                                low(split0["att"] + n, oh[:, n, :], ol[:, n, :])
                        if h < KVH and k % 2 and k < 10:
                            take(h, k // 2)
                    if h < KVH:
                        rope(h)
                for k in range(KT):
                    t = out_tile("att_out", k)
                    tile_whole(dve, t)
                    dve.tensor_copy(yo_a[:, k, :], gp[t % 4][:, :]).then_inc(bank_read[t % 4], 1)
                    if k:
                        add_square(post_round[1], k - 1)
                add_square(post_round[1], KT - 1)
                post_norm_of(1, yo_a)

            def add_to_x(name, v):
                for k in range(KT + 1):
                    if k < KT:
                        t = out_tile(name, k)
                        tile_whole(dve, t)
                        dve.tensor_tensor(xT[:, k, :], gp[t % 4][:, :], xT[:, k, :], ALU.add).then_inc(bank_read[t % 4], 1)
                        if v in deferred:
                            value_of_x(v, k)
                    if k > 0:
                        if v in deferred:
                            low_of_x(v, k - 1)
                        else:
                            add_square(pre_round[v], k - 1)

            def conv_pool():
                t0 = tiles_of("cp")[0]
                step(dve.memset(apad[:, :, 0:CW - 1], 0.0))
                step(dve.memset(ub[:, :, 0:16], 0.0))
                for half in range(2):
                    for j in range(2):
                        t = t0 + 4 * half + j
                        tile_whole(dve, t)
                        dve.tensor_tensor(sig[:, j, :], gp[t % 4][:, :], rstd[:, :], ALU.mult).then_inc(bank_read[t % 4], 1)
                    for j in range(2):
                        t = t0 + 4 * half + 2 + j
                        tile_whole(dve, t)
                        dve.tensor_tensor(apad[:, 2 * half + j, CW - 1:], gp[t % 4][:, :], rstd[:, :],
                                          ALU.mult).then_inc(bank_read[t % 4], 1)
                    for j in range(2):
                        tile_taken(dve, t0 + 4 * half + 2 + j)
                        dve.wait_ge(sig_ready, 2 * half + j + 1)
                        a = apad[:, 2 * half + j, CW - 1:]
                        gated = step(dve.tensor_tensor(a, a, sig[:, j, :], ALU.mult))
                    after(gated)
                    last = [0, 0]
                    for i in range(CW - 1, -1, -1):
                        for j in range(2):
                            c = 2 * half + j
                            col = P_DW + 4 * i + c
                            src, w = apad[:, c, i:i + L], prm[:, col:col + 1]
                            if i == CW - 1:
                                last[j] = step(dve.tensor_scalar(acc[:, c, :], src, w, prm[:, P_DWB + c:P_DWB + c + 1],
                                                                 ALU.mult, ALU.add))
                                continue
                            after(last[j])
                            ins = dve.scalar_tensor_tensor(acc[:, c, :], src, w, acc[:, c, :], ALU.mult, ALU.add)
                            if i:
                                last[j] = step(ins)
                            else:
                                ins.then_inc(conv_ready, 1)
                n0 = split0["cp"]
                for g in range(4):
                    t = t0 + 8 + g
                    tile_whole(dve, t)
                    dve.tensor_tensor(ub[:, g, 16:], gp[t % 4][:, :], rstd[:, :], ALU.mult).then_inc(bank_read[t % 4], 1)
                    tile_taken(dve, t)
                    src = ub[:, g, :]
                    w = 1
                    while w < POOLW[g]:
                        dst = ws[:, 0 if w in (1, 4) else 1, :]
                        step(dve.tensor_tensor(dst[:, 2 * w - 1:], src[:, 2 * w - 1:], src[:, w - 1:16 + L - w], ALU.add))
                        after()
                        src, w = dst, 2 * w
                    d = dp[:, g % 2, :]
                    if g >= 2:
                        dve.wait_ge(pool_ready, g - 1)
                    step(dve.tensor_scalar(d, src[:, 16:], 1.0 / w, None, ALU.mult))
                    after()
                    step(dve.tensor_tensor(d[:, 0:16], src[:, 16:32], cst[:, C_RC + 16 * g:C_RC + 16 * g + 16], ALU.mult))
                    after()
                    dve.tensor_tensor(d, d, ub[:, g, 16:], ALU.subtract).then_inc(window_ready, 1)
                    if g:
                        pooled(g - 1)
                pooled(3)
                dve.wait_ge(mean_ready, 1)
                for t in range(4):
                    dve.scalar_tensor_tensor(acc[:, t, :], mp[0][:, :], -1.0 / 512, acc[:, t, :], ALU.mult,
                                             ALU.add).then_inc(centred, 1)
                dve.wait_ge(lrstd_ready, 1)
                for t in range(4):
                    dve.scalar_tensor_tensor(acc[:, t, :], acc[:, t, :], prm[:, P_LNG + t:P_LNG + t + 1], lrstd[:, :],
                                             ALU.mult, ALU.mult).then_inc(ln_ready, 1)
                for t in range(4):
                    dve.wait_ge(hi_ready, n0 + 4 + t + 1)
                    dve.tensor_tensor(cl[:, t, :], acc[:, t, :], ch[:, t, :].bitcast(F32),
                                      ALU.subtract).then_inc(split_done, 1)
                add_to_x("cp_out", 3)

            def pooled(g):
                n = split0["cp"] + g
                dve.wait_ge(pool_ready, g + 1)
                dve.tensor_scalar(value_slot(n), mp[2][:, :], prm[:, P_PSC + g:P_PSC + g + 1], None,
                                  ALU.mult).then_inc(value_ready, 1)
                low(n, ch[:, 4 + g, :], cl[:, 4 + g, :])

            def ffn(i, v):
                t0, n0 = tiles_of(f"up{i}")[0], split0[f"up{i}"]
                for n in range(FT // 2):
                    for j in range(2):
                        t = t0 + 4 * n + j
                        tile_whole(dve, t)
                        dve.tensor_tensor(sq[:, j, :], gp[t % 4][:, :], rstd[:, :], ALU.mult).then_inc(bank_read[t % 4], 1)
                    for j in range(2):
                        t = t0 + 4 * n + 2 + j
                        tile_whole(dve, t)
                        dve.tensor_tensor(value_slot(n0 + 2 * n + j), gp[t % 4][:, :], rstd[:, :],
                                          ALU.mult).then_inc(bank_read[t % 4], 1)
                    for j in range(2):
                        tile_taken(dve, t0 + 4 * n + 2 + j)
                        dve.wait_ge(silu_ready, 2 * KVH + FT * (v // 5) + 2 * n + j + 1)
                        value = val[:, (n0 + j) % 2, :]
                        dve.tensor_tensor(value, value, sq[:, j, :], ALU.mult).then_inc(value_ready, 1)
                    for j in range(2):
                        low(n0 + 2 * n + j, gh[:, 2 * n + j, :], gl[:, 2 * n + j, :])
                add_to_x(f"down{i}", v + 1)

            def hgrn():
                t0 = tiles_of("hg")[0]
                l0, l1, s0 = prm[:, P_LB:P_LB + 8], prm[:, P_LB + 8:P_LB + 16], lbc[:, 2, :]
                step(dve.tensor_tensor(s0, l0, l1, ALU.max))
                after()
                step(dve.tensor_tensor(lbc[:, 0, :], l1, s0, ALU.subtract))
                dve.tensor_tensor(lbc[:, 1, :], l0, s0, ALU.subtract).then_inc(lb_diff, 1)
                dve.wait_ge(lb_exp, 1)
                step(dve.tensor_tensor(s0, lbc[:, 0, :], lbc[:, 1, :], ALU.add))
                after()
                step(dve.reciprocal(s0, s0))
                after()
                step(dve.tensor_tensor(lbc[:, 0, :], lbc[:, 0, :], s0, ALU.mult))
                after()
                step(dve.tensor_scalar(lbc[:, 1, :], lbc[:, 0, :], -1.0, 1.0, ALU.mult, ALU.add))
                after()
                dve.wait_ge(mask_landed, 16)

                def forget(p, j):
                    tile_taken(dve, t0 + 8 * p + 2 + j)
                    q, f = 2 * p + j, hb[:, p % 2, j, :]
                    dve.tensor_scalar(f, f, lbc[:, 1, q:q + 1], lbc[:, 0, q:q + 1], ALU.mult, ALU.add).then_inc(f_lin, 1)
                    dve.wait_ge(f_lin, q + 1)
                    dve.tensor_scalar(hk[:, p % 2, j, :], f, -1.0, 1.0, ALU.mult, ALU.add).then_inc(f_ready, 1)

                def scan(p, j):
                    dve.wait_ge(ln_f, 2 * p + j + 1)
                    b = hb[:, p % 2, j, :]
                    dve.tensor_tensor_scan(b, cst[:, C_RESET:C_RESET + L], b, 0.0, ALU.mult, ALU.add).then_inc(hb_ready, 1)

                def halves(v, w):
                    v = v.rearrange("p (n k w) -> p n k w", k=2, w=w)
                    return v[:, :, 0, :], v[:, :, 1, :]

                def level_diff(m):
                    n, s = m // 8, m % 8
                    if not s or n >= HH:
                        return
                    w, lv = LEVELS[s - 1], 7 * n + s - 1
                    dve.wait_ge(hb_ready, n + 1)
                    if lv >= 3:
                        dve.wait_ge(lv_ready, 8 * ((lv - 3) // 7) + (lv - 3) % 7 + 2)
                    (bl, br), (xl, xr) = halves(hb[:, n // 2 % 2, n % 2, :], w), halves(XL[:, lv % 3, :], w)
                    ref = bl[:, :, w - 1:w].to_broadcast([P, L // (2 * w), w])
                    step(dve.tensor_tensor(xl, bl, ref, ALU.subtract))
                    dve.tensor_tensor(xr, ref, br, ALU.subtract).then_inc(diff_ready, 1)

                def level_products(m):
                    n, s = m // 8, m % 8
                    if not s or n >= HH:
                        return
                    w, lv, b, j = LEVELS[s - 1], 7 * n + s - 1, n // 2 % 2, n % 2
                    dve.wait_ge(dexp_ready, lv + 1)
                    tile_taken(dve, t0 + 8 * (n // 2) + j)
                    (kl, _), (_, qright), (xl, xr) = halves(hk[:, b, j, :], w), halves(hq[:, b, j, :], w), halves(XL[:, lv % 3, :], w)
                    step(dve.tensor_tensor(xl, xl, kl, ALU.mult))
                    dve.tensor_tensor(xr, xr, qright, ALU.mult).then_inc(x_ready, 1)

                def collect(m):
                    n, s = m // 8, m % 8
                    dve.wait_ge(lv_ready, m + 1)
                    lm = lmask[:, s - 1 if s else len(LEVELS), :].unsqueeze(1).to_broadcast([P, NCH, P])
                    dst = SM[:, n % 2, :].rearrange("p (c t) -> p c t", c=NCH)
                    src = mp[m % 2][:, :].rearrange("p (c t) -> p c t", c=NCH)
                    if s == 0:
                        if n >= 2:
                            dve.wait_ge(ho_ready, n - 1)
                        dve.tensor_tensor(dst, src, lm, ALU.mult).then_inc(lv_read, 1)
                    else:
                        dve.wait_ge(lv_read, m)
                        dve.copy_predicated(dst, lm.bitcast(U32), src).then_inc(lv_read, 1)

                def key_diff(n):
                    b = hb[:, n // 2 % 2, n % 2, 0:3 * P].rearrange("p (c t) -> p c t", c=3)
                    if n:
                        dve.wait_ge(kt_turned, n)
                    dve.tensor_tensor(Ke[:, :, :], b[:, :, P - 1:P].to_broadcast([P, 3, P]), b,
                                      ALU.subtract).then_inc(ke_diff, 1)

                def key_product(n):
                    dve.wait_ge(ke_exp, n + 1)
                    ke = Ke[:, :, :].rearrange("p c t -> p (c t)")
                    dve.tensor_tensor(ke, ke, hk[:, n // 2 % 2, n % 2, 0:3 * P], ALU.mult).then_inc(ke_ready, 1)

                def query_product(n):
                    dve.wait_ge(qe_exp, n + 1)
                    qe = Qe[:, :, :].rearrange("p c t -> p (c t)")
                    dve.tensor_tensor(qe, qe, hq[:, n // 2 % 2, n % 2, P:], ALU.mult).then_inc(qe_ready, 1)

                def recur(n):
                    dve.wait_ge(hst_ready, n + 1)
                    dve.wait_ge(qe_exp, n + 1)
                    if n:
                        dve.wait_ge(ho_ready, n)
                    step(dve.tensor_copy(St[:, 0, :], mp[2][:, 0:P]))
                    after()
                    step(dve.scalar_tensor_tensor(St[:, 1, :], St[:, 0, :], ebl[:, n % 2, 1:2], mp[2][:, P:2 * P],
                                                  ALU.mult, ALU.add))
                    after()
                    dve.scalar_tensor_tensor(St[:, 2, :], St[:, 1, :], ebl[:, n % 2, 2:3], mp[2][:, 2 * P:3 * P],
                                             ALU.mult, ALU.add).then_inc(hs_ready, 1)

                def head_value(n):
                    dve.wait_ge(hrstd_ready, n + 1)
                    v = value_slot(split0["hg"] + n)
                    dve.scalar_tensor_tensor(v, mp[3][:, :], prm[:, P_GN + n:P_GN + n + 1], rstd[:, :], ALU.mult,
                                             ALU.mult).then_inc(hscaled, 1)
                    dve.wait_ge(hscaled, n + 1)
                    tile_taken(dve, t0 + 8 * (n // 2) + 6 + n % 2)
                    dve.tensor_tensor(v, v, hg[:, n % 3, :], ALU.mult).then_inc(value_ready, 1)

                for p in range(HH // 2 + 1):
                    for k in range(16):
                        n, s = 2 * (p - 1) + k // 8, k % 8
                        if p:
                            m = 8 * n + s
                            level_diff(m + 2)
                            level_products(m + 1)
                            if s == 0:
                                key_diff(n)
                            elif s == 1:
                                key_product(n)
                            elif s == 3:
                                query_product(n)
                            elif s == 4 and n:
                                head_value(n - 1)
                            elif s == 5:
                                recur(n)
                            elif s == 6 and n:
                                low(split0["hg"] + n - 1, hoh[:, n - 1, :], hol[:, n - 1, :])
                            collect(m)
                        if p < HH // 2:
                            if k in (6, 8):
                                forget(p, (k - 6) // 2)
                            if k in (8, 10):
                                scan(p, (k - 8) // 2)
                    if p == 0:
                        level_diff(1)
                head_value(HH - 1)
                low(split0["hg"] + HH - 1, hoh[:, HH - 1, :], hol[:, HH - 1, :])
                add_to_x("hg_out", 5)

            mixers = (mamba, attention, conv_pool, lambda: ffn(0, 3), hgrn, lambda: ffn(1, 5))
            for v in range(PHASES):
                mixers[v]()
                pre_norm_of(v + 1)


INPUTS = ["x", "positions", "pre_norm", "post_norm", "ssm_w_in", "ssm_conv_w", "ssm_conv_b", "ssm_dt_bias",
          "ssm_a_log", "ssm_d", "ssm_gate_norm", "ssm_w_out", "att_w_in", "att_sinks", "att_w_out",
          "norm_mix_g_2", "norm_ffn_g_2", "final_g_2", "cp_w_in_2", "cp_dw_w_2", "cp_dw_b_2", "cp_ln_g_2",
          "cp_ln_b_2", "cp_pool_w_2", "cp_pool_scale_2", "cp_w_out_2", "hg_w_in_2", "hg_lb_logits_2",
          "hg_gn_g_2", "hg_w_out_2", "ffn_w1_2", "ffn_w3_2", "ffn_w2_2"]


def kernel(**inputs):
    import numpy as _np
    import concourse.bacc as _bacc
    from concourse import mybir as _mybir
    from concourse.bass_utils import run_bass_kernel_spmd as _run

    nc = _bacc.Bacc("TRN2", target_bir_lowering=False, num_devices=1)
    arrays, args = {}, []
    consts = dict(zip(("shape_const", "level_mask"), shape_constants()))
    for name in INPUTS + list(consts):
        a = _np.ascontiguousarray(consts[name] if name in consts else inputs[name])
        arrays[name] = a
        args.append(nc.dram_tensor(name, a.shape, _mybir.dt.from_np(a.dtype), kind="ExternalInput").ap())
    args.append(nc.dram_tensor("out", (1, L, D), _mybir.dt.float32, kind="ExternalOutput").ap())
    build(nc, *args)
    r = _run(nc, [arrays], core_ids=[0])
    return r.results[0]["out"]
```

```python
from contextlib import ExitStack

import concourse.bass as bass
import numpy as np
from concourse import mybir

ALU = mybir.AluOpType
ACT = mybir.ActivationFunctionType
AX = mybir.AxisListType
F32 = mybir.dt.float32
F32R = mybir.dt.float32r
I32 = mybir.dt.int32
U32 = mybir.dt.uint32

P = 128
L = 512
D = 1024
KT = D // P
NCH = L // P
EPS = 1e-6

SI = 2048
SH = 32
SG = 8
HPG = SH // SG
HD = 64
SB0, SC0, SDT0 = 2 * SI, 2 * SI + 1024, 2 * SI + 2048
TAPS = 4
KVH = 4
CW = 31
POOLW = (2, 4, 8, 16)
HH = 8
LEVELS = (64, 32, 16, 8, 4, 2, 1)
DFF = 2816
FT = DFF // P
UC = 256
NEG = -1.0e30
MAGIC = 1.5 * 2.0 ** 23
N_PAR = 19
DT_V = 3

C_ID, C_CAUSAL, C_BAND, C_ROT, C_RESET, C_RC, C_INV = 0, 128, 256, 512, 640, 1152, 1216
C_N = 1217
P_CONVW, P_DW = 0, 128
P_PRE, P_POST, P_CONVB, P_GATE, P_MIX, P_FFN, P_FINAL, P_GN = 256, 272, 288, 320, 336, 352, 368, 376
P_DWB, P_LNG, P_LNB, P_PSC, P_LB, P_SKIP = 384, 388, 392, 396, 400, 416


def shape_constants():
    i = np.arange(P)
    c = np.zeros((P, C_N), np.float32)
    c[:, C_ID:C_ID + P] = np.eye(P)
    c[:, C_CAUSAL:C_CAUSAL + P] = i[:, None] <= i[None, :]
    c[:, C_BAND:C_BAND + P] = np.where(i[None, :] > i[:, None], 0.0, NEG)
    c[:, C_BAND + P:C_BAND + 2 * P] = np.where(i[None, :] <= i[:, None], 0.0, NEG)
    for base in (0, 64):
        for d in range(8):
            c[base + d + 8, C_ROT + base + d] = -1.0
            c[base + d, C_ROT + base + d + 8] = 1.0
    c[:, C_RESET:C_RESET + L] = np.arange(L)[None, :] % P != 0
    for g, w in enumerate(POOLW):
        c[:, C_RC + 16 * g:C_RC + 16 * g + 16] = 1.0 / np.minimum(np.arange(16) + 1, w)
    inv = np.float32(500000.0) ** (-np.arange(0, 16, 2, dtype=np.float32) / np.float32(16))
    c[:, C_INV] = [inv[d % 64 % 8] if d % 64 < 16 else 0.0 for d in i]
    m = np.zeros((P, (len(LEVELS) + 1) * P), np.float32)
    for n, w in enumerate(LEVELS):
        s, t = i[:, None], i[None, :]
        m[:, n * P:(n + 1) * P] = (s // (2 * w) == t // (2 * w)) & (s % (2 * w) < w) & (t % (2 * w) >= w)
    m[:, len(LEVELS) * P:] = np.eye(P)
    return c, m


def conv_tile(g, j):
    return (2 * g, 2 * g + 1, 16 + g, 24 + g)[j]


PI_BELOW = 3.1415925


def two_pi_parts():
    left, out = 2 * np.pi, []
    for n in (5, 13, 21):
        out.append(float(np.floor(left * 2.0 ** n) / 2.0 ** n))
        left -= out[-1]
    return out + [float(np.float32(left))]


class Unit:

    def __init__(self, w, pieces, k0, kt, tiles, first, last):
        self.w, self.pieces, self.k0, self.kt = w, pieces, k0, kt
        self.tiles, self.first, self.last = tiles, first, last
        self.cols = max(c + n for c, _, n in pieces)


def plan(w):
    units, phases = [], {}
    state = {"tile": 0}

    def add(name, weight, columns, shares):
        u0, t0 = len(units), state["tile"]
        n = sum(x[2] for x in columns) // P
        tiles = list(range(t0, t0 + n))
        for j, (k0, kt) in enumerate(shares):
            units.append(Unit(weight, columns, k0, kt, tiles, j == 0, j == len(shares) - 1))
        state["tile"] += n
        lo, hi, a, b = phases.get(name, (u0, None, t0, None))
        phases[name] = (lo, len(units), a, state["tile"])

    whole = [(0, KT)]

    def out_proj(name, weight, early, late):
        add(name, weight, [(0, 0, D // 2)], early)
        for n in range(2, 4):
            add(name, weight, [(0, n * UC, UC)], late)

    def ffn(i):
        for n in range(DFF // UC):
            add(f"up{i}", w["w1"][i], [(0, n * UC, UC)], whole)
            add(f"up{i}", w["w3"][i], [(0, n * UC, UC)], whole)
        for n in range(D // UC):
            add(f"down{i}", w["w2"][i], [(0, n * UC, UC)], [(0, 8), (8, 8), (16, 6)])

    add("ssm", w["ssm_in"], [(0, SDT0, 32), (32, SDT0 - 96, 96)], whole)
    for g in range(SG):
        add("ssm", w["ssm_in"], [(0, SI + g * UC, UC)], whole)
        add("ssm", w["ssm_in"], [(0, SB0 + g * P, P), (P, SC0 + g * P, P)], whole)
        add("ssm", w["ssm_in"], [(0, g * UC, UC)], whole)
    out_proj("ssm_out", w["ssm_out"], [(0, 4), (4, 4), (8, 4), (12, 4)], [(0, 8), (8, 8)])
    for h in range(KVH):
        add("att", w["att_in"], [(0, h * UC, UC)], whole)
        add("att", w["att_in"], [(0, D + h * HD, HD), (HD, D + 256 + h * HD, HD)], whole)
        add("att", w["att_in"], [(0, D + 512 + h * UC, UC)], whole)
    out_proj("att_out", w["att_out"], [(0, 4), (4, 2), (6, 2)], whole)
    for n in range(2):
        add("cp", w["cp_in"], [(0, 512 + n * UC, UC)], whole)
        add("cp", w["cp_in"], [(0, n * UC, UC)], whole)
    for n in range(2):
        add("cp", w["cp_in"], [(0, 1024 + n * UC, UC)], whole)
    out_proj("cp_out", w["cp_out"], [(4, 4), (0, 4)], whole)
    ffn(0)
    for p in range(HH // 2):
        for j in range(4):
            add("hg", w["hg_in"], [(0, j * D + p * UC, UC)], whole)
    out_proj("hg_out", w["hg_out"], [(0, 4), (4, 2), (6, 2)], whole)
    ffn(1)
    return units, phases


def build(nc, x, positions, pre_norm, post_norm, ssm_w_in, ssm_conv_w, ssm_conv_b, ssm_dt_bias,
          ssm_a_log, ssm_d, ssm_gate_norm, ssm_w_out, att_w_in, att_sinks, att_w_out, norm_mix,
          norm_ffn, final_g, cp_w_in, cp_dw_w, cp_dw_b, cp_ln_g, cp_ln_b, cp_pool_w, cp_pool_scale,
          cp_w_out, hg_w_in, hg_lb_logits, hg_gn_g, hg_w_out, ffn_w1, ffn_w3, ffn_w2,
          shape_const, level_mask, out):
    units, phases = plan({
        "ssm_in": ssm_w_in[0], "ssm_out": ssm_w_out[0], "att_in": att_w_in[0], "att_out": att_w_out[0],
        "cp_in": cp_w_in[0], "cp_out": cp_w_out[0], "hg_in": hg_w_in[0], "hg_out": hg_w_out[0],
        "w1": [ffn_w1[0], ffn_w1[1]], "w3": [ffn_w3[0], ffn_w3[1]], "w2": [ffn_w2[0], ffn_w2[1]]})
    part_end, unit_end, parts = {}, [], 0
    for u in units:
        for t in u.tiles:
            parts += 1
            part_end[t] = parts
        unit_end.append(parts)

    def tiles_of(name):
        return range(phases[name][2], phases[name][3])

    ssm0 = phases["ssm"][2] + 1

    def end_of(name):
        return unit_end[phases[name][1] - 1]

    split0, n = {}, 0
    for name, count in (("pre0", KT), ("y", 16), ("pre1", KT), ("att", KT), ("pre2", KT), ("cp", KT),
                        ("pre3", KT), ("up0", FT), ("pre4", KT), ("hg", KT), ("pre5", KT), ("up1", FT), ("out", 0)):
        split0[name] = n
        n += count

    y_split = [range(0, 4), range(4, 8), range(8, 10), range(10, 12), range(12, 13), range(13, 14)]

    pre_round, post_round = [0, 2, 4, 5, 6, 7, 8], [1, 3]

    with ExitStack() as ctx:
        def sb(name, shape, dt=F32):
            return ctx.enter_context(nc.sbuf_tensor(name, shape, dt))

        def sem(name):
            return ctx.enter_context(nc.semaphore(name))

        cst = sb("cst", [P, C_N])
        ones = sb("ones", [P, P])
        prm = sb("prm", [P, 4 * P])
        eps_col = sb("eps_col", [P, 1])
        xT = sb("xT", [P, KT, L])
        hh_at = nc.sbuf_base() if callable(nc.sbuf_base) else nc.sbuf_base
        hh = sb("hh", [P, KT, L], F32R)
        hl = sb("hl", [P, KT, L], F32R)
        stage = sb("stage", [P, 2, KT * UC])
        wh = sb("wh", [P, 2, KT * UC], F32R)
        wl = sb("wl", [P, 2, KT * UC], F32R)
        sq = sb("sq", [P, 2, L])
        val = sb("val", [P, 2, L])
        root = sb("root", [P, L])
        rstd = sb("rstd", [P, L])
        sqsum = sb("sqsum", [P, L])
        arena_bytes = 92704
        arena = sb("arena", [P, arena_bytes // 4])
        a0 = nc.sbuf_base - arena_bytes if not callable(nc.sbuf_base) else nc.sbuf_base() - arena_bytes

        class Region:

            def __init__(self, at=0):
                self.at = at

            def take(self, name, shape, dt=F32):
                size = 4
                for d in shape[1:]:
                    size *= d
                t = nc.alloc_sbuf_tensor_at(name, shape, dt, offset=a0 + self.at)
                self.at += -(-size // 32) * 32
                assert self.at <= arena_bytes, (name, self.at)
                return t

        ident = cst[:, C_ID:C_ID + P]

        R = Region()
        xin = R.take("xin", [P, NCH, D])
        prow = R.take("prow", [P, 4, P])
        skip_raw = R.take("skip_raw", [16, 2])
        R = Region()
        y = R.take("m_y", [P, 16, L])
        after_y = R.at
        raw = R.take("m_raw", [P, 2, TAPS - 1 + L])
        xs = R.take("m_xs", [P, 2, 4, L])
        sz = R.take("m_sz", [P, 2, L])
        xdt = R.take("m_xdt", [P, NCH, HPG * HD])
        xde = R.take("m_xde", [P, NCH - 1, HPG * HD])
        Bt = R.take("m_Bt", [P, NCH - 1, P])
        cbm = R.take("m_cbm", [P, NCH, P])
        G = R.take("m_G", [P, HPG, L])
        EC = R.take("m_EC", [P, HPG, L])
        Hs = R.take("m_Hs", [P, NCH - 1, HPG * HD])
        cd = R.take("m_cd", [P, HPG, NCH])
        tokT = R.take("m_tokT", [P, 3, NCH, SH])
        acs_hl = R.take("m_acs_hl", [2 * SH, L], F32R)
        pick = R.take("m_pick", [2 * SH, SH], F32R)
        R = Region(after_y - 12 * 2048)
        dtmp = [R.take(f"m_dt{i}", [SH, L]) for i in range(10)]
        acs = R.take("m_acs", [SH, L])
        hcol = R.take("m_hcol", [SH, 4])
        yl = nc.alloc_sbuf_tensor_at("m_yl", [P, 16, L], F32R, offset=a0)
        R = Region(after_y)
        yo_m = R.take("m_yo", [P, KT, L])
        rg = R.take("m_rg", [P, L])

        R = Region()
        oh = R.take("a_oh", [P, KT, L], F32R)
        ol = R.take("a_ol", [P, KT, L], F32R)
        yo_a = nc.alloc_sbuf_tensor_at("a_yo", [P, KT, L], F32, offset=a0 + R.at)
        cosT = R.take("a_cos", [P, L])
        sinT = R.take("a_sin", [P, L])
        qraw = R.take("a_qraw", [P, 2, L])
        kvraw = R.take("a_kvraw", [P, L])
        qr = R.take("a_qr", [P, 2, 2, L])
        kd = R.take("a_kd", [P, 2, 2, L])
        vt = R.take("a_vt", [P, 2, NCH, HD])
        rtmp = R.take("a_rtmp", [P, 2, L])
        pp = R.take("a_pp", [P, 2, 2, UC])
        pT = R.take("a_pT", [P, 2, 2, 2, P])
        sgate = R.take("a_sgate", [P, 2, 2, L])
        srow = R.take("a_srow", [P, 2, 12])
        sinks = R.take("a_sinks", [P, 16])
        posi = nc.alloc_sbuf_tensor_at("a_posi", [P, L], I32, offset=a0)
        R = Region(2048)
        trig = [R.take(f"a_trig{i}", [P, L]) for i in range(3)]
        R = Region()
        ch = R.take("c_h", [P, KT, L], F32R)
        cl = R.take("c_l", [P, KT, L], F32R)
        apad = R.take("c_a", [P, 4, CW - 1 + L])
        acc = R.take("c_acc", [P, 4, L])
        sig = R.take("c_sig", [P, 2, L])
        ub = R.take("c_u", [P, 4, 16 + L])
        ws = R.take("c_ws", [P, 2, 16 + L])
        dp = R.take("c_dp", [P, 2, L])
        poolw = R.take("c_pw", [P, 4, P])
        lrstd = R.take("c_lrstd", [P, L])
        taps = R.take("c_taps", [P, CW, P])
        R = Region()
        gh = R.take("f_h", [P, FT, L], F32R)
        gl = R.take("f_l", [P, FT, L], F32R)
        rows_out = nc.alloc_sbuf_tensor_at("rows_out", [P, NCH, D], F32, offset=hh_at)
        R = Region()
        hoh = R.take("h_oh", [P, KT, L], F32R)
        hol = R.take("h_ol", [P, KT, L], F32R)
        hq = R.take("h_q", [P, 2, 2, L])
        hk = R.take("h_k", [P, 2, 2, L])
        hb = R.take("h_b", [P, 2, 2, L])
        hvt = R.take("h_vt", [P, 2, 2, L])
        hg = R.take("h_g", [P, 3, L])
        XL = R.take("h_x", [P, 3, L])
        SM = R.take("h_sm", [P, 2, L])
        Ke = R.take("h_ke", [P, NCH - 1, P])
        Kt = R.take("h_kt", [P, NCH - 1, P])
        Qe = R.take("h_qe", [P, NCH - 1, P])
        St = R.take("h_st", [P, NCH - 1, P])
        lmask = R.take("h_mask", [P, len(LEVELS) + 1, P])
        lbc = R.take("h_lb", [P, 3, 8])
        ebl = R.take("h_ebl", [P, 2, NCH])

        gp = [ctx.enter_context(nc.psum_tensor(f"gp{i}", [P, L], F32)) for i in range(4)]
        mp = [ctx.enter_context(nc.psum_tensor(f"mp{i}", [P, L], F32)) for i in range(4)]

        landed = [sem(f"weights_landed{i}") for i in range(2)]
        hi_done = sem("weights_hi_done")
        weights_split = sem("weights_split")
        gemm_part = sem("gemm_part")
        bank_read = [sem(f"bank_read{i}") for i in range(4)]
        value_ready, hi_ready, split_done = sem("value_ready"), sem("hi_ready"), sem("split_done")
        sq_ready, sq_added, sum_ready, rstd_ready = (sem(s) for s in ("sq_ready", "sq_added", "sum_ready", "rstd_ready"))
        silu_ready = sem("silu_ready")
        x_tile = sem("x_tile")
        dve_step, act_step = sem("dve_step"), sem("act_step")
        in_landed, par_landed, prm_turned, x_turned = (sem(s) for s in (
            "in_landed", "par_landed", "prm_turned", "x_turned"))
        prm_ready, dt_read, tap_ready, zsilu_ready = (sem(s) for s in (
            "prm_ready", "dt_read", "tap_ready", "zsilu_ready"))
        skip_ready = sem("skip_ready")
        const_set, const_landed = sem("const_set"), sem("const_landed")
        dt_a, dt_v, dt_turned, tok_ready = (sem(s) for s in ("dt_act", "dt_vec", "dt_turned", "tok_ready"))
        conv_done, silu_done = sem("conv_done"), sem("silu_done")
        xt_ready, xt_read, bt_ready, bt_read, cb_ready, cb_read = (sem(s) for s in (
            "xt_ready", "xt_read", "bt_ready", "bt_read", "cb_ready", "cb_read"))
        bc_ready, e_ready, seg_ready, dec_ready, gc_ready = (sem(s) for s in (
            "bc_ready", "e_ready", "seg_ready", "dec_ready", "gc_ready"))
        st_ready, h_ready, y_ready, y_read, yg_ready, gsq_ready = (sem(s) for s in (
            "st_ready", "h_ready", "y_ready", "y_read", "yg_ready", "gsq_ready"))
        gate_sq, gate_sum, gate_rstd = (sem(s) for s in ("gate_sq", "gate_sum", "gate_rstd"))
        posi_landed, trig_ready, sin_done = sem("posi_landed"), sem("trig_ready"), sem("sin_done")
        rot_read = sem("rot_read")
        rot_ready, v_turned, qk_ready = sem("rot_ready"), sem("v_turned"), sem("qk_ready")
        s_ready, s_read, m_ready, p_ready, pn_ready, pt_turned, pt_copied, pv_done = (sem(s) for s in (
            "s_ready", "s_read", "m_ready", "p_ready", "pn_ready", "pt_turned", "pt_copied", "pv_done"))
        taps_ready, gated_ready, last_conv, last_ready, pool_step = (sem(s) for s in (
            "taps_ready", "gated_ready", "last_conv", "last_ready", "pool_step"))
        poolw_landed, conv_ready, mean_ready, centred, lsq_ready, var_ready = (sem(s) for s in (
            "poolw_landed", "conv_ready", "mean_ready", "centred", "lsq_ready", "var_ready"))
        lrstd_ready, ln_ready, window_ready, pool_ready = (sem(s) for s in (
            "lrstd_ready", "ln_ready", "window_ready", "pool_ready"))
        mask_landed, lb_diff, lb_exp, f_lin, f_ready, ln_f, hb_ready = (sem(s) for s in (
            "mask_landed", "lb_diff", "lb_exp", "f_lin", "f_ready", "ln_f", "hb_ready"))
        vt_turned, vt_ready, diff_ready, dexp_ready, x_ready, lv_ready, lv_read = (sem(s) for s in (
            "vt_turned", "vt_ready", "diff_ready", "dexp_ready", "x_ready", "lv_ready", "lv_read"))
        ke_diff, ke_exp, ke_ready, kt_turned, kt_ready, hst_ready, hs_ready = (sem(s) for s in (
            "ke_diff", "ke_exp", "ke_ready", "kt_turned", "kt_ready", "hst_ready", "hs_ready"))
        qe_exp, qe_ready = sem("qe_exp"), sem("qe_ready")
        ho_ready, hsq_ready, hsum_ready, hrstd_ready, hscaled = (sem(s) for s in (
            "ho_ready", "hsq_ready", "hsum_ready", "hrstd_ready", "hscaled"))
        out_turned, out_copied, out_landed = sem("out_turned"), sem("out_copied"), sem("out_landed")
        even_ready, odd_ready = sem("even_rows_ready"), sem("odd_rows_ready")
        fsig_ready, hgate_ready = sem("fsig_ready"), sem("hgate_ready")
        sig_ready = sem("sig_ready")

        def tile_whole(eng, t):
            eng.wait_ge(gemm_part, part_end[t])

        def tile_taken(eng, t):
            eng.wait_ge(bank_read[t % 4], t // 4 + 1)

        def out_tile(name, k):
            return phases[name][2] + k

        in_names = ["ssm", "att", "cp", "up0", "hg", "up1"]
        out_names = ["ssm_out", "att_out", "cp_out", "down0", "hg_out", "down1"]

        def h_free(eng, v):
            eng.wait_ge(gemm_part, end_of(out_names[0] if v == 1 else in_names[v - 1]))

        def x_wait(eng, v, k):
            if v <= 2:
                eng.wait_ge(x_tile, KT * v + k + 1)
            else:
                tile_taken(eng, out_tile(out_names[v - 1], k))

        norm_cols = (P_PRE, P_PRE + KT, P_MIX, P_FFN, P_MIX + KT, P_FFN + KT, P_FINAL)

        block = ctx.enter_context(nc.Block())

        def load_parameters(eng, half):
            def load(dst, src):
                eng.dma_start(dst, src).then_inc(par_landed, 16)

            def rows(s, r0, n, src):
                load(prow[r0:r0 + n, s, :], src)

            if half == 0:
                load(cst[:, C_ID + P:], shape_const[:, C_ID + P:])
                rows(2, 0, 16, pre_norm.rearrange("l (t p) -> (l t) p", p=P))
                rows(2, 16, 16, post_norm.rearrange("l (t p) -> (l t) p", p=P))
                rows(2, 32, 32, ssm_conv_b.rearrange("l (t p) -> (l t) p", p=P))
                rows(2, 64, 16, ssm_gate_norm.rearrange("l (t p) -> (l t) p", p=P))
                rows(2, 80, 16, norm_mix.rearrange("l (t p) -> (l t) p", p=P))
                rows(2, 96, 16, norm_ffn.rearrange("l (t p) -> (l t) p", p=P))
                rows(2, 112, 8, final_g.rearrange("(t p) -> t p", p=P))
                rows(2, 120, 8, hg_gn_g.rearrange("l (t p) -> (l t) p", p=P))
            else:
                rows(0, 0, P, ssm_conv_w.rearrange("o k (t p) -> (o k t) p", p=P))
                rows(1, 0, CW * 4, cp_dw_w.rearrange("o k (t p) -> (o k t) p", p=P))
                rows(3, 0, 4, cp_dw_b.rearrange("l (t p) -> (l t) p", p=P))
                rows(3, 4, 4, cp_ln_g.rearrange("l (t p) -> (l t) p", p=P))
                rows(3, 8, 4, cp_ln_b.rearrange("l (t p) -> (l t) p", p=P))
                rows(3, 12, 4, cp_pool_scale.rearrange("l (t p) -> (l t) p", p=P))
                rows(3, 16, 16, hg_lb_logits.rearrange("l (t p) -> (l t) p", p=P))
                load(skip_raw[:, :], ssm_d.rearrange("o (t j) -> (o t) j", j=2))
                load(hcol[:, 0:1], ssm_dt_bias.rearrange("o h -> h o"))
                load(hcol[:, 1:2], ssm_a_log.rearrange("o h -> h o"))

        @block.sync
        def _(sp):
            for c in range(NCH):
                sp.dma_start(xin[:, c, :], x[0, c * P:(c + 1) * P, :]).then_inc(in_landed, 16)
            load_parameters(sp, 1)
            for u in range(len(units)):
                un = units[u]
                if u >= 2:
                    sp.wait_ge(weights_split, 2 * (u - 1))
                dst = stage[:, u % 2, 0:un.kt * un.cols].rearrange("p (k n) -> p k n", k=un.kt)
                for c, n0, w in un.pieces:
                    src = un.w[un.k0 * P:(un.k0 + un.kt) * P, n0:n0 + w].rearrange("(k p) n -> p k n", p=P)
                    sp.dma_start(dst[:, :, c:c + w], src).then_inc(landed[u % 2], 16)
            for c in range(NCH):
                sp.wait_ge(odd_ready if c % 2 else even_ready, c // 2 + 1)
                sp.dma_start(out[0, c * P:(c + 1) * P, :], rows_out[:, c, :]).then_inc(out_landed, 16)
            sp.wait_ge(out_landed, 16 * NCH)

        def add_square(eng, r, k):
            if k:
                eng.wait_ge(sq_ready, KT * r + k + 1)
                n = (KT - 1) * r + k - 1
                if k > 1:
                    eng.wait_ge(sq_added, n)
                eng.tensor_tensor(sqsum[:, :], sqsum[:, :], sq[:, k % 2, :], ALU.add).then_inc(sq_added, 1)

        def window_out(g):
            return dp[:, g, :] if g < 2 else sig[:, g - 2, :]

        def window_means(pool):
            steps = 0
            for g in range(4):
                tile_taken(pool, tiles_of("cp")[0] + 8 + g)
                src, w = ub[:, g, :], 1
                while w < POOLW[g]:
                    dst = ws[:, 0 if w in (1, 4) else 1, :]
                    pool.tensor_tensor(dst[:, 2 * w - 1:], src[:, 2 * w - 1:], src[:, w - 1:16 + L - w],
                                       ALU.add).then_inc(pool_step, 1)
                    steps += 1
                    pool.wait_ge(pool_step, steps)
                    src, w = dst, 2 * w
                d = window_out(g)
                pool.tensor_scalar(d, src[:, 16:], 1.0 / w, 1.0, ALU.mult, ALU.mult).then_inc(pool_step, 1)
                pool.wait_ge(pool_step, steps + 1)
                pool.tensor_tensor(d[:, 0:16], src[:, 16:32], cst[:, C_RC + 16 * g:C_RC + 16 * g + 16],
                                   ALU.mult).then_inc(pool_step, 1)
                steps += 2
                pool.wait_ge(pool_step, steps)
                pool.tensor_tensor(d, d, ub[:, g, 16:], ALU.subtract).then_inc(window_ready, 1)

        @block.gpsimd
        def _(pool):
            count = [0, 0]
            for u in range(len(units)):
                un, s = units[u], u % 2
                n = un.kt * un.cols
                count[s] += 16 * len(un.pieces)
                pool.wait_ge(landed[s], count[s])
                if u >= 2:
                    pool.wait_ge(gemm_part, unit_end[u - 2])
                half = un.kt // 2 * un.cols
                for i, part in enumerate((slice(0, half), slice(half, n))):
                    pool.tensor_scalar(wh[:, s, part], stage[:, s, part], 1.0, 1.0, ALU.mult,
                                       ALU.mult).then_inc(hi_done, 1)
                    pool.wait_ge(hi_done, 2 * u + i + 1)
                    pool.tensor_tensor(wl[:, s, part], stage[:, s, part], wh[:, s, part].bitcast(F32),
                                       ALU.subtract).then_inc(weights_split, 1)
                for v, name in ((1, "att"), (2, "cp")):
                    if u == phases[name][0] + 1:
                        for k in range(1, KT):
                            add_square(pool, pre_round[v], k)
                if u == phases["cp_out"][0] + 1:
                    window_means(pool)

        @block.tensor
        def _(pe):
            def granules(name, hi, lo, split, lead=0, after_first=None):
                u0, u1, t0, _ = phases[name]
                for k in range(KT if lead else 0):
                    pe.wait_ge(split_done, split(k) + 1)
                    for u in range(u0, u0 + lead):
                        s = u % 2
                        wvh = wh[:, s, 0:KT * units[u].cols].rearrange("p (k n) -> p k n", k=KT)
                        wvl = wl[:, s, 0:KT * units[u].cols].rearrange("p (k n) -> p k n", k=KT)
                        if k in (0, KT // 2):
                            pe.wait_ge(weights_split, 2 * u + 1 + k // (KT // 2))
                        for m, t in enumerate(units[u].tiles):
                            if k == 0 and t >= 4:
                                pe.wait_ge(bank_read[t % 4], t // 4)
                            cols = slice(m * P, (m + 1) * P)
                            bank = gp[t % 4]
                            pe.matmul(bank[:, :], wvh[:, k, cols], hi(k), start=(k == 0), stop=False)
                            pe.matmul(bank[:, :], wvl[:, k, cols], hi(k), start=False, stop=False)
                            mm = pe.matmul(bank[:, :], wvh[:, k, cols], lo(k), start=False, stop=(k == KT - 1))
                            if k == KT - 1:
                                mm.then_inc(gemm_part, 1)
                            if k == KT - lead and t == t0 and after_first:
                                after_first()
                            if k >= KT - 2:
                                yield
                for u in range(u0 + lead, u1):
                    un, s = units[u], u % 2
                    wvh = wh[:, s, 0:un.kt * un.cols].rearrange("p (k n) -> p k n", k=un.kt)
                    wvl = wl[:, s, 0:un.kt * un.cols].rearrange("p (k n) -> p k n", k=un.kt)
                    for m, t in enumerate(un.tiles):
                        bank = gp[t % 4]
                        if m == 0:
                            pe.wait_ge(weights_split, 2 * u + 1)
                        if un.first and t >= 4:
                            pe.wait_ge(bank_read[t % 4], t // 4)
                        for k in range(un.kt):
                            if k == un.kt // 2:
                                yield
                                if m == 0:
                                    pe.wait_ge(weights_split, 2 * u + 2)
                            kk = un.k0 + k
                            if t == t0:
                                pe.wait_ge(split_done, split(kk) + 1)
                            cols = slice(m * P, (m + 1) * P)
                            start = un.first and k == 0
                            stop = un.last and k == un.kt - 1
                            pe.matmul(bank[:, :], wvh[:, k, cols], hi(kk), start=start, stop=False)
                            pe.matmul(bank[:, :], wvl[:, k, cols], hi(kk), start=False, stop=False)
                            mm = pe.matmul(bank[:, :], wvh[:, k, cols], lo(kk), start=False, stop=stop)
                        mm.then_inc(gemm_part, 1)
                        yield

            def h_granules(name, norm, lead=0, after_first=None):
                return granules(name, lambda k: hh[:, k, :], lambda k: hl[:, k, :], lambda k: split0[norm] + k,
                                lead, after_first)

            def run(gran, n=None):
                if n is None:
                    for _ in gran:
                        pass
                else:
                    for _ in range(n):
                        next(gran, None)

            def sum_squares(r):
                pe.wait_ge(sq_added, (KT - 1) * (r + 1))
                pe.matmul(mp[3][:, :], ones[:, :], sqsum[:, :], start=True, stop=True).then_inc(sum_ready, 1)

            pe.wait_ge(const_landed, 16)
            pe.wait_ge(in_landed, 16 * NCH)
            for k in range(KT):
                if k == 4:
                    pe.wait_ge(par_landed, 16 * N_PAR)
                    pe.wait_ge(skip_ready, 1)
                    for s, rows in enumerate((P, CW * 4, P, 48)):
                        mm = pe.transpose(mp[0][:, s * P:s * P + rows], prow[0:rows, s, :], ident[0:rows, 0:rows])
                    mm.then_inc(prm_turned, 1)
                if k >= 2:
                    pe.wait_ge(x_tile, k - 1)
                for c in range(NCH):
                    mm = pe.transpose(mp[1 + k % 2][:, c * P:(c + 1) * P], xin[:, c, k * P:(k + 1) * P], ident)
                mm.then_inc(x_turned, 1)

            def mamba():
                gran = h_granules("ssm", "pre0", 2, lambda: sum_squares(pre_round[0]))
                run(gran, 6)

                def turn_dt():
                    pe.wait_ge(dt_v, DT_V)
                    for i, src in enumerate((acs, dtmp[6], dtmp[8])):
                        for c in range(NCH):
                            mm = pe.transpose(mp[2][:, (i * NCH + c) * SH:(i * NCH + c + 1) * SH],
                                              src[:, c * P:(c + 1) * P], ident[0:SH, 0:SH])
                    mm.then_inc(dt_turned, 1)

                def turn_and_cb(g):
                    xg = xs[:, g % 2]
                    for t in range(2):
                        pe.wait_ge(silu_done, 4 * g + t + 1)
                        if g:
                            pe.wait_ge(y_read, 2 * g)
                        for c in range(NCH):
                            mm = pe.transpose(mp[t][:, c * P:(c + 1) * P], xg[:, t, c * P:(c + 1) * P], ident)
                        mm.then_inc(xt_ready, 1)
                    pe.wait_ge(silu_done, 4 * g + 4)
                    if g:
                        pe.wait_ge(h_ready, g)
                    pe.wait_ge(tok_ready, 1)
                    for c in range(NCH - 1):
                        mm = pe.transpose(mp[2][:, c * P:(c + 1) * P], xg[:, 2, c * P:(c + 1) * P], ident)
                    mm.then_inc(bt_ready, 1)
                    for c in range(NCH):
                        s = slice(c * P, (c + 1) * P)
                        mm = pe.matmul(mp[3][:, s], xg[:, 2, s], xg[:, 3, s], start=True, stop=True)
                    mm.then_inc(cb_ready, 1)

                def spread(g, h):
                    if h < 2:
                        pe.wait_ge(xt_read, 2 * g + h + 1)
                    else:
                        pe.wait_ge(e_ready, 4 * g + h - 1)
                        pe.wait_ge(seg_ready, 4 * g + h - 1)
                    hd = HPG * g + h
                    pe.matmul(mp[h % 2][:, :], pick[:, hd:hd + 1].to_broadcast([2 * SH, P]), acs_hl[:, :],
                              start=True, stop=True).then_inc(bc_ready, 1)

                def states(g):
                    pe.wait_ge(bt_read, g + 1)
                    pe.wait_ge(cb_read, g + 1)
                    pe.wait_ge(xt_read, 2 * g + 2)
                    for c in range(NCH - 1):
                        dst = mp[2][:, c * 256:(c + 1) * 256] if c < 2 else mp[3][:, 0:256]
                        mm = pe.matmul(dst, Bt[:, c, :], xde[:, c, :], start=True, stop=True)
                    mm.then_inc(st_ready, 1)

                def y_tile(g, t):
                    pe.wait_ge(e_ready, 4 * g + 3 + t)
                    pe.wait_ge(seg_ready, 4 * g + 3 + t)
                    pe.wait_ge(gc_ready, 4 * g + 2 * t + 2)
                    pe.wait_ge(h_ready, g + 1)
                    for j in range(2):
                        h = 2 * t + j
                        hs = slice(h * HD, (h + 1) * HD)
                        for c in range(NCH):
                            s = slice(c * P, (c + 1) * P)
                            dst = mp[t][j * HD:(j + 1) * HD, s]
                            mm = pe.matmul(dst, xdt[:, c, hs], G[:, h, s], start=True, stop=(c == 0))
                            if c:
                                mm = pe.matmul(dst, Hs[:, c - 1, hs], EC[:, h, s], start=False, stop=True)
                    mm.then_inc(y_ready, 1)

                gran_out = granules("ssm_out", lambda k: (hh if k < KT else hl)[:, k % KT, :],
                                    lambda k: yl[:, k, :], lambda k: split0["y"] + k)
                for g in range(SG + 1):
                    def mix(slot):
                        if g == 0:
                            if slot == 5:
                                turn_dt()
                            return
                        p = g - 1
                        if slot == 0:
                            turn_and_cb(p)
                        elif slot == 1:
                            spread(p, 0)
                            spread(p, 1)
                        elif slot == 2:
                            spread(p, 2)
                            spread(p, 3)
                            states(p)
                        elif slot == 4:
                            y_tile(p, 0)
                        elif slot == 5:
                            y_tile(p, 1)

                    for slot in range(6):
                        if g < SG and (g or slot > 1):
                            run(gran, 2)
                        mix(slot)
                        if g == SG:
                            run(gran_out, (2, 4, 4, 4, 4, 4)[slot])
                pe.wait_ge(gate_sq, 1)
                pe.matmul(mp[3][:, :], ones[:, :], sqsum[:, :], start=True, stop=True).then_inc(gate_sum, 1)
                run(gran_out)
                pe.wait_ge(gate_rstd, 1)
                sum_squares(post_round[0])

            def attention():
                gran = h_granules("att", "pre1", 2, lambda: sum_squares(pre_round[1]))

                def rotate(h, tiles):
                    for j in tiles:
                        tile_taken(pe, tiles_of("att")[0] + 5 * h + j)
                        if j < 2 and h:
                            pe.wait_ge(s_read, 8 * h)
                        elif j == 2:
                            pe.wait_ge(rot_read, h + 1)
                        src = qraw[:, j, :] if j < 2 else kvraw[:, :]
                        pe.matmul(mp[j % 2][:, :], cst[:, C_ROT:C_ROT + P], src, start=True,
                                  stop=True).then_inc(rot_ready, 1)
                    if 2 not in tiles:
                        return
                    if h:
                        pe.wait_ge(pt_copied, 8 * h)
                    for c in range(NCH):
                        mm = pe.transpose(mp[2][:, c * P:(c + 1) * P], kvraw[:, c * P:(c + 1) * P], ident)
                    mm.then_inc(v_turned, 1)

                def scores(h, i):
                    t, n = i // 4, i % 4
                    pe.wait_ge(qk_ready, h + 1)
                    if i >= 2:
                        pe.wait_ge(s_read, 8 * h + i - 1)
                    for j in range(2):
                        k0 = max(n - 1, 0) * P
                        w = (n + 1) * P - k0
                        mm = pe.matmul(mp[i % 2][:, (j + 1) * UC - w:(j + 1) * UC],
                                       qr[:, h % 2, t, n * P:(n + 1) * P], kd[:, h % 2, j, k0:k0 + w],
                                       start=True, stop=True)
                    mm.then_inc(s_ready, 1)

                def turn_p(h, i):
                    pe.wait_ge(pn_ready, 8 * h + i + 1)
                    if h or i:
                        pe.wait_ge(pt_copied, 8 * h + i)
                    for j in range(2):
                        for half in range(2):
                            if i % 4 or half:
                                mm = pe.transpose(mp[2][:, (2 * j + half) * P:(2 * j + half + 1) * P],
                                                  pp[:, i % 2, j, half * P:(half + 1) * P], ident)
                    mm.then_inc(pt_turned, 1)

                def pv(h, i):
                    t, n = i // 4, i % 4
                    pe.wait_ge(pt_copied, 8 * h + i + 1)
                    if i in (0, 4) and 2 * h + i // 4:
                        pe.wait_ge(value_ready, split0["att"] + 2 * h + i // 4)
                    for j in range(2):
                        for half in range(0 if n else 1, 2):
                            mm = pe.matmul(mp[3][j * HD:(j + 1) * HD, n * P:(n + 1) * P],
                                           vt[:, h % 2, n - 1 + half, :], pT[:, i % 2, j, half, :],
                                           start=(half == 0 or n == 0), stop=(half == 1))
                    mm.then_inc(pv_done, 1)

                gran_out = granules("att_out", lambda k: oh[:, k, :], lambda k: ol[:, k, :],
                                    lambda k: split0["att"] + k)
                for h in range(KVH + 1):
                    for k in range(11):
                        if h < KVH:
                            run(gran, (2, 1, 1, 1, 1, 1, 1, 1, 0, 1, 0)[k])
                        else:
                            run(gran_out, (2, 1, 1, 1, 1, 2, 2, 2, 2, 2, 0)[k])
                        if h:
                            if 0 <= k - 2 < 8:
                                turn_p(h - 1, k - 2)
                            if 0 <= k - 3 < 8:
                                pv(h - 1, k - 3)
                            if k < 8:
                                scores(h - 1, k)
                        if h < KVH and k == 9:
                            rotate(h, (0, 1))
                    if h < KVH:
                        rotate(h, (2,))
                run(gran_out)
                sum_squares(post_round[1])

            def conv_pool():
                run(h_granules("cp", "pre2", 2, lambda: sum_squares(pre_round[2])))
                pe.wait_ge(gated_ready, 4)
                for i in range(CW):
                    pe.wait_ge(taps_ready, i + 1)
                    mm = pe.matmul(mp[1][:, :], taps[:, i, :], apad[:, 3, i:i + L], start=(i == 0), stop=(i == CW - 1))
                mm.then_inc(last_conv, 1)
                pe.wait_ge(poolw_landed, 16)
                for g in range(4):
                    pe.wait_ge(window_ready, g + 1)
                    if g >= 2:
                        pe.wait_ge(hi_ready, split0["cp"] + g - 1)
                    pe.matmul(mp[2 + g % 2][:, :], poolw[:, g, :], window_out(g), start=True,
                              stop=True).then_inc(pool_ready, 1)
                for t in range(4):
                    if t < 3:
                        pe.wait_ge(conv_ready, t + 1)
                    else:
                        pe.wait_ge(last_ready, 1)
                    mm = pe.matmul(mp[0][:, :], ones[:, :], acc[:, t, :], start=(t == 0), stop=(t == 3))
                mm.then_inc(mean_ready, 1)
                gran = granules("cp_out", lambda k: ch[:, k, :], lambda k: cl[:, k, :],
                                lambda k: split0["cp"] + (k + 4) % KT)
                run(gran, 3)
                for t in range(4):
                    pe.wait_ge(lsq_ready, t + 1)
                    pe.matmul(mp[1][:, :], ones[:, :], sq[:, t % 2, :], start=(t == 0),
                              stop=(t == 3)).then_inc(var_ready, 1)
                run(gran)

            def ffn(i, v, turn=None):
                run(h_granules(f"up{i}", f"pre{v}", 1, lambda: sum_squares(pre_round[v])))
                gran = granules(f"down{i}", lambda k: gh[:, k, :], lambda k: gl[:, k, :],
                                lambda k: split0[f"up{i}"] + k)
                if turn:
                    for k in range(0, KT, 2):
                        run(gran, 16 if k == 0 else 12 if k < KT - 2 else None)
                        turn(k)
                        turn(k + 1)
                run(gran)

            def hgrn():
                gran = h_granules("hg", "pre4", 1, lambda: sum_squares(pre_round[4]))

                def level(n, s):
                    m = 8 * n + s
                    b, j = n // 2 % 2, n % 2
                    if m >= 2:
                        pe.wait_ge(lv_read, m - 1)
                    if s:
                        pe.wait_ge(x_ready, 7 * n + s)
                    else:
                        pe.wait_ge(hb_ready, n + 1)
                        tile_taken(pe, tiles_of("hg")[0] + 8 * (n // 2) + j)
                    x = XL[:, (7 * n + s - 1) % 3, :]
                    for c in range(NCH):
                        cs = slice(c * P, (c + 1) * P)
                        mm = pe.matmul(mp[m % 2][:, cs], x[:, cs] if s else hk[:, b, j, cs],
                                       x[:, cs] if s else hq[:, b, j, cs], start=True, stop=True)
                    mm.then_inc(lv_ready, 1)

                def turn_k(n):
                    pe.wait_ge(ke_ready, n + 1)
                    pe.wait_ge(vt_ready, 2 * (n // 2 + 1))
                    if n:
                        pe.wait_ge(hs_ready, n)
                    for c in range(NCH - 1):
                        mm = pe.transpose(mp[2][:, c * P:(c + 1) * P], Ke[:, c, :], ident)
                    mm.then_inc(kt_turned, 1)

                def states(n):
                    b, j = n // 2 % 2, n % 2
                    pe.wait_ge(kt_ready, n + 1)
                    if n:
                        pe.wait_ge(hrstd_ready, n)
                    for c in range(NCH - 1):
                        cs = slice(c * P, (c + 1) * P)
                        mm = pe.matmul(mp[2][:, cs], Kt[:, c, :], hvt[:, b, j, cs], start=True, stop=True)
                    mm.then_inc(hst_ready, 1)

                def turn_v(p, j):
                    tile_taken(pe, tiles_of("hg")[0] + 8 * p + 4 + j)
                    if j:
                        pe.wait_ge(vt_ready, 2 * p + 1)
                    elif p:
                        pe.wait_ge(hs_ready, 2 * p)
                    for c in range(NCH):
                        mm = pe.transpose(mp[2][:, c * P:(c + 1) * P], hvt[:, p % 2, j, c * P:(c + 1) * P], ident)
                    mm.then_inc(vt_turned, 1)

                def output(n):
                    b, j = n // 2 % 2, n % 2
                    pe.wait_ge(lv_read, 8 * n + 8)
                    pe.wait_ge(hs_ready, n + 1)
                    pe.wait_ge(qe_ready, n + 1)
                    if n:
                        pe.wait_ge(hscaled, n)
                    for c in range(NCH):
                        cs = slice(c * P, (c + 1) * P)
                        mm = pe.matmul(mp[3][:, cs], hvt[:, b, j, cs], SM[:, n % 2, cs], start=True, stop=(c == 0))
                        if c:
                            mm = pe.matmul(mp[3][:, cs], St[:, c - 1, :], Qe[:, c - 1, :], start=False, stop=True)
                    mm.then_inc(ho_ready, 1)

                def head_sum(n):
                    pe.wait_ge(hsq_ready, n + 1)
                    if n + 1 < HH:
                        pe.wait_ge(kt_ready, n + 2)
                    pe.matmul(mp[2][:, :], ones[:, :], sq[:, n % 2, :], start=True, stop=True).then_inc(hsum_ready, 1)

                gran_out = granules("hg_out", lambda k: hoh[:, k, :], lambda k: hol[:, k, :],
                                    lambda k: split0["hg"] + k)
                for p in range(HH // 2 + 1):
                    for k in range(16):
                        n, s = 2 * (p - 1) + k // 8, k % 8
                        run(gran if p < HH // 2 else gran_out, 1)
                        if p:
                            level(n, s)
                            if s == 1 and n:
                                output(n - 1)
                            elif s == 2:
                                turn_k(n)
                            elif s == 3 and n:
                                head_sum(n - 1)
                            elif s == 5:
                                states(n)
                        if p < HH // 2 and k >= 14:
                            turn_v(p, k - 14)
                output(HH - 1)
                head_sum(HH - 1)
                run(gran_out)

            def turn_out(k):
                pe.wait_ge(value_ready, split0["out"] + k + 1)
                if k >= 2:
                    pe.wait_ge(out_copied, k - 1)
                for c in range(NCH):
                    mm = pe.transpose(mp[k % 2][:, c * P:(c + 1) * P], val[:, k % 2, c * P:(c + 1) * P], ident)
                mm.then_inc(out_turned, 1)

            mamba()
            attention()
            conv_pool()
            ffn(0, 3)
            hgrn()
            ffn(1, 5, turn_out)
            pe.wait_ge(sq_added, (KT - 1) * (pre_round[6] + 1))
            for c in range(NCH):
                mm = pe.matmul(mp[3][:, c:c + 1], sqsum[:, c * P:(c + 1) * P], ones[:, 0:1], start=True, stop=True)
            mm.then_inc(sum_ready, 1)

        @block.scalar
        def _(act):
            steps = [0]

            def step(ins):
                ins.then_inc(act_step, 1)
                steps[0] += 1
                return steps[0]

            def after(n=None):
                act.wait_ge(act_step, steps[0] if n is None else n)

            def high(n, dst):
                act.wait_ge(value_ready, n + 1)
                act.activation(dst, val[:, n % 2, :], ACT.Copy).then_inc(hi_ready, 1)

            def square(r, k, src):
                if k:
                    n = (KT - 1) * r + k - 2
                    if n > 0:
                        act.wait_ge(sq_added, n)
                    dst = sq[:, k % 2, :]
                else:
                    if r:
                        act.wait_ge(sum_ready, r)
                    dst = sqsum[:, :]
                act.activation(dst, src[:, k, :], ACT.Square).then_inc(sq_ready, 1)

            def load_ln():
                act.preload_act_table_set("natural_log")

            def inverse_root(bank, n, dst):
                step(act.activation(root[:, :], bank[:, :], ACT.Ln, bias=eps_col[:, 0:1], scale=1.0 / n))
                after()
                return act.activation(dst, root[:, :], ACT.Exp, scale=-0.5)

            def take_rstd(r):
                load_ln()
                act.wait_ge(sum_ready, r + 1)
                inverse_root(mp[3], D, rstd[:, :]).then_inc(rstd_ready, 1)

            def post_norm_of(i, yo):
                for k in range(KT):
                    tile_taken(act, out_tile(out_names[i], k))
                    square(post_round[i], k, yo)
                take_rstd(post_round[i])

            def value_of_x(v, k):
                n = split0[f"pre{v}"] + k
                w = prm[:, norm_cols[v] + k:norm_cols[v] + k + 1]
                x_wait(act, v, k)
                if n >= 2:
                    act.wait_ge(split_done, n - 1)
                act.activation(val[:, n % 2, :], xT[:, k, :], ACT.Copy, scale=w).then_inc(value_ready, 1)
                act.activation(hh[:, k, :], xT[:, k, :], ACT.Copy, scale=w).then_inc(hi_ready, 1)

            def pre_norm_of(v):
                r = pre_round[v]
                for k in range(KT):
                    if k == 0 and v:
                        h_free(act, v)
                    if v <= 2:
                        value_of_x(v, k)
                    else:
                        high(split0[f"pre{v}"] + k, hh[:, k, :])
                    x_wait(act, v, k)
                    square(r, k, xT)
                take_rstd(r)

            act.dma_start(ident, shape_const[:, C_ID:C_ID + P]).then_inc(const_landed, 16)
            load_parameters(act, 0)

            act.preload_act_table_set("natural_log")
            act.wait_ge(const_set, 1)
            act.wait_ge(prm_ready, 1)
            pre_norm_of(0)

            def mamba():
                u, ab, e, w, lw = dtmp[0:5]
                act.activation(hcol[:, 2:3], hcol[:, 1:2], ACT.Exp).then_inc(dt_a, 1)
                tile_taken(act, 0)
                act.activation(u[:, :], u[:, :], ACT.Identity, bias=hcol[:, 0:1]).then_inc(dt_read, 1)
                act.wait_ge(dt_read, 1)
                step(act.activation(ab[:, :], u[:, :], ACT.Abs))
                after()
                act.activation(e[:, :], ab[:, :], ACT.Exp, scale=-1.0).then_inc(dt_a, 1)
                act.wait_ge(dt_v, 1)
                act.activation(lw[:, :], w[:, :], ACT.Ln).then_inc(dt_a, 1)
                act.wait_ge(dt_v, DT_V - 1)
                act.activation(dtmp[7][:, :], dtmp[7][:, :], ACT.Exp).then_inc(dt_a, 1)

                def last_tap(g, j):
                    t = ssm0 + 6 * g + j
                    n = 4 * g + j
                    col = P_CONVW + 3 * 32 + conv_tile(g, j)
                    tile_taken(act, t)
                    if g >= 2:
                        act.wait_ge(y_read, 2 * (g - 1))
                    act.activation(xs[:, g % 2, j, :], raw[:, n % 2, TAPS - 1:], ACT.Copy,
                                   scale=prm[:, col:col + 1]).then_inc(tap_ready, 1)

                def silu(g, j):
                    col = P_CONVB + conv_tile(g, j)
                    act.wait_ge(conv_done, 4 * g + j + 1)
                    v = xs[:, g % 2, j, :]
                    act.activation(v, v, ACT.Silu, bias=prm[:, col:col + 1]).then_inc(silu_done, 1)

                def silu_z(g, j):
                    tile_taken(act, ssm0 + 6 * g + 4 + j)
                    act.activation(sz[:, j, :], sz[:, j, :], ACT.Silu).then_inc(zsilu_ready, 1)

                def copy_B(g):
                    act.wait_ge(bt_ready, g + 1)
                    act.activation(Bt[:, :, :].rearrange("p c n -> p (c n)"), mp[2][:, 0:3 * P],
                                   ACT.Copy).then_inc(bt_read, 1)

                def decay_to_start(g, h):
                    act.wait_ge(bc_ready, 4 * g + h + 1)
                    if h == 0 and g:
                        act.wait_ge(y_ready, 2 * g)
                    act.activation(EC[:, h, :], mp[h % 2][:, :], ACT.Exp).then_inc(e_ready, 1)

                def decay_between(g, h):
                    act.wait_ge(seg_ready, 4 * g + h + 1)
                    act.activation(G[:, h, :], G[:, h, :], ACT.Exp).then_inc(dec_ready, 1)

                def gate_square(g, t):
                    n = 2 * g + t
                    act.wait_ge(yg_ready, n + 1)
                    act.activation(sq[:, t, :], val[:, t, :], ACT.Square).then_inc(gsq_ready, 1)

                def high_y(k):
                    if k == 0:
                        act.wait_ge(gemm_part, end_of("ssm"))
                    act.wait_ge(value_ready, split0["y"] + k + 1)
                    act.activation((hh if k < KT else hl)[:, k % KT, :], y[:, k, :], ACT.Copy).then_inc(hi_ready, 1)

                for g in range(SG + 1):
                    p = g - 1
                    for slot in range(6):
                        if g == SG:
                            for k in y_split[slot]:
                                high_y(k)
                        pair = (2 * slot - 2, 2 * slot - 1)
                        if g > 0 and slot in (1, 2):
                            for h in pair:
                                decay_to_start(p, h)
                        if g < SG:
                            if slot < 4:
                                last_tap(g, slot)
                            if slot == 5:
                                silu(g, 3)
                        if g > 0:
                            if slot == 0:
                                copy_B(p)
                            elif slot in (1, 2):
                                for h in pair:
                                    decay_between(p, h)
                            elif slot == 4:
                                gate_square(p, 0)
                            elif slot == 5:
                                gate_square(p, 1)
                        if g < SG:
                            if slot >= 4:
                                silu_z(g, slot - 4)
                            if 2 <= slot < 4:
                                silu(g, slot - 2)
                            if slot == 4:
                                silu(g, 2)
                for k in range(14, 16):
                    high_y(k)
                load_ln()
                act.wait_ge(gate_sum, 1)
                inverse_root(mp[3], SI, rg[:, :]).then_inc(gate_rstd, 1)
                post_norm_of(0, yo_m)

            def attention():
                act.dma_start(posi[:, :], positions[0:1, :].to_broadcast([P, L])).then_inc(posi_landed, 16)
                act.dma_start(sinks[:, :], att_sinks[0:1, :].to_broadcast([P, 16])).then_inc(posi_landed, 16)

                def gate(h, j):
                    tile_taken(act, tiles_of("att")[0] + 5 * h + 3 + j)
                    v = sgate[:, h % 2, j, :]
                    act.activation(v, v, ACT.Silu).then_inc(silu_ready, 1)

                def exps(h, i):
                    act.wait_ge(m_ready, 8 * h + i + 1)
                    b = i % 2
                    k0 = 0 if i % 4 else P
                    for j in range(2):
                        v = pp[:, b, j, k0:]
                        act.activation(v, v, ACT.Exp, bias=srow[:, b, 2 + j:3 + j], scale=0.125,
                                       accum_out=srow[:, b, 6 + j:7 + j])
                    act.activation(srow[:, b, 8:10], srow[:, b, 4:6], ACT.Exp).then_inc(p_ready, 1)

                def copy_p(h, i):
                    act.wait_ge(pt_turned, 8 * h + i + 1)
                    if i >= 2 or h:
                        act.wait_ge(pv_done, 8 * h + i - 1)
                    k0 = 0 if i % 4 else 1
                    act.activation(pT[:, i % 2, :, k0:, :],
                                   mp[2][:, :].rearrange("p (j k i) -> p j k i", j=2, k=2)[:, :, k0:, :],
                                   ACT.Copy).then_inc(pt_copied, 1)

                act.wait_ge(trig_ready, 1)
                act.activation(sinT[:, :], sinT[:, :], ACT.Sin)
                act.activation(cosT[:, :], cosT[:, :], ACT.Sin).then_inc(sin_done, 1)
                for h in range(KVH + 1):
                    for k in range(12):
                        if h:
                            if 0 <= k - 2 < 8:
                                copy_p(h - 1, k - 2)
                            if k in (7, 11):
                                n = 2 * (h - 1) + (k == 11)
                                high(split0["att"] + n, oh[:, n, :])
                            if k < 8:
                                exps(h - 1, k)
                        if h < KVH and k in (7, 9):
                            gate(h, (k - 7) // 2)
                post_norm_of(1, yo_a)

            def conv_pool():
                act.dma_start(poolw[:, :, :], cp_pool_w[0].rearrange("g c d -> c g d")).then_inc(poolw_landed, 16)
                t0 = tiles_of("cp")[0]
                for i in range(CW):
                    col = P_DW + 4 * i + 3
                    act.activation(taps[:, i, :], ident, ACT.Copy, scale=prm[:, col:col + 1]).then_inc(taps_ready, 1)
                for half in range(2):
                    for j in range(2):
                        t = t0 + 4 * half + j
                        tile_taken(act, t)
                        act.activation(sig[:, j, :], sig[:, j, :], ACT.Sigmoid).then_inc(sig_ready, 1)
                n0 = split0["cp"]
                act.wait_ge(last_conv, 1)
                act.activation(acc[:, 3, :], mp[1][:, :], ACT.Identity,
                               bias=prm[:, P_DWB + 3:P_DWB + 4]).then_inc(last_ready, 1)
                for g in range(4):
                    act.wait_ge(pool_ready, g + 1)
                    act.activation(ub[:, g, 16:], mp[2 + g % 2][:, :], ACT.Copy,
                                   scale=prm[:, P_PSC + g:P_PSC + g + 1]).then_inc(value_ready, 1)
                    act.wait_ge(value_ready, n0 + g + 1)
                    act.activation(ch[:, 4 + g, :], ub[:, g, 16:], ACT.Copy).then_inc(hi_ready, 1)
                for t in range(4):
                    act.wait_ge(centred, t + 1)
                    if t >= 2:
                        act.wait_ge(var_ready, t - 1)
                    act.activation(sq[:, t % 2, :], acc[:, t, :], ACT.Square).then_inc(lsq_ready, 1)
                load_ln()
                act.wait_ge(var_ready, 4)
                inverse_root(mp[1], 4 * P, lrstd[:, :]).then_inc(lrstd_ready, 1)
                for t in range(4):
                    act.wait_ge(ln_ready, t + 1)
                    act.activation(acc[:, t, :], acc[:, t, :], ACT.Silu,
                                   bias=prm[:, P_LNB + t:P_LNB + t + 1]).then_inc(value_ready, 1)
                    act.wait_ge(value_ready, n0 + 4 + t + 1)
                    act.activation(ch[:, t, :], acc[:, t, :], ACT.Copy).then_inc(hi_ready, 1)

            def ffn(i, v):
                t0, n0 = tiles_of(f"up{i}")[0], split0[f"up{i}"]
                for n in range(FT // 2):
                    for j in range(2):
                        tile_taken(act, t0 + 4 * n + j)
                        act.activation(sq[:, j, :], sq[:, j, :], ACT.Silu).then_inc(silu_ready, 1)
                    for j in range(2):
                        high(n0 + 2 * n + j, gh[:, 2 * n + j, :])

            def hgrn():
                act.dma_start(lmask[:, :, :].rearrange("p l t -> p (l t)"), level_mask).then_inc(mask_landed, 16)
                act.wait_ge(lb_diff, 1)
                act.activation(lbc[:, 0:2, :], lbc[:, 0:2, :], ACT.Exp).then_inc(lb_exp, 1)
                t0 = tiles_of("hg")[0]

                def take(p, j):
                    if j in (2, 3):
                        v, f, done = hb[:, p % 2, j - 2, :], ACT.Sigmoid, fsig_ready
                    elif j >= 6:
                        v, f, done = hg[:, (2 * p + j - 6) % 3, :], ACT.Silu, hgate_ready
                    else:
                        return
                    tile_taken(act, t0 + 8 * p + j)
                    act.activation(v, v, f).then_inc(done, 1)

                def log_f(p, j):
                    act.wait_ge(f_ready, 2 * p + j + 1)
                    v = hb[:, p % 2, j, :]
                    act.activation(v, v, ACT.Ln).then_inc(ln_f, 1)

                def level_exp(m):
                    n, s = m // 8, m % 8
                    if s and n < HH:
                        x = XL[:, (7 * n + s - 1) % 3, :]
                        act.wait_ge(diff_ready, 7 * n + s)
                        act.activation(x, x, ACT.Exp, scale=-1.0).then_inc(dexp_ready, 1)

                def key_exp(n):
                    act.wait_ge(ke_diff, n + 1)
                    ke = Ke[:, :, :].rearrange("p c t -> p (c t)")
                    act.activation(ke, ke, ACT.Exp).then_inc(ke_exp, 1)

                def query_exp(n):
                    b, j = n // 2 % 2, n % 2
                    if n:
                        act.wait_ge(ho_ready, n)
                    act.activation(ebl[:, n % 2, :], hb[:, b, j, P - 1::P], ACT.Exp)
                    act.activation(Qe[:, :, :].rearrange("p c t -> p (c t)"), hb[:, b, j, P:],
                                   ACT.Exp).then_inc(qe_exp, 1)

                def copy_kt(n):
                    act.wait_ge(kt_turned, n + 1)
                    act.activation(Kt[:, :, :].rearrange("p c t -> p (c t)"), mp[2][:, 0:3 * P],
                                   ACT.Copy).then_inc(kt_ready, 1)

                def copy_vt(p, j):
                    act.wait_ge(vt_turned, 2 * p + j + 1)
                    if p >= 2:
                        act.wait_ge(ho_ready, 2 * (p - 1))
                    act.activation(hvt[:, p % 2, j, :], mp[2][:, :], ACT.Copy).then_inc(vt_ready, 1)

                def head_square(n):
                    act.wait_ge(ho_ready, n + 1)
                    if n >= 2:
                        act.wait_ge(hsum_ready, n - 1)
                    act.activation(sq[:, n % 2, :], mp[3][:, :], ACT.Square).then_inc(hsq_ready, 1)

                def head_root(n):
                    act.wait_ge(hsum_ready, n + 1)
                    if n:
                        act.wait_ge(hscaled, n)
                    inverse_root(mp[2], P, root[:, :]).then_inc(hrstd_ready, 1)

                def head_high(n):
                    high(split0["hg"] + n, hoh[:, n, :])

                for p in range(HH // 2 + 1):
                    for k in range(16):
                        n, s = 2 * (p - 1) + k // 8, k % 8
                        if p:
                            level_exp(8 * n + s + 2)
                            if s == 0:
                                key_exp(n)
                            elif s == 1 and n:
                                head_square(n - 1)
                            elif s == 2:
                                copy_kt(n)
                                query_exp(n)
                            elif s == 3 and n:
                                head_root(n - 1)
                            elif s == 5 and n:
                                head_high(n - 1)
                        if p < HH // 2:
                            if k % 2:
                                take(p, k // 2)
                            if k in (7, 9):
                                log_f(p, (k - 7) // 2)
                            if k >= 14:
                                copy_vt(p, k - 14)
                    if p == 0:
                        level_exp(1)
                head_square(HH - 1)
                head_root(HH - 1)
                head_high(HH - 1)

            def last_norm():
                r = pre_round[6]
                for k in range(KT):
                    x_wait(act, 6, k)
                    square(r, k, xT)
                    act.wait_ge(out_turned, k + 1)
                    act.activation(rows_out[:, :, k * P:(k + 1) * P],
                                   mp[k % 2][:, :].rearrange("p (c d) -> p c d", c=NCH), ACT.Copy).then_inc(out_copied, 1)
                load_ln()
                act.wait_ge(sum_ready, r + 1)
                step(act.activation(root[:, 0:NCH], mp[3][:, 0:NCH], ACT.Ln, bias=eps_col[:, 0:1], scale=1.0 / D))
                after()
                act.activation(rstd[:, 0:NCH], root[:, 0:NCH], ACT.Exp, scale=-0.5).then_inc(rstd_ready, 1)
                act.wait_ge(rstd_ready, r + 1)
                for c in (1, 3):
                    act.activation(rows_out[:, c, :], rows_out[:, c, :], ACT.Copy,
                                   scale=rstd[:, c:c + 1]).then_inc(odd_ready, 1)

            mamba()
            pre_norm_of(1)
            attention()
            pre_norm_of(2)
            conv_pool()
            pre_norm_of(3)
            ffn(0, 3)
            pre_norm_of(4)
            hgrn()
            pre_norm_of(5)
            ffn(1, 5)
            last_norm()

        @block.vector
        def _(dve):
            steps = [0]

            def step(ins):
                ins.then_inc(dve_step, 1)
                steps[0] += 1
                return steps[0]

            def after(n=None):
                dve.wait_ge(dve_step, steps[0] if n is None else n)

            def value_slot(n):
                if n >= 2:
                    dve.wait_ge(split_done, n - 1)
                return val[:, n % 2, :]

            def low(n, hi, lo):
                dve.wait_ge(hi_ready, n + 1)
                dve.tensor_tensor(lo, val[:, n % 2, :], hi.bitcast(F32), ALU.subtract).then_inc(split_done, 1)

            def value_of_x(v, k):
                x_wait(dve, v, k)
                col = norm_cols[v] + k
                dve.tensor_scalar(value_slot(split0[f"pre{v}"] + k), xT[:, k, :], prm[:, col:col + 1], None,
                                  ALU.mult).then_inc(value_ready, 1)

            def low_of_x(v, k):
                if k == 0 and v:
                    h_free(dve, v)
                low(split0[f"pre{v}"] + k, hh[:, k, :], hl[:, k, :])
                if v not in (1, 2):
                    add_square(dve, pre_round[v], k)

            def post_norm_of(i, yo):
                v = i + 1
                dve.wait_ge(rstd_ready, post_round[i] + 1)
                n = [0] * KT
                for k in range(KT + 2):
                    if 0 < k <= KT:
                        after(n[k - 1])
                        dve.tensor_tensor(xT[:, k - 1, :], xT[:, k - 1, :], yo[:, k - 1, :],
                                          ALU.add).then_inc(x_tile, 1)
                    if k < KT:
                        col = P_POST + KT * i + k
                        n[k] = step(dve.scalar_tensor_tensor(yo[:, k, :], yo[:, k, :], prm[:, col:col + 1],
                                                             rstd[:, :], ALU.mult, ALU.mult))
                    if k > 1:
                        low_of_x(v, k - 2)

            dve.memset(ones[:, :], 1.0)
            dve.memset(eps_col[:, :], EPS).then_inc(const_set, 1)
            def take_x(k):
                dve.wait_ge(x_turned, k + 1)
                dve.tensor_copy(xT[:, k, :], mp[1 + k % 2][:, :]).then_inc(x_tile, 1)

            for k in range(4):
                take_x(k)
            dve.wait_ge(par_landed, 16 * N_PAR)
            dve.tensor_copy(prow[32:48, 3, :].rearrange("t (j d) -> t j d", j=2),
                            skip_raw[:, :].unsqueeze(2).to_broadcast([16, 2, HD])).then_inc(skip_ready, 1)
            dve.wait_ge(prm_turned, 1)
            step(dve.tensor_copy(prm[:, 0:252], mp[0][:, 0:252]))
            dve.tensor_copy(prm[:, 256:432], mp[0][:, 256:432]).then_inc(prm_ready, 1)
            dve.wait_ge(prm_ready, 1)
            for k in range(KT):
                if k < 4:
                    take_x(4 + k)
                low_of_x(0, k)
            dve.wait_ge(rstd_ready, pre_round[0] + 1)

            def mamba():
                u, e, w, lw, a, dt, dx, co = (dtmp[0], dtmp[2], dtmp[3], dtmp[4], dtmp[5], dtmp[6],
                                              dtmp[8], dtmp[9])
                df = dtmp[7]
                step(dve.memset(raw[:, :, 0:TAPS - 1], 0.0))
                step(dve.memset(sqsum[:, :], 0.0))

                def take(g, j):
                    t, n = ssm0 + 6 * g + j, 4 * g + j
                    tile_whole(dve, t)
                    if j >= 4:
                        if g:
                            dve.wait_ge(yg_ready, 2 * g - 5 + j)
                        dst = sz[:, j - 4, :]
                    else:
                        if n >= 2:
                            dve.wait_ge(conv_done, n - 1)
                        dst = raw[:, n % 2, TAPS - 1:]
                    dve.tensor_tensor(dst, gp[t % 4][:, :], rstd[:, :], ALU.mult).then_inc(bank_read[t % 4], 1)

                tile_whole(dve, 0)
                dve.tensor_tensor(u[:, :], gp[0][0:SH, :], rstd[0:SH, :], ALU.mult).then_inc(bank_read[0], 1)
                take(0, 0)
                take(0, 1)
                dve.wait_ge(dt_a, 2)
                step(dve.tensor_scalar(hcol[:, 3:4], hcol[:, 2:3], -1.0, None, ALU.mult))
                dve.tensor_scalar(w[:, :], e[:, :], 1.0, None, ALU.add).then_inc(dt_v, 1)
                dve.wait_ge(dt_v, 1)
                step(dve.tensor_scalar(co[:, :], w[:, :], -1.0, None, ALU.add))
                step(dve.reciprocal(dx[:, :], w[:, :]))
                after()
                step(dve.tensor_tensor(co[:, :], e[:, :], co[:, :], ALU.subtract))
                after()
                step(dve.tensor_tensor(co[:, :], co[:, :], dx[:, :], ALU.mult))
                dve.wait_ge(dt_a, 3)
                after()
                step(dve.tensor_tensor(co[:, :], co[:, :], lw[:, :], ALU.add))
                after()
                step(dve.scalar_tensor_tensor(dt[:, :], u[:, :], 0.0, co[:, :], ALU.max, ALU.add))
                after()
                step(dve.tensor_scalar(a[:, :], dt[:, :], hcol[:, 3:4], None, ALU.mult))
                after()
                step(dve.tensor_tensor_scan(acs[:, :], cst[0:SH, C_RESET:C_RESET + L], a[:, :], 0.0,
                                            ALU.mult, ALU.add))
                after()
                for part in range(2):
                    step(dve.tensor_copy(pick[part * SH:(part + 1) * SH, :], ident[0:SH, 0:SH]))
                step(dve.tensor_copy(acs_hl[0:SH, :], acs[:, :]))
                after()
                step(dve.tensor_tensor(acs_hl[SH:2 * SH, :], acs[:, :], acs_hl[0:SH, :].bitcast(F32), ALU.subtract))
                acs3 = acs[:, :].rearrange("h (c l) -> h c l", c=NCH)
                dve.tensor_tensor(df[:, :].rearrange("h (c l) -> h c l", c=NCH),
                                  acs3[:, :, P - 1:P].to_broadcast([SH, NCH, P]), acs3,
                                  ALU.subtract).then_inc(dt_v, 1)
                dve.wait_ge(dt_a, 4)
                dve.tensor_tensor(dx[:, :], df[:, :], dt[:, :], ALU.mult).then_inc(dt_v, 1)

                def conv(g, j):
                    n = 4 * g + j
                    dve.wait_ge(tap_ready, n + 1)
                    v = xs[:, g % 2, j, :]
                    for i in range(TAPS - 2, -1, -1):
                        col = P_CONVW + i * 32 + conv_tile(g, j)
                        ins = dve.scalar_tensor_tensor(v, raw[:, n % 2, i:i + L], prm[:, col:col + 1], v,
                                                       ALU.mult, ALU.add)
                        if i:
                            step(ins)
                            after()
                        else:
                            ins.then_inc(conv_done, 1)

                def scale_x(g, t):
                    dve.wait_ge(xt_ready, 2 * g + t + 1)
                    if t == 0 and g:
                        dve.wait_ge(y_ready, 2 * g)
                    src = mp[t][:, :].rearrange("p (c h d) -> p c h d", c=NCH, h=2)
                    for dst, i, n in ((xdt, 1, NCH), (xde, 2, NCH - 1)):
                        o = dst[:, :, t * P:(t + 1) * P].rearrange("p c (h d) -> p c h d", h=2)
                        f = tokT[:, i, 0:n, HPG * g + 2 * t:HPG * g + 2 * t + 2].unsqueeze(3).to_broadcast([P, n, 2, HD])
                        ins = dve.tensor_tensor(o, src[:, 0:n], f, ALU.mult)
                        if i == 1:
                            step(ins)
                    ins.then_inc(xt_read, 1)

                def mask_cb(g):
                    dve.wait_ge(cb_ready, g + 1)
                    m = cst[:, C_CAUSAL:C_CAUSAL + P].unsqueeze(1).to_broadcast([P, NCH, P])
                    dve.tensor_tensor(cbm[:, :, :], mp[3][:, :].rearrange("p (c l) -> p c l", c=NCH), m,
                                      ALU.mult).then_inc(cb_read, 1)

                def segment(g, h):
                    dve.wait_ge(e_ready, 4 * g + h + 1)
                    step(dve.tensor_copy(cd[:, h, :], EC[:, h, P - 1::P]))
                    for c in range(NCH):
                        s = slice(c * P, (c + 1) * P)
                        f = tokT[:, 0, c, HPG * g + h:HPG * g + h + 1]
                        ins = dve.tensor_scalar(G[:, h, s], mp[h % 2][:, s], f, f, ALU.min, ALU.subtract)
                        if c < NCH - 1:
                            step(ins)
                    ins.then_inc(seg_ready, 1)

                def products(g, h):
                    dve.wait_ge(dec_ready, 4 * g + h + 1)
                    dve.wait_ge(cb_read, g + 1)
                    step(dve.tensor_tensor(G[:, h, :], G[:, h, :], cbm[:, :, :].rearrange("p c l -> p (c l)"), ALU.mult))
                    after()
                    dve.tensor_tensor(EC[:, h, :], EC[:, h, :], xs[:, g % 2, 3, :], ALU.mult).then_inc(gc_ready, 1)

                def recur(g):
                    dve.wait_ge(st_ready, g + 1)
                    step(dve.tensor_copy(Hs[:, 0, :], mp[2][:, 0:256]))
                    for c in (1, 2):
                        after()
                        f = cd[:, :, c].unsqueeze(2).to_broadcast([P, HPG, HD])
                        step(dve.tensor_tensor(Hs[:, c, :].rearrange("p (h d) -> p h d", h=HPG),
                                               Hs[:, c - 1, :].rearrange("p (h d) -> p h d", h=HPG), f, ALU.mult))
                        after()
                        ins = dve.tensor_tensor(Hs[:, c, :], Hs[:, c, :],
                                                mp[2][:, 256:512] if c == 1 else mp[3][:, 0:256], ALU.add)
                        if c == 1:
                            step(ins)
                    ins.then_inc(h_ready, 1)

                def gate_y(g, t):
                    n = 2 * g + t
                    col = P_SKIP + n
                    dve.wait_ge(y_ready, n + 1)
                    dve.wait_ge(zsilu_ready, n + 1)
                    if n >= 2:
                        dve.wait_ge(gsq_ready, n - 1)
                    v = val[:, t, :]
                    dve.scalar_tensor_tensor(v, xs[:, g % 2, t, :], prm[:, col:col + 1], mp[t][:, :],
                                             ALU.mult, ALU.add).then_inc(y_read, 1)
                    dve.wait_ge(y_read, n + 1)
                    dve.tensor_tensor(v, v, sz[:, t, :], ALU.mult).then_inc(yg_ready, 1)
                    dve.wait_ge(yg_ready, n + 1)
                    dve.tensor_scalar(y[:, n, :], v, prm[:, P_GATE + n:P_GATE + n + 1], None,
                                      ALU.mult).then_inc(value_ready, 1)
                    dve.wait_ge(gsq_ready, n + 1)
                    ins = dve.tensor_tensor(sqsum[:, :], sqsum[:, :], sq[:, t, :], ALU.add)
                    if n < 15:
                        step(ins)
                        after()
                    else:
                        ins.then_inc(gate_sq, 1)

                def low_y(k):
                    dve.wait_ge(hi_ready, split0["y"] + k + 1)
                    dve.tensor_tensor(yl[:, k, :], y[:, k, :], (hh if k < KT else hl)[:, k % KT, :].bitcast(F32),
                                      ALU.subtract).then_inc(split_done, 1)

                for g in range(SG + 1):
                    p = g - 1
                    for slot in range(6):
                        if g < SG and slot < 4 and (g or slot > 1):
                            take(g, slot)
                        if g > 0:
                            if slot == 0:
                                scale_x(p, 0)
                                scale_x(p, 1)
                                mask_cb(p)
                            elif slot == 1:
                                segment(p, 0)
                                segment(p, 1)
                                products(p, 0)
                                products(p, 1)
                            elif slot == 2:
                                segment(p, 2)
                                segment(p, 3)
                                recur(p)
                                products(p, 2)
                                products(p, 3)
                            elif slot == 4:
                                gate_y(p, 0)
                            elif slot == 5:
                                gate_y(p, 1)
                        if g < SG and slot >= 4:
                            take(g, slot)
                        if g < SG and 1 <= slot <= 4:
                            conv(g, slot - 1)
                        if g == 0 and slot == 5:
                            dve.wait_ge(dt_turned, 1)
                            dve.tensor_copy(tokT[:, :, :, :].rearrange("p i c h -> p (i c h)"),
                                            mp[2][:, 0:3 * NCH * SH]).then_inc(tok_ready, 1)
                            dve.wait_ge(tok_ready, 1)
                        if g == SG:
                            for k in y_split[slot]:
                                low_y(k)
                for k in range(14, 16):
                    low_y(k)
                dve.wait_ge(gate_rstd, 1)
                for k in range(KT):
                    t = out_tile("ssm_out", k)
                    tile_whole(dve, t)
                    dve.tensor_tensor(yo_m[:, k, :], gp[t % 4][:, :], rg[:, :], ALU.mult).then_inc(bank_read[t % 4], 1)
                    if k:
                        add_square(dve, post_round[0], k - 1)
                add_square(dve, post_round[0], KT - 1)
                post_norm_of(0, yo_m)

            def attention():
                parts = two_pi_parts()
                posf, t0, t1 = trig[0], trig[1], trig[2]
                for b in range(2):
                    step(dve.memset(kd[HD:, b, 0, :], 0.0))
                    step(dve.memset(kd[0:HD, b, 1, :], 0.0))
                def tables():
                    dve.wait_ge(posi_landed, 32)
                    step(dve.tensor_copy(posf[:, :], posi[:, :]))
                    after()
                    step(dve.tensor_scalar(posf[:, :], posf[:, :], cst[:, C_INV:C_INV + 1], None, ALU.mult))
                    after()
                    for dst, shift in ((sinT, 0.0), (cosT, 0.25)):
                        step(dve.tensor_scalar(t0[:, :], posf[:, :], 0.15915494309189535, shift, ALU.mult, ALU.add))
                        after()
                        step(dve.tensor_scalar(t0[:, :], t0[:, :], MAGIC, None, ALU.add))
                        after()
                        step(dve.tensor_scalar(t0[:, :], t0[:, :], -MAGIC, None, ALU.add))
                        after()
                        src = posf
                        for c in parts:
                            step(dve.scalar_tensor_tensor(t1[:, :], t0[:, :], -c, src[:, :], ALU.mult, ALU.add))
                            after()
                            src = t1
                        if shift:
                            step(dve.tensor_scalar(t1[:, :], t1[:, :], float(np.pi / 2), None, ALU.add))
                            after()
                        ins = dve.tensor_scalar(dst[:, :], t1[:, :], PI_BELOW, -PI_BELOW, ALU.min, ALU.max)
                        if shift:
                            ins.then_inc(trig_ready, 1)
                        else:
                            step(ins)

                def mask_scores(h, i):
                    dve.wait_ge(s_ready, 8 * h + i + 1)
                    if i >= 2 or h:
                        dve.wait_ge(pt_turned, 8 * h + i - 1)
                    b, k0 = i % 2, (0 if i % 4 else P)
                    v = pp[:, b, :, k0:]
                    src = mp[i % 2][:, :].rearrange("p (j k) -> p j k", j=2)[:, :, k0:]
                    band = cst[:, C_BAND + k0:C_BAND + UC].unsqueeze(1).to_broadcast([P, 2, UC - k0])
                    dve.tensor_tensor(v, src, band, ALU.add).then_inc(s_read, 1)
                    dve.wait_ge(s_read, 8 * h + i + 1)
                    step(dve.tensor_reduce(srow[:, b, 0:2], v, AX.X, ALU.max))
                    after()
                    sk = sinks[:, HPG * h + 2 * (i // 4):HPG * h + 2 * (i // 4) + 2]
                    step(dve.scalar_tensor_tensor(srow[:, b, 0:2], srow[:, b, 0:2], 0.125, sk, ALU.mult, ALU.max))
                    after()
                    step(dve.tensor_scalar(srow[:, b, 2:4], srow[:, b, 0:2], -1.0, None, ALU.mult))
                    dve.tensor_tensor(srow[:, b, 4:6], sk, srow[:, b, 0:2], ALU.subtract).then_inc(m_ready, 1)

                def normalise(h, i):
                    dve.wait_ge(p_ready, 8 * h + i + 1)
                    b, k0 = i % 2, (0 if i % 4 else P)
                    step(dve.tensor_tensor(srow[:, b, 6:8], srow[:, b, 6:8], srow[:, b, 8:10], ALU.add))
                    after()
                    step(dve.reciprocal(srow[:, b, 10:12], srow[:, b, 6:8]))
                    after()
                    step(dve.tensor_scalar(pp[:, b, 0, k0:], pp[:, b, 0, k0:], srow[:, b, 10:11], None, ALU.mult))
                    dve.tensor_scalar(pp[:, b, 1, k0:], pp[:, b, 1, k0:], srow[:, b, 11:12], None,
                                      ALU.mult).then_inc(pn_ready, 1)

                def gate_o(h, t):
                    n = split0["att"] + 2 * h + t
                    dve.wait_ge(pv_done, 8 * h + 4 * t + 4)
                    dve.wait_ge(silu_ready, 2 * h + t + 1)
                    dve.tensor_tensor(value_slot(n), mp[3][:, :], sgate[:, h % 2, t, :],
                                      ALU.mult).then_inc(value_ready, 1)

                def take(h, j):
                    t = tiles_of("att")[0] + 5 * h + j
                    tile_whole(dve, t)
                    if h:
                        dve.wait_ge(qk_ready, h)
                    dst = qraw[:, j, :] if j < 2 else kvraw[:, :] if j == 2 else sgate[:, h % 2, j - 3, :]
                    dve.tensor_tensor(dst, gp[t % 4][:, :], rstd[:, :], ALU.mult).then_inc(bank_read[t % 4], 1)

                def rope(h, tiles):
                    t0 = tiles_of("att")[0] + 5 * h
                    for j in tiles:
                        dve.wait_ge(rot_ready, 3 * h + j + 1)
                        tile_taken(dve, t0 + j)
                        rows = slice(0, P if j < 2 else HD)
                        src = qraw[rows, j, :] if j < 2 else kvraw[rows, :]
                        dst = qr[rows, h % 2, j, :] if j < 2 else kd[rows, h % 2, 0, :]
                        if j or h:
                            after()
                        ins = dve.tensor_tensor(rtmp[rows, 0, :], mp[j % 2][rows, :], sinT[rows, :], ALU.mult)
                        if j == 0:
                            ins.then_inc(rot_read, 1)
                        else:
                            step(ins)
                        step(dve.tensor_tensor(rtmp[rows, 1, :], src, cosT[rows, :], ALU.mult))
                        after()
                        step(dve.tensor_tensor(dst, rtmp[rows, 0, :], rtmp[rows, 1, :], ALU.add))
                    if 2 not in tiles:
                        return
                    after()
                    step(dve.tensor_copy(kd[HD:, h % 2, 1, :], kd[0:HD, h % 2, 0, :]))
                    dve.wait_ge(v_turned, h + 1)
                    dve.tensor_copy(vt[:, h % 2, :, :], mp[2][:, :].rearrange("p (c d) -> p c d", c=NCH)[:, :, HD:]
                                    ).then_inc(qk_ready, 1)

                for h in range(KVH + 1):
                    for k in range(12):
                        if h < KVH and k == 11:
                            rope(h, (2,))
                        if h:
                            if k == 11:
                                gate_o(h - 1, 1)
                            if 1 <= k <= 8:
                                normalise(h - 1, k - 1)
                            if k < 8:
                                mask_scores(h - 1, k)
                            if k == 6:
                                gate_o(h - 1, 0)
                            if k in (7, 11):
                                n = 2 * (h - 1) + (k == 11)
                                low(split0["att"] + n, oh[:, n, :], ol[:, n, :])
                        if h < KVH and k % 2 and k < 10:
                            take(h, k // 2)
                            if h == 0 and k == 5:
                                tables()
                        if h < KVH and k == 10:
                            if h == 0:
                                dve.wait_ge(sin_done, 1)
                            rope(h, (0, 1))
                for k in range(KT):
                    t = out_tile("att_out", k)
                    tile_whole(dve, t)
                    dve.tensor_copy(yo_a[:, k, :], gp[t % 4][:, :]).then_inc(bank_read[t % 4], 1)
                    if k:
                        add_square(dve, post_round[1], k - 1)
                add_square(dve, post_round[1], KT - 1)
                post_norm_of(1, yo_a)

            def out_value(k):
                n = split0["out"] + k
                x_wait(dve, 6, k)
                if k >= 2:
                    dve.wait_ge(out_turned, k - 1)
                else:
                    dve.wait_ge(split_done, n - 1)
                dve.tensor_scalar(val[:, k % 2, :], xT[:, k, :], prm[:, P_FINAL + k:P_FINAL + k + 1], None,
                                  ALU.mult).then_inc(value_ready, 1)

            def add_to_x(name, v):
                for k in range(KT + 1):
                    if k < KT:
                        t = out_tile(name, k)
                        tile_whole(dve, t)
                        dve.tensor_tensor(xT[:, k, :], gp[t % 4][:, :], xT[:, k, :], ALU.add).then_inc(bank_read[t % 4], 1)
                        if v == 6:
                            out_value(k)
                        else:
                            value_of_x(v, k)
                    if k > 0:
                        if v == 6:
                            add_square(dve, pre_round[v], k - 1)
                        else:
                            low_of_x(v, k - 1)

            def conv_pool():
                t0 = tiles_of("cp")[0]
                step(dve.memset(apad[:, :, 0:CW - 1], 0.0))
                step(dve.memset(ub[:, :, 0:16], 0.0))

                def take(i):
                    half, j = i // 4, i % 2
                    if i >= 8:
                        dst = ub[:, i - 8, 16:]
                    elif i % 4 < 2:
                        dst = sig[:, j, :]
                    else:
                        dst = apad[:, 2 * half + j, CW - 1:]
                    tile_whole(dve, t0 + i)
                    dve.tensor_tensor(dst, gp[(t0 + i) % 4][:, :], rstd[:, :], ALU.mult).then_inc(bank_read[(t0 + i) % 4], 1)

                def gate(half):
                    for j in range(2):
                        tile_taken(dve, t0 + 4 * half + 2 + j)
                        dve.wait_ge(sig_ready, 2 * half + j + 1)
                        a = apad[:, 2 * half + j, CW - 1:]
                        dve.tensor_tensor(a, a, sig[:, j, :], ALU.mult).then_inc(gated_ready, 1)
                    dve.wait_ge(gated_ready, 2 * half + 2)

                def convolve(tiles):
                    last = {}
                    for i in range(CW - 1, -1, -1):
                        for c in tiles:
                            col = P_DW + 4 * i + c
                            src, w = apad[:, c, i:i + L], prm[:, col:col + 1]
                            if i == CW - 1:
                                last[c] = step(dve.tensor_scalar(acc[:, c, :], src, w, prm[:, P_DWB + c:P_DWB + c + 1],
                                                                 ALU.mult, ALU.add))
                                continue
                            after(last[c])
                            ins = dve.scalar_tensor_tensor(acc[:, c, :], src, w, acc[:, c, :], ALU.mult, ALU.add)
                            if i:
                                last[c] = step(ins)
                            else:
                                ins.then_inc(conv_ready, 1)
                        yield CW - 1 - i

                for i in range(4):
                    take(i)
                gate(0)
                for n in convolve((0, 1)):
                    if n % 4 == 2:
                        take(4 + n // 4)
                    if n == 15:
                        gate(1)
                for n in convolve((2,)):
                    pass
                n0 = split0["cp"]
                for g in range(4):
                    dve.wait_ge(hi_ready, n0 + g + 1)
                    dve.tensor_tensor(cl[:, 4 + g, :], ub[:, g, 16:], ch[:, 4 + g, :].bitcast(F32),
                                      ALU.subtract).then_inc(split_done, 1)
                dve.wait_ge(mean_ready, 1)
                for t in range(4):
                    dve.scalar_tensor_tensor(acc[:, t, :], mp[0][:, :], -1.0 / 512, acc[:, t, :], ALU.mult,
                                             ALU.add).then_inc(centred, 1)
                dve.wait_ge(lrstd_ready, 1)
                for t in range(4):
                    dve.scalar_tensor_tensor(acc[:, t, :], acc[:, t, :], prm[:, P_LNG + t:P_LNG + t + 1], lrstd[:, :],
                                             ALU.mult, ALU.mult).then_inc(ln_ready, 1)
                for t in range(4):
                    dve.wait_ge(hi_ready, n0 + 4 + t + 1)
                    dve.tensor_tensor(cl[:, t, :], acc[:, t, :], ch[:, t, :].bitcast(F32),
                                      ALU.subtract).then_inc(split_done, 1)
                add_to_x("cp_out", 3)

            def ffn(i, v):
                t0, n0 = tiles_of(f"up{i}")[0], split0[f"up{i}"]
                for n in range(FT // 2):
                    for j in range(2):
                        t = t0 + 4 * n + j
                        tile_whole(dve, t)
                        dve.tensor_tensor(sq[:, j, :], gp[t % 4][:, :], rstd[:, :], ALU.mult).then_inc(bank_read[t % 4], 1)
                    for j in range(2):
                        t = t0 + 4 * n + 2 + j
                        tile_whole(dve, t)
                        dve.tensor_tensor(value_slot(n0 + 2 * n + j), gp[t % 4][:, :], rstd[:, :],
                                          ALU.mult).then_inc(bank_read[t % 4], 1)
                    for j in range(2):
                        tile_taken(dve, t0 + 4 * n + 2 + j)
                        dve.wait_ge(silu_ready, 2 * KVH + FT * (v // 5) + 2 * n + j + 1)
                        value = val[:, (n0 + j) % 2, :]
                        dve.tensor_tensor(value, value, sq[:, j, :], ALU.mult).then_inc(value_ready, 1)
                    for j in range(2):
                        low(n0 + 2 * n + j, gh[:, 2 * n + j, :], gl[:, 2 * n + j, :])
                add_to_x(f"down{i}", v + 1)

            def hgrn():
                t0 = tiles_of("hg")[0]
                l0, l1, s0 = prm[:, P_LB:P_LB + 8], prm[:, P_LB + 8:P_LB + 16], lbc[:, 2, :]
                step(dve.tensor_tensor(s0, l0, l1, ALU.max))
                after()
                step(dve.tensor_tensor(lbc[:, 0, :], l1, s0, ALU.subtract))
                dve.tensor_tensor(lbc[:, 1, :], l0, s0, ALU.subtract).then_inc(lb_diff, 1)
                dve.wait_ge(lb_exp, 1)
                step(dve.tensor_tensor(s0, lbc[:, 0, :], lbc[:, 1, :], ALU.add))
                after()
                step(dve.reciprocal(s0, s0))
                after()
                step(dve.tensor_tensor(lbc[:, 0, :], lbc[:, 0, :], s0, ALU.mult))
                after()
                step(dve.tensor_scalar(lbc[:, 1, :], lbc[:, 0, :], -1.0, 1.0, ALU.mult, ALU.add))
                after()
                dve.wait_ge(mask_landed, 16)

                def take(p, j):
                    t, b = t0 + 8 * p + j, p % 2
                    tile_whole(dve, t)
                    if j < 6:
                        if p >= 2:
                            dve.wait_ge(ho_ready, 2 * (p - 1))
                        dst = (hq, hb, hvt)[j // 2][:, b, j % 2, :]
                    else:
                        dst = hg[:, (2 * p + j - 6) % 3, :]
                    dve.tensor_tensor(dst, gp[t % 4][:, :], rstd[:, :], ALU.mult).then_inc(bank_read[t % 4], 1)

                def forget(p, j):
                    dve.wait_ge(fsig_ready, 2 * p + j + 1)
                    q, f = 2 * p + j, hb[:, p % 2, j, :]
                    dve.tensor_scalar(f, f, lbc[:, 1, q:q + 1], lbc[:, 0, q:q + 1], ALU.mult, ALU.add).then_inc(f_lin, 1)
                    dve.wait_ge(f_lin, q + 1)
                    dve.tensor_scalar(hk[:, p % 2, j, :], f, -1.0, 1.0, ALU.mult, ALU.add).then_inc(f_ready, 1)

                def scan(p, j):
                    dve.wait_ge(ln_f, 2 * p + j + 1)
                    b = hb[:, p % 2, j, :]
                    dve.tensor_tensor_scan(b, cst[:, C_RESET:C_RESET + L], b, 0.0, ALU.mult, ALU.add).then_inc(hb_ready, 1)

                def halves(v, w):
                    v = v.rearrange("p (n k w) -> p n k w", k=2, w=w)
                    return v[:, :, 0, :], v[:, :, 1, :]

                def level_diff(m):
                    n, s = m // 8, m % 8
                    if not s or n >= HH:
                        return
                    w, lv = LEVELS[s - 1], 7 * n + s - 1
                    dve.wait_ge(hb_ready, n + 1)
                    if lv >= 3:
                        dve.wait_ge(lv_ready, 8 * ((lv - 3) // 7) + (lv - 3) % 7 + 2)
                    (bl, br), (xl, xr) = halves(hb[:, n // 2 % 2, n % 2, :], w), halves(XL[:, lv % 3, :], w)
                    ref = bl[:, :, w - 1:w].to_broadcast([P, L // (2 * w), w])
                    step(dve.tensor_tensor(xl, bl, ref, ALU.subtract))
                    dve.tensor_tensor(xr, ref, br, ALU.subtract).then_inc(diff_ready, 1)

                def level_products(m):
                    n, s = m // 8, m % 8
                    if not s or n >= HH:
                        return
                    w, lv, b, j = LEVELS[s - 1], 7 * n + s - 1, n // 2 % 2, n % 2
                    dve.wait_ge(dexp_ready, lv + 1)
                    tile_taken(dve, t0 + 8 * (n // 2) + j)
                    (kl, _), (_, qright), (xl, xr) = halves(hk[:, b, j, :], w), halves(hq[:, b, j, :], w), halves(XL[:, lv % 3, :], w)
                    step(dve.tensor_tensor(xl, xl, kl, ALU.mult))
                    dve.tensor_tensor(xr, xr, qright, ALU.mult).then_inc(x_ready, 1)

                def collect(m):
                    n, s = m // 8, m % 8
                    dve.wait_ge(lv_ready, m + 1)
                    lm = lmask[:, s - 1 if s else len(LEVELS), :].unsqueeze(1).to_broadcast([P, NCH, P])
                    dst = SM[:, n % 2, :].rearrange("p (c t) -> p c t", c=NCH)
                    src = mp[m % 2][:, :].rearrange("p (c t) -> p c t", c=NCH)
                    if s == 0:
                        if n >= 2:
                            dve.wait_ge(ho_ready, n - 1)
                        dve.tensor_tensor(dst, src, lm, ALU.mult).then_inc(lv_read, 1)
                    else:
                        dve.wait_ge(lv_read, m)
                        dve.copy_predicated(dst, lm.bitcast(U32), src).then_inc(lv_read, 1)

                def key_diff(n):
                    b = hb[:, n // 2 % 2, n % 2, 0:3 * P].rearrange("p (c t) -> p c t", c=3)
                    if n:
                        dve.wait_ge(kt_turned, n)
                    dve.tensor_tensor(Ke[:, :, :], b[:, :, P - 1:P].to_broadcast([P, 3, P]), b,
                                      ALU.subtract).then_inc(ke_diff, 1)

                def key_product(n):
                    dve.wait_ge(ke_exp, n + 1)
                    ke = Ke[:, :, :].rearrange("p c t -> p (c t)")
                    dve.tensor_tensor(ke, ke, hk[:, n // 2 % 2, n % 2, 0:3 * P], ALU.mult).then_inc(ke_ready, 1)

                def query_product(n):
                    dve.wait_ge(qe_exp, n + 1)
                    qe = Qe[:, :, :].rearrange("p c t -> p (c t)")
                    dve.tensor_tensor(qe, qe, hq[:, n // 2 % 2, n % 2, P:], ALU.mult).then_inc(qe_ready, 1)

                def recur(n):
                    dve.wait_ge(hst_ready, n + 1)
                    dve.wait_ge(qe_exp, n + 1)
                    if n:
                        dve.wait_ge(ho_ready, n)
                    step(dve.tensor_copy(St[:, 0, :], mp[2][:, 0:P]))
                    after()
                    step(dve.scalar_tensor_tensor(St[:, 1, :], St[:, 0, :], ebl[:, n % 2, 1:2], mp[2][:, P:2 * P],
                                                  ALU.mult, ALU.add))
                    after()
                    dve.scalar_tensor_tensor(St[:, 2, :], St[:, 1, :], ebl[:, n % 2, 2:3], mp[2][:, 2 * P:3 * P],
                                             ALU.mult, ALU.add).then_inc(hs_ready, 1)

                def head_value(n):
                    dve.wait_ge(hrstd_ready, n + 1)
                    v = value_slot(split0["hg"] + n)
                    dve.scalar_tensor_tensor(v, mp[3][:, :], prm[:, P_GN + n:P_GN + n + 1], root[:, :], ALU.mult,
                                             ALU.mult).then_inc(hscaled, 1)
                    dve.wait_ge(hscaled, n + 1)
                    dve.wait_ge(hgate_ready, n + 1)
                    dve.tensor_tensor(v, v, hg[:, n % 3, :], ALU.mult).then_inc(value_ready, 1)

                for p in range(HH // 2 + 1):
                    for k in range(16):
                        n, s = 2 * (p - 1) + k // 8, k % 8
                        if p:
                            m = 8 * n + s
                            level_diff(m + 2)
                            level_products(m + 1)
                            if s == 0:
                                key_diff(n)
                            elif s == 1:
                                key_product(n)
                            elif s == 3:
                                query_product(n)
                            elif s == 4 and n:
                                head_value(n - 1)
                            elif s == 5:
                                recur(n)
                            elif s == 6 and n:
                                low(split0["hg"] + n - 1, hoh[:, n - 1, :], hol[:, n - 1, :])
                            collect(m)
                        if p < HH // 2:
                            if k % 2:
                                take(p, k // 2)
                            if k in (6, 8):
                                forget(p, (k - 6) // 2)
                            if k in (8, 10):
                                scan(p, (k - 8) // 2)
                    if p == 0:
                        level_diff(1)
                head_value(HH - 1)
                low(split0["hg"] + HH - 1, hoh[:, HH - 1, :], hol[:, HH - 1, :])
                add_to_x("hg_out", 5)

            mamba()
            dve.wait_ge(rstd_ready, pre_round[1] + 1)
            attention()
            dve.wait_ge(rstd_ready, pre_round[2] + 1)
            conv_pool()
            dve.wait_ge(rstd_ready, pre_round[3] + 1)
            ffn(0, 3)
            dve.wait_ge(rstd_ready, pre_round[4] + 1)
            hgrn()
            dve.wait_ge(rstd_ready, pre_round[5] + 1)
            ffn(1, 5)
            dve.wait_ge(rstd_ready, pre_round[6] + 1)
            for c in (0, 2):
                dve.tensor_scalar(rows_out[:, c, :], rows_out[:, c, :], rstd[:, c:c + 1], None,
                                  ALU.mult).then_inc(even_ready, 1)


INPUTS = ["x", "positions", "pre_norm", "post_norm", "ssm_w_in", "ssm_conv_w", "ssm_conv_b", "ssm_dt_bias",
          "ssm_a_log", "ssm_d", "ssm_gate_norm", "ssm_w_out", "att_w_in", "att_sinks", "att_w_out",
          "norm_mix_g_2", "norm_ffn_g_2", "final_g_2", "cp_w_in_2", "cp_dw_w_2", "cp_dw_b_2", "cp_ln_g_2",
          "cp_ln_b_2", "cp_pool_w_2", "cp_pool_scale_2", "cp_w_out_2", "hg_w_in_2", "hg_lb_logits_2",
          "hg_gn_g_2", "hg_w_out_2", "ffn_w1_2", "ffn_w3_2", "ffn_w2_2"]


def kernel(**inputs):
    import numpy as _np
    import concourse.bacc as _bacc
    from concourse import mybir as _mybir
    from concourse.bass_utils import run_bass_kernel_spmd as _run

    nc = _bacc.Bacc("TRN2", target_bir_lowering=False, num_devices=1)
    arrays, args = {}, []
    consts = dict(zip(("shape_const", "level_mask"), shape_constants()))
    for name in INPUTS + list(consts):
        a = _np.ascontiguousarray(consts[name] if name in consts else inputs[name])
        arrays[name] = a
        args.append(nc.dram_tensor(name, a.shape, _mybir.dt.from_np(a.dtype), kind="ExternalInput").ap())
    args.append(nc.dram_tensor("out", (1, L, D), _mybir.dt.float32, kind="ExternalOutput").ap())
    build(nc, *args)
    r = _run(nc, [arrays], core_ids=[0])
    return r.results[0]["out"]
```
